# Optimizing a Trainium2 kernel written in Bass

```python
import math
import jax
import jax.numpy as jnp
from jax import lax
import jax, jax.numpy as jnp
import numpy as np

D_MODEL = 1024
BATCH = 1
SEQ = 256
DEPTH = 2

N_EVEN = (DEPTH + 1) // 2
N_ODD = DEPTH // 2
N_VRES = max(N_EVEN - 1, 0)

MIX_HALF = D_MODEL // 2

RW_WIDTH = MIX_HALF
RW_HEAD_DIM = 64
RW_HEADS = RW_WIDTH // RW_HEAD_DIM
RW_DECAY_RANK = 64
RW_ICLR_RANK = 64
RW_GATE_RANK = 128
RW_VRES_RANK = 32
RW_SHIFT_COLS = 3 * RW_WIDTH + RW_DECAY_RANK + RW_ICLR_RANK + RW_GATE_RANK
RW_SPLITS = (RW_WIDTH, 2 * RW_WIDTH, 3 * RW_WIDTH, 3 * RW_WIDTH + RW_DECAY_RANK,
             3 * RW_WIDTH + RW_DECAY_RANK + RW_ICLR_RANK)
RW_LN_EPS = 64e-5

POOL_WIDTH = MIX_HALF
POOL_WINDOWS = (2, 4, 8, 16)
POOL_GROUPS = len(POOL_WINDOWS)
POOL_GROUP_DIM = POOL_WIDTH // POOL_GROUPS

EVEN_IN = RW_SHIFT_COLS + POOL_WIDTH
EVEN_MIX = RW_WIDTH + POOL_WIDTH

DA_WIDTH = MIX_HALF
DA_HEAD_DIM = 64
DA_VALUE_DIM = 2 * DA_HEAD_DIM
DA_HEADS = DA_WIDTH // DA_VALUE_DIM
DA_QK_COLS = DA_HEADS * 2 * DA_HEAD_DIM
ROPE_THETA = 10000.0
Q_BLOCK = 128
SUBLN_EPS = 1e-5

S5_WIDTH = MIX_HALF
S5_GROUP_DIM = 16
S5_GROUPS = S5_WIDTH // S5_GROUP_DIM
S5_STATE = 64

ODD_IN = 2 * DA_QK_COLS + DA_WIDTH + S5_WIDTH
ODD_MIX = DA_WIDTH + S5_WIDTH

MOE_GROUPS = 4
MOE_EXPERTS_PER_GROUP = 8
MOE_EXPERTS = MOE_GROUPS * MOE_EXPERTS_PER_GROUP
MOE_TOP_K = 2
MOE_HIDDEN = D_MODEL // 2
MOE_BLOCK = 128

RMS_EPS = 1e-6


def rms_norm(x, g, eps=RMS_EPS):
    xf = x.astype(jnp.float32)
    y = xf * lax.rsqrt(jnp.mean(xf * xf, axis=-1, keepdims=True) + eps)
    return (y * g.astype(jnp.float32)).astype(x.dtype)

def token_shift(u):
    return jnp.pad(u, ((0, 0), (1, 0), (0, 0)))[:, :-1]

def rwkv7_recurrence(r, w, k, v, a, b):
    bsz, _, n_heads, n = r.shape
    seq = tuple(jnp.moveaxis(t.astype(jnp.float32), 1, 0) for t in (r, w, k, v, a, b))

    def step(state, inp):
        r_t, w_t, k_t, v_t, a_t, b_t = inp
        sa = jnp.einsum('bhij,bhj->bhi', state, a_t)
        state = (state * w_t[:, :, None, :] + sa[..., None] * b_t[:, :, None, :]
                 + v_t[..., None] * k_t[:, :, None, :])
        return state, jnp.einsum('bhij,bhj->bhi', state, r_t)

    s0 = jnp.zeros((bsz, n_heads, n, n), jnp.float32)
    _, y = lax.scan(step, s0, seq)
    return jnp.moveaxis(y, 0, 1)

def multiscale_pool(u, pool_w, pool_scale):
    bsz, t_len, _ = u.shape
    uf = u.astype(jnp.float32).reshape(bsz, t_len, POOL_GROUPS, POOL_GROUP_DIM)
    csum = jnp.cumsum(uf, axis=1)
    n_seen = jnp.arange(1, t_len + 1, dtype=jnp.float32)
    diffs = []
    for gi, win in enumerate(POOL_WINDOWS):
        c = csum[:, :, gi]
        lagged = jnp.pad(c, ((0, 0), (win, 0), (0, 0)))[:, :t_len]
        mean = (c - lagged) / jnp.minimum(n_seen, float(win))[None, :, None]
        diffs.append(mean - uf[:, :, gi])
    d = jnp.stack(diffs, axis=2).astype(u.dtype)
    y = jnp.einsum('btgc,gcd->btgd', d, pool_w)
    return y.reshape(bsz, t_len, POOL_WIDTH) * pool_scale

def even_mixer(h, v_first, w_in, mu, w0, w2, a0, a2, g2, k_k, k_a, r_k, ln_g, ln_b, vres,
               pool_w, pool_scale, w_out):
    bsz, t_len, _ = h.shape
    u = h @ w_in
    u_rw, u_pool = u[..., :RW_SHIFT_COLS], u[..., RW_SHIFT_COLS:]
    m = u_rw + (token_shift(u_rw) - u_rw) * mu
    r, k, v, dw, da, dg = jnp.split(m, RW_SPLITS, axis=-1)
    w = -jax.nn.softplus(-(w0 + jnp.tanh(dw) @ w2)) - 0.5
    decay = jnp.exp(-jnp.exp(w.astype(jnp.float32)))
    a = jax.nn.sigmoid(a0 + da @ a2)
    g = jax.nn.sigmoid(dg) @ g2
    if v_first is None:
        v_first = v
    else:
        v0, v1, v2 = vres
        v = v + (v_first - v) * jax.nn.sigmoid(v0 + (v @ v1) @ v2)

    def heads(t):
        return t.reshape(bsz, t_len, RW_HEADS, RW_HEAD_DIM)

    kk = heads(k * k_k).astype(jnp.float32)
    kk = kk / jnp.maximum(jnp.sqrt(jnp.sum(kk * kk, axis=-1, keepdims=True)), 1e-12)
    k = k * (1.0 + (a - 1.0) * k_a)
    rh, kh, vh, ah = heads(r), heads(k), heads(v), heads(a)
    y = rwkv7_recurrence(rh, heads(decay), kh, vh, -kk, kk * ah.astype(jnp.float32))
    mean = jnp.mean(y, axis=-1, keepdims=True)
    var = jnp.mean(jnp.square(y - mean), axis=-1, keepdims=True)
    y = ((y - mean) * lax.rsqrt(var + RW_LN_EPS)).reshape(bsz, t_len, RW_WIDTH)
    y = (y * ln_g + ln_b).astype(h.dtype)
    bonus = jnp.sum(rh * kh * r_k, axis=-1, keepdims=True) * vh
    o_rw = (y + bonus.reshape(bsz, t_len, RW_WIDTH)) * g
    o_pool = multiscale_pool(u_pool, pool_w, pool_scale)
    return jnp.concatenate([o_rw, o_pool], axis=-1) @ w_out, v_first

def rope_tables(t_len, dim):
    inv_freq = ROPE_THETA ** (-jnp.arange(0, dim, 2, dtype=jnp.float32) / dim)
    ang = jnp.arange(t_len, dtype=jnp.float32)[:, None] * inv_freq[None, :]
    return jnp.cos(ang), jnp.sin(ang)

def apply_rope(x, cos, sin):
    xf = x.astype(jnp.float32)
    x1, x2 = jnp.split(xf, 2, axis=-1)
    c = cos[:, None, None, :]
    s = sin[:, None, None, :]
    return jnp.concatenate([x1 * c - x2 * s, x2 * c + x1 * s], axis=-1).astype(x.dtype)

def diff_attention(q, k, v, lam):
    t_len = q.shape[1]
    scale = DA_HEAD_DIM ** -0.5
    pos = jnp.arange(t_len)
    outs = []
    for s in range(0, t_len, Q_BLOCK):
        e = s + Q_BLOCK
        sc = jnp.einsum('bqhmd,bkhmd->bhmqk', q[:, s:e], k[:, :e]).astype(jnp.float32) * scale
        mask = pos[s:e, None] >= pos[None, :e]
        p = jax.nn.softmax(jnp.where(mask, sc, -jnp.inf), axis=-1)
        attn = p[:, :, 0] - lam * p[:, :, 1]
        outs.append(jnp.einsum('bhqk,bkhd->bqhd', attn.astype(v.dtype), v[:, :e]))
    return jnp.concatenate(outs, axis=1)

def s5_mixer(u, a_re, a_im, log_step, b_re, b_im, c_re, c_im, d_skip, w_glu):
    bsz, t_len, _ = u.shape
    f32 = jnp.float32
    uf = u.astype(f32).reshape(bsz, t_len, S5_GROUPS, S5_GROUP_DIM)
    lam = lax.complex(jnp.minimum(a_re.astype(f32), -1e-4), a_im.astype(f32))
    step = jnp.exp(log_step.astype(f32))
    lam_bar = jnp.exp(lam * step)
    b_bar = ((lam_bar - 1.0) / lam)[..., None] * lax.complex(b_re.astype(f32), b_im.astype(f32))
    c_mat = lax.complex(c_re.astype(f32), c_im.astype(f32))
    bu = jnp.einsum('gpc,btgc->btgp', b_bar, uf.astype(jnp.complex64))
    a_seq = jnp.broadcast_to(lam_bar, bu.shape)

    def combine(left, right):
        a_l, b_l = left
        a_r, b_r = right
        return a_r * a_l, a_r * b_l + b_r

    _, states = lax.associative_scan(combine, (a_seq, bu), axis=1)
    y = jnp.einsum('gcp,btgp->btgc', c_mat, states).real + d_skip.astype(f32) * uf
    z = jax.nn.gelu(y.reshape(bsz, t_len, S5_WIDTH)).astype(u.dtype)
    return z * jax.nn.sigmoid(z @ w_glu)

def odd_mixer(h, layer_idx, w_in, q_norm, k_norm, lam_q1, lam_k1, lam_q2, lam_k2, subln,
              a_re, a_im, log_step, b_re, b_im, c_re, c_im, d_skip, w_glu, w_out):
    bsz, t_len, _ = h.shape
    f32 = jnp.float32
    u = h @ w_in
    q, k, v, u_s5 = jnp.split(u, (DA_QK_COLS, 2 * DA_QK_COLS, 2 * DA_QK_COLS + DA_WIDTH), axis=-1)
    q = q.reshape(bsz, t_len, DA_HEADS, 2, DA_HEAD_DIM)
    k = k.reshape(bsz, t_len, DA_HEADS, 2, DA_HEAD_DIM)
    v = v.reshape(bsz, t_len, DA_HEADS, DA_VALUE_DIM)
    cos, sin = rope_tables(t_len, DA_HEAD_DIM)
    q = apply_rope(rms_norm(q, q_norm), cos, sin)
    k = apply_rope(rms_norm(k, k_norm), cos, sin)
    lam_init = 0.8 - 0.6 * math.exp(-0.3 * layer_idx)
    lam = (jnp.exp(jnp.sum(lam_q1.astype(f32) * lam_k1.astype(f32)))
           - jnp.exp(jnp.sum(lam_q2.astype(f32) * lam_k2.astype(f32))) + lam_init)
    o = diff_attention(q, k, v, lam)
    o = rms_norm(o, subln, SUBLN_EPS) * (1.0 - lam_init)
    o_attn = o.reshape(bsz, t_len, DA_WIDTH)
    o_ssm = s5_mixer(u_s5, a_re, a_im, log_step, b_re, b_im, c_re, c_im, d_skip, w_glu)
    return jnp.concatenate([o_attn, o_ssm], axis=-1) @ w_out

def routed_experts(hf, expert_idx, gates, w_gate, w_up, w_down):
    n_tok, d = hf.shape
    n_slot = n_tok * MOE_TOP_K
    flat_e = expert_idx.reshape(-1)
    flat_tok = jnp.arange(n_slot, dtype=jnp.int32) // MOE_TOP_K
    flat_g = gates.reshape(-1)
    order = jnp.argsort(flat_e)
    sorted_e = flat_e[order]
    counts = jnp.bincount(flat_e, length=MOE_EXPERTS)
    padded = (counts + MOE_BLOCK - 1) // MOE_BLOCK * MOE_BLOCK
    seg_start = jnp.cumsum(counts) - counts
    cum_padded = jnp.cumsum(padded)
    pad_start = cum_padded - padded
    dest = pad_start[sorted_e] + jnp.arange(n_slot, dtype=jnp.int32) - seg_start[sorted_e]
    n_blocks = -(-n_slot // MOE_BLOCK) + MOE_EXPERTS
    n_pad = n_blocks * MOE_BLOCK
    buf_tok = jnp.full((n_pad,), n_tok, jnp.int32).at[dest].set(flat_tok[order])
    buf_gate = jnp.zeros((n_pad,), jnp.float32).at[dest].set(flat_g[order])
    block_start = jnp.arange(n_blocks, dtype=cum_padded.dtype) * MOE_BLOCK
    block_expert = jnp.minimum(jnp.searchsorted(cum_padded, block_start, side='right'),
                               MOE_EXPERTS - 1).astype(jnp.int32)
    h_pad = jnp.concatenate([hf, jnp.zeros((1, d), hf.dtype)], axis=0)

    def run_block(args):
        tok, e, gt = args
        xb = h_pad[tok]
        hidden = jax.nn.silu(xb @ w_gate[e]) * (xb @ w_up[e])
        return (hidden @ w_down[e]) * gt[:, None].astype(xb.dtype)

    ys = lax.map(run_block, (buf_tok.reshape(n_blocks, MOE_BLOCK), block_expert,
                             buf_gate.reshape(n_blocks, MOE_BLOCK)))
    out = jnp.zeros((n_tok + 1, d), hf.dtype).at[buf_tok].add(ys.reshape(n_pad, d))
    return out[:n_tok]

def hier_moe(h, w_group, b_group, w_expert, b_expert, w_gate, w_up, w_down):
    bsz, t_len, d = h.shape
    n_tok = bsz * t_len
    hf = h.reshape(n_tok, d)
    rows = jnp.arange(n_tok)
    g_logits = (hf @ w_group + b_group).astype(jnp.float32)
    g_prob = jax.nn.softmax(g_logits, axis=-1)
    g_top = jnp.argmax(g_logits, axis=-1).astype(jnp.int32)
    g_w = g_prob[rows, g_top]
    e_logits = (hf @ w_expert + b_expert).astype(jnp.float32)
    e_logits = e_logits.reshape(n_tok, MOE_GROUPS, MOE_EXPERTS_PER_GROUP)[rows, g_top]
    e_prob = jax.nn.softmax(e_logits, axis=-1)
    top_p, top_j = lax.top_k(e_prob, MOE_TOP_K)
    gates = g_w[:, None] * top_p / jnp.sum(top_p, axis=-1, keepdims=True)
    expert_idx = g_top[:, None] * MOE_EXPERTS_PER_GROUP + top_j.astype(jnp.int32)
    y = routed_experts(hf, expert_idx, gates, w_gate, w_up, w_down)
    return y.reshape(bsz, t_len, d)

def first_inputs(seed: int = 0) -> dict:
    key = jax.random.key(seed)
    keys = jax.random.split(key, 64)
    counter = [0]

    def nk():
        counter[0] += 1
        return keys[counter[0] - 1]

    f32 = jnp.float32

    def nrm(shape, scale):
        return scale * jax.random.normal(nk(), shape, f32)

    def gain(shape, base=1.0, noise=0.02):
        return base + noise * jax.random.normal(nk(), shape, f32)

    def unif(shape, lo, hi):
        return jax.random.uniform(nk(), shape, f32, lo, hi)

    d = D_MODEL
    res = (2.0 * DEPTH) ** -0.5
    return {
        'x': nrm((BATCH, SEQ, d), 1.0),
        'norm_mix_g': gain((DEPTH, d)),
        'norm_ffn_g': gain((DEPTH, d)),
        'even_w_in': nrm((N_EVEN, d, EVEN_IN), d ** -0.5),
        'rw_mu': unif((N_EVEN, RW_SHIFT_COLS), 0.0, 1.0),
        'rw_w0': unif((N_EVEN, RW_WIDTH), -6.0, -1.0),
        'rw_w2': nrm((N_EVEN, RW_DECAY_RANK, RW_WIDTH), RW_DECAY_RANK ** -0.5),
        'rw_a0': nrm((N_EVEN, RW_WIDTH), 0.1),
        'rw_a2': nrm((N_EVEN, RW_ICLR_RANK, RW_WIDTH), RW_ICLR_RANK ** -0.5),
        'rw_g2': nrm((N_EVEN, RW_GATE_RANK, RW_WIDTH), RW_GATE_RANK ** -0.5),
        'rw_k_k': gain((N_EVEN, RW_WIDTH), 0.85, 0.05),
        'rw_k_a': gain((N_EVEN, RW_WIDTH), 1.0, 0.05),
        'rw_r_k': nrm((N_EVEN, RW_HEADS, RW_HEAD_DIM), 0.1),
        'rw_ln_g': gain((N_EVEN, RW_WIDTH)),
        'rw_ln_b': nrm((N_EVEN, RW_WIDTH), 0.02),
        'rw_v0': nrm((N_VRES, RW_WIDTH), 0.1),
        'rw_v1': nrm((N_VRES, RW_WIDTH, RW_VRES_RANK), RW_WIDTH ** -0.5),
        'rw_v2': nrm((N_VRES, RW_VRES_RANK, RW_WIDTH), RW_VRES_RANK ** -0.5),
        'pool_w': nrm((N_EVEN, POOL_GROUPS, POOL_GROUP_DIM, POOL_GROUP_DIM), POOL_GROUP_DIM ** -0.5),
        'pool_scale': gain((N_EVEN, POOL_WIDTH)),
        'even_w_out': nrm((N_EVEN, EVEN_MIX, d), EVEN_MIX ** -0.5 * res),
        'odd_w_in': nrm((N_ODD, d, ODD_IN), d ** -0.5),
        'da_q_norm': gain((N_ODD, DA_HEAD_DIM)),
        'da_k_norm': gain((N_ODD, DA_HEAD_DIM)),
        'da_lam_q1': nrm((N_ODD, DA_HEAD_DIM), 0.1),
        'da_lam_k1': nrm((N_ODD, DA_HEAD_DIM), 0.1),
        'da_lam_q2': nrm((N_ODD, DA_HEAD_DIM), 0.1),
        'da_lam_k2': nrm((N_ODD, DA_HEAD_DIM), 0.1),
        'da_subln': gain((N_ODD, DA_VALUE_DIM)),
        's5_a_re': gain((N_ODD, S5_GROUPS, S5_STATE), -0.5, 0.01),
        's5_a_im': math.pi * jnp.arange(S5_STATE, dtype=f32) + nrm((N_ODD, S5_GROUPS, S5_STATE), 0.01),
        's5_log_step': unif((N_ODD, S5_GROUPS, S5_STATE), math.log(1e-3), math.log(1e-1)),
        's5_b_re': nrm((N_ODD, S5_GROUPS, S5_STATE, S5_GROUP_DIM), (2.0 * S5_GROUP_DIM) ** -0.5),
        's5_b_im': nrm((N_ODD, S5_GROUPS, S5_STATE, S5_GROUP_DIM), (2.0 * S5_GROUP_DIM) ** -0.5),
        's5_c_re': nrm((N_ODD, S5_GROUPS, S5_GROUP_DIM, S5_STATE), (2.0 * S5_STATE) ** -0.5),
        's5_c_im': nrm((N_ODD, S5_GROUPS, S5_GROUP_DIM, S5_STATE), (2.0 * S5_STATE) ** -0.5),
        's5_d': nrm((N_ODD, S5_GROUPS, S5_GROUP_DIM), 1.0),
        's5_w_glu': nrm((N_ODD, S5_WIDTH, S5_WIDTH), S5_WIDTH ** -0.5),
        'odd_w_out': nrm((N_ODD, ODD_MIX, d), ODD_MIX ** -0.5 * res),
        'moe_w_group': nrm((DEPTH, d, MOE_GROUPS), d ** -0.5),
        'moe_b_group': nrm((DEPTH, MOE_GROUPS), 0.01),
        'moe_w_expert': nrm((DEPTH, d, MOE_EXPERTS), d ** -0.5),
        'moe_b_expert': nrm((DEPTH, MOE_EXPERTS), 0.01),
        'moe_w_gate': nrm((DEPTH, MOE_EXPERTS, d, MOE_HIDDEN), d ** -0.5),
        'moe_w_up': nrm((DEPTH, MOE_EXPERTS, d, MOE_HIDDEN), d ** -0.5),
        'moe_w_down': nrm((DEPTH, MOE_EXPERTS, MOE_HIDDEN, d), MOE_HIDDEN ** -0.5 * res),
    }

def first_block(x, norm_mix_g, norm_ffn_g,
              even_w_in, rw_mu, rw_w0, rw_w2, rw_a0, rw_a2, rw_g2, rw_k_k, rw_k_a, rw_r_k,
              rw_ln_g, rw_ln_b, rw_v0, rw_v1, rw_v2, pool_w, pool_scale, even_w_out,
              odd_w_in, da_q_norm, da_k_norm, da_lam_q1, da_lam_k1, da_lam_q2, da_lam_k2, da_subln,
              s5_a_re, s5_a_im, s5_log_step, s5_b_re, s5_b_im, s5_c_re, s5_c_im, s5_d, s5_w_glu,
              odd_w_out,
              moe_w_group, moe_b_group, moe_w_expert, moe_b_expert, moe_w_gate, moe_w_up, moe_w_down):
    v_first = None
    for layer in range(DEPTH):
        i = layer // 2
        h = rms_norm(x, norm_mix_g[layer])
        if layer % 2 == 0:
            vres = None if v_first is None else (rw_v0[i - 1], rw_v1[i - 1], rw_v2[i - 1])
            mix, v_first = even_mixer(h, v_first, even_w_in[i], rw_mu[i], rw_w0[i], rw_w2[i],
                                      rw_a0[i], rw_a2[i], rw_g2[i], rw_k_k[i], rw_k_a[i], rw_r_k[i],
                                      rw_ln_g[i], rw_ln_b[i], vres, pool_w[i], pool_scale[i],
                                      even_w_out[i])
        else:
            mix = odd_mixer(h, layer, odd_w_in[i], da_q_norm[i], da_k_norm[i], da_lam_q1[i],
                            da_lam_k1[i], da_lam_q2[i], da_lam_k2[i], da_subln[i], s5_a_re[i],
                            s5_a_im[i], s5_log_step[i], s5_b_re[i], s5_b_im[i], s5_c_re[i],
                            s5_c_im[i], s5_d[i], s5_w_glu[i], odd_w_out[i])
        x = x + mix
        h = rms_norm(x, norm_ffn_g[layer])
        x = x + hier_moe(h, moe_w_group[layer], moe_b_group[layer], moe_w_expert[layer],
                         moe_b_expert[layer], moe_w_gate[layer], moe_w_up[layer], moe_w_down[layer])
    return x


EPS = 1e-6
CHUNK = 128

RET_HEADS = 4
RET_DK = 256
RET_DV = 512
RET_QK = RET_HEADS * RET_DK
RET_V = RET_HEADS * RET_DV
ROPE_BASE = 10000.0

SSD_INNER = 2 * D_MODEL
SSD_HEADDIM = 64
SSD_HEADS = SSD_INNER // SSD_HEADDIM
SSD_GROUPS = 4
SSD_HPG = SSD_HEADS // SSD_GROUPS
SSD_STATE = 128
SSD_CONV = 4
SSD_BC = SSD_GROUPS * SSD_STATE
SSD_CONV_CH = SSD_INNER + 2 * SSD_BC

D_FF = -(-8 * D_MODEL // (3 * 256)) * 256

IN_SIZES = (RET_QK, RET_QK, RET_V, RET_V, SSD_INNER, SSD_CONV_CH, SSD_HEADS, D_MODEL, D_MODEL)
D_IN = sum(IN_SIZES)


def rmsnorm(x, w):
    xf = x.astype(jnp.float32)
    y = xf * lax.rsqrt(jnp.mean(xf * xf, axis=-1, keepdims=True) + EPS)
    return (y * w.astype(jnp.float32)).astype(x.dtype)

def rotary(t, pos):
    half = t.shape[-1] // 2
    inv = ROPE_BASE ** (-jnp.arange(half, dtype=jnp.float32) / half)
    ang = pos.astype(jnp.float32)[:, None] * inv[None, :]
    cos = jnp.cos(ang)[None, :, None, :]
    sin = jnp.sin(ang)[None, :, None, :]
    t1, t2 = t[..., :half], t[..., half:]
    return jnp.concatenate([t1 * cos - t2 * sin, t1 * sin + t2 * cos], axis=-1)

def retention(q, k, v):
    bsz, s = q.shape[0], q.shape[1]
    nc = s // CHUNK
    log_g = jnp.log(1.0 - 2.0 ** (-5.0 - jnp.arange(RET_HEADS, dtype=jnp.float32)))
    idx = jnp.arange(CHUNK, dtype=jnp.float32)
    diff = idx[:, None] - idx[None, :]
    causal = diff >= 0
    intra = jnp.where(causal[None], jnp.exp(log_g[:, None, None] * jnp.maximum(diff, 0.0)[None]), 0.0)
    q_decay = jnp.exp(log_g[:, None] * (idx + 1.0))[None, :, :, None]
    k_decay = jnp.exp(log_g[:, None] * (CHUNK - 1.0 - idx))[None, :, :, None]
    chunk_decay = jnp.exp(log_g * CHUNK)[None, :, None, None]

    def to_chunks(t):
        return t.reshape(bsz, nc, CHUNK, RET_HEADS, t.shape[-1]).transpose(1, 0, 3, 2, 4)

    def step(state, inp):
        qc, kc, vc = inp
        sc = jnp.einsum('bhid,bhjd->bhij', qc, kc) * intra[None]
        y = jnp.einsum('bhij,bhjv->bhiv', sc, vc) + jnp.einsum('bhid,bhdv->bhiv', qc, state) * q_decay
        state = state * chunk_decay + jnp.einsum('bhjd,bhjv->bhdv', kc * k_decay, vc)
        return state, y

    init = jnp.zeros((bsz, RET_HEADS, RET_DK, RET_DV), jnp.float32)
    _, ys = lax.scan(step, init, (to_chunks(q), to_chunks(k), to_chunks(v)))
    return ys.transpose(1, 0, 3, 2, 4).reshape(bsz, s, RET_HEADS, RET_DV)

def ssd_scan(xdt, la, bm, cm):
    bsz, s = xdt.shape[0], xdt.shape[1]
    nc = s // CHUNK
    mask = jnp.tril(jnp.ones((CHUNK, CHUNK), dtype=bool))[None, :, :, None, None]

    def to_chunks(t):
        return jnp.moveaxis(t.reshape((bsz, nc, CHUNK) + t.shape[2:]), 1, 0)

    def step(state, inp):
        xc, lac, bc, cc = inp
        acs = jnp.cumsum(lac, axis=1)
        seg = acs[:, :, None] - acs[:, None, :]
        lmat = jnp.where(mask, jnp.exp(jnp.where(mask, seg, 0.0)), 0.0)
        cb = jnp.einsum('bign,bjgn->bijg', cc, bc)
        y = jnp.einsum('bijgr,bjgrp->bigrp', cb[..., None] * lmat, xc)
        y = y + jnp.einsum('bign,bgrpn->bigrp', cc, state) * jnp.exp(acs)[..., None]
        last = acs[:, -1]
        state = state * jnp.exp(last)[..., None, None] + jnp.einsum(
            'bjgn,bjgrp->bgrpn', bc, xc * jnp.exp(last[:, None] - acs)[..., None])
        return state, y

    init = jnp.zeros((bsz, SSD_GROUPS, SSD_HPG, SSD_HEADDIM, SSD_STATE), jnp.float32)
    _, ys = lax.scan(step, init, (to_chunks(xdt), to_chunks(la), to_chunks(bm), to_chunks(cm)))
    return jnp.moveaxis(ys, 0, 1).reshape(xdt.shape)

def causal_dwconv(x, w, b):
    out = lax.conv_general_dilated(
        x, w[:, None, :], window_strides=(1,), padding=[(SSD_CONV - 1, 0)],
        dimension_numbers=('NWC', 'WIO', 'NWC'), feature_group_count=x.shape[-1])
    return out + b

def hybrid_mixer(h, w_in, ret_out, conv_w, conv_b, dt_bias, a_log, d_skip, ssd_norm_w, ssd_out, w_o):
    bsz, s, _ = h.shape
    u = h @ w_in
    q, k, v, g_ret, z, xbc, dt, gate_ret, gate_ssd = jnp.split(u, list(np.cumsum(IN_SIZES)[:-1]), axis=-1)
    pos = jnp.arange(s)

    qf = rotary(q.astype(jnp.float32).reshape(bsz, s, RET_HEADS, RET_DK), pos)
    kf = rotary(k.astype(jnp.float32).reshape(bsz, s, RET_HEADS, RET_DK), pos) * (RET_DK ** -0.5)
    vf = v.astype(jnp.float32).reshape(bsz, s, RET_HEADS, RET_DV)
    yr = retention(qf, kf, vf)
    yr = yr * lax.rsqrt(jnp.mean(yr * yr, axis=-1, keepdims=True) + EPS)
    yr = (jax.nn.silu(g_ret.astype(jnp.float32)) * yr.reshape(bsz, s, RET_V)).astype(h.dtype)
    o_ret = yr @ ret_out

    xbc = jax.nn.silu(causal_dwconv(xbc, conv_w, conv_b))
    xs, bm, cm = jnp.split(xbc, [SSD_INNER, SSD_INNER + SSD_BC], axis=-1)
    xs = xs.astype(jnp.float32).reshape(bsz, s, SSD_GROUPS, SSD_HPG, SSD_HEADDIM)
    bm = bm.astype(jnp.float32).reshape(bsz, s, SSD_GROUPS, SSD_STATE)
    cm = cm.astype(jnp.float32).reshape(bsz, s, SSD_GROUPS, SSD_STATE)
    dtp = jax.nn.softplus(dt.astype(jnp.float32) + dt_bias.astype(jnp.float32))
    dtp = dtp.reshape(bsz, s, SSD_GROUPS, SSD_HPG)
    a = -jnp.exp(a_log.astype(jnp.float32)).reshape(SSD_GROUPS, SSD_HPG)
    ys = ssd_scan(xs * dtp[..., None], dtp * a, bm, cm)
    ys = ys + d_skip.astype(jnp.float32).reshape(SSD_GROUPS, SSD_HPG)[:, :, None] * xs
    ys = ys.reshape(bsz, s, SSD_INNER) * jax.nn.silu(z.astype(jnp.float32))
    ysg = ys.reshape(bsz, s, SSD_GROUPS, SSD_INNER // SSD_GROUPS)
    ysg = ysg * lax.rsqrt(jnp.mean(ysg * ysg, axis=-1, keepdims=True) + EPS)
    ys = (ysg.reshape(bsz, s, SSD_INNER) * ssd_norm_w.astype(jnp.float32)).astype(h.dtype)
    o_ssd = ys @ ssd_out

    merged = jax.nn.sigmoid(gate_ret) * o_ret + jax.nn.sigmoid(gate_ssd) * o_ssd
    return merged @ w_o

def swiglu(h, w_gate_up, w_down):
    gu = h @ w_gate_up
    gate, up = jnp.split(gu, [D_FF], axis=-1)
    return (jax.nn.silu(gate) * up) @ w_down

def second_inputs(seed: int = 0) -> dict:
    key = jax.random.key(seed)
    ks = jax.random.split(key, 20)
    f32 = jnp.float32

    def nrm(k, shape, fan_in):
        return jax.random.normal(k, shape, f32) * (fan_in ** -0.5)

    def gain(k, shape):
        return 1.0 + 0.02 * jax.random.normal(k, shape, f32)

    dt0 = jnp.exp(jax.random.uniform(ks[6], (DEPTH, SSD_HEADS), f32, math.log(1e-3), math.log(1e-1)))
    dt_bias = dt0 + jnp.log(-jnp.expm1(-dt0))
    a_log = jnp.log(jax.random.uniform(ks[7], (DEPTH, SSD_HEADS), f32, 1.0, 16.0))
    return {
        "x": jax.random.normal(ks[0], (BATCH, SEQ, D_MODEL), f32),
        "norm_mix_w": gain(ks[1], (DEPTH, D_MODEL)),
        "w_in": nrm(ks[2], (DEPTH, D_MODEL, D_IN), D_MODEL),
        "ret_out": nrm(ks[3], (DEPTH, RET_V, D_MODEL), RET_V),
        "conv_w": nrm(ks[4], (DEPTH, SSD_CONV, SSD_CONV_CH), SSD_CONV),
        "conv_b": 0.02 * jax.random.normal(ks[5], (DEPTH, SSD_CONV_CH), f32),
        "dt_bias": dt_bias,
        "a_log": a_log,
        "d_skip": gain(ks[8], (DEPTH, SSD_HEADS)),
        "ssd_norm_w": gain(ks[9], (DEPTH, SSD_INNER)),
        "ssd_out": nrm(ks[10], (DEPTH, SSD_INNER, D_MODEL), SSD_INNER),
        "w_o": nrm(ks[11], (DEPTH, D_MODEL, D_MODEL), D_MODEL),
        "norm_ffn_w": gain(ks[12], (DEPTH, D_MODEL)),
        "w_gate_up": nrm(ks[13], (DEPTH, D_MODEL, 2 * D_FF), D_MODEL),
        "w_down": nrm(ks[14], (DEPTH, D_FF, D_MODEL), D_FF),
        "final_norm_w": gain(ks[15], (D_MODEL,)),
    }

def second_block(x, norm_mix_w, w_in, ret_out, conv_w, conv_b, dt_bias, a_log, d_skip, ssd_norm_w,
              ssd_out, w_o, norm_ffn_w, w_gate_up, w_down, final_norm_w):
    h = x
    for l in range(DEPTH):
        h = h + hybrid_mixer(rmsnorm(h, norm_mix_w[l]), w_in[l], ret_out[l], conv_w[l], conv_b[l],
                             dt_bias[l], a_log[l], d_skip[l], ssd_norm_w[l], ssd_out[l], w_o[l])
        h = h + swiglu(rmsnorm(h, norm_ffn_w[l]), w_gate_up[l], w_down[l])
    return rmsnorm(h, final_norm_w)


def setup_inputs(seed=0):
    out = dict(first_inputs(seed))
    for name, value in second_inputs(seed + 1).items():
        if name != "x":
            out[name + "_2"] = value
    return out


def reference(
    x, norm_mix_g, norm_ffn_g, even_w_in, rw_mu, rw_w0, rw_w2, rw_a0, rw_a2, rw_g2, rw_k_k,
    rw_k_a, rw_r_k, rw_ln_g, rw_ln_b, rw_v0, rw_v1, rw_v2, pool_w, pool_scale, even_w_out,
    odd_w_in, da_q_norm, da_k_norm, da_lam_q1, da_lam_k1, da_lam_q2, da_lam_k2, da_subln,
    s5_a_re, s5_a_im, s5_log_step, s5_b_re, s5_b_im, s5_c_re, s5_c_im, s5_d, s5_w_glu,
    odd_w_out, moe_w_group, moe_b_group, moe_w_expert, moe_b_expert, moe_w_gate, moe_w_up,
    moe_w_down, norm_mix_w_2, w_in_2, ret_out_2, conv_w_2, conv_b_2, dt_bias_2, a_log_2,
    d_skip_2, ssd_norm_w_2, ssd_out_2, w_o_2, norm_ffn_w_2, w_gate_up_2, w_down_2,
    final_norm_w_2,
):
    x = first_block(
        x, norm_mix_g, norm_ffn_g, even_w_in, rw_mu, rw_w0, rw_w2, rw_a0, rw_a2, rw_g2, rw_k_k,
        rw_k_a, rw_r_k, rw_ln_g, rw_ln_b, rw_v0, rw_v1, rw_v2, pool_w, pool_scale, even_w_out,
        odd_w_in, da_q_norm, da_k_norm, da_lam_q1, da_lam_k1, da_lam_q2, da_lam_k2, da_subln,
        s5_a_re, s5_a_im, s5_log_step, s5_b_re, s5_b_im, s5_c_re, s5_c_im, s5_d, s5_w_glu,
        odd_w_out, moe_w_group, moe_b_group, moe_w_expert, moe_b_expert, moe_w_gate, moe_w_up,
        moe_w_down,
    )
    return second_block(
        x, norm_mix_w_2, w_in_2, ret_out_2, conv_w_2, conv_b_2, dt_bias_2, a_log_2, d_skip_2,
        ssd_norm_w_2, ssd_out_2, w_o_2, norm_ffn_w_2, w_gate_up_2, w_down_2, final_norm_w_2,
    )


_drawn_inputs = setup_inputs


def setup_inputs(seed=0):
    import zlib

    import numpy as np

    out = dict(_drawn_inputs(seed))
    spreads = {}
    factors = {'rw_a0': 2.94,
     'rw_ln_g': 3.434,
     'rw_ln_b': 2.908,
     'da_q_norm': 4.146,
     'da_k_norm': 6.255,
     'da_lam_q1': 3.899,
     'da_lam_k1': 5.083,
     'da_subln': 4.423,
     's5_a_re': 64.0,
     's5_a_im': 24.928,
     's5_log_step': 23.016,
     's5_b_re': 25.064,
     's5_b_im': 30.112,
     's5_c_re': 25.528,
     's5_c_im': 28.512,
     'moe_b_group': 3.385,
     'moe_b_expert': 3.596,
     'conv_b_2': 3.132,
     'd_skip_2': 6.34,
     'ssd_norm_w_2': 4.168,
     'norm_ffn_w_2': 2.98,
     'final_norm_w_2': 8.259}
    for name, (base, spread) in spreads.items():
        noise = np.random.default_rng([zlib.crc32(name.encode()), seed]).standard_normal(out[name].shape)
        drawn = base * np.exp(spread * noise) if base else spread * noise
        out[name] = jnp.asarray(drawn.astype(out[name].dtype))
    for name, factor in factors.items():
        out[name] = (out[name] * factor).astype(out[name].dtype)
    return out
```

```python
import math
from contextlib import ExitStack

import numpy as np

import concourse.bass as bass
from concourse import mybir
from concourse.alu_op_type import AluOpType as ALU

F32 = mybir.dt.float32
ACT = mybir.ActivationFunctionType
AX = mybir.AxisListType
T = 256
NSLOT = 6
SLOT = 4096
NE = 32
STAGES = ["even", "moe0", "odd", "moe1", "hyb0", "ffn0", "hyb1", "ffn1", "fin"]

PCOLS = [
    ("g_even", 8), ("g_moe0", 8), ("g_odd", 8), ("g_moe1", 8), ("g_hyb0", 8), ("g_ffn0", 8),
    ("g_hyb1", 8), ("g_ffn1", 8), ("mu", 14), ("w0", 4), ("a0", 4), ("k_k", 4), ("k_a", 4),
    ("r_k", 4), ("ln_g", 4), ("ln_b", 4), ("pool_scale", 4), ("qn", 1), ("kn", 1), ("subln", 1),
    ("s5_re", 16), ("s5_im", 16), ("s5_ls", 16), ("s5_d", 4), ("lam", 256), ("rb0", 36),
    ("rb1", 36), ("eps6", 1), ("eps5", 1), ("epsln", 1), ("one", 1), ("hpi", 1), ("ident", 128), ("ones", 128),
    ("ones64", 128), ("tri", 128), ("iota", 32),
]
CAP = 32


def pcol_table():
    at, out = 0, {}
    for name, n in PCOLS:
        out[name] = (at, n)
        at += n
    return out, at


PT, NP = pcol_table()


def chunk_table(stages):
    out = []
    for st in stages:
        if st == "even":
            out += [(f"even_in{i}", 8, 512 if i < 4 else 256) for i in range(5)]
            out += [("lora", 3, 512)]
            out += [("even_out0", 8, 512), ("even_out1", 8, 512)]
        if st in ("moe0", "moe1"):
            out += [(st + "_r", 8, 36)]
            for q in range(NE // 4):
                out += [(f"{st}_g{q}_{c}", 8, 512) for c in range(4)]
                out += [(f"{st}_u{q}_{c}", 8, 512) for c in range(4)]
                out += [(f"{st}_d{q}_{c}", 4, 1024) for c in range(4)]
        if st == "odd":
            out += [(f"odd_in{i}", 8, 512) for i in range(4)]
            out += [("s5_B", 1, 4096), ("s5_C", 1, 4096), ("glu", 4, 512)]
            out += [("odd_out0", 8, 512), ("odd_out1", 8, 512)]
        if st in ("hyb0", "hyb1"):
            for h in range(4):
                out += [(f"{st}_qk{h}", 8, 512), (f"{st}_v{h}", 8, 512), (f"{st}_g{h}", 8, 512)]
            out += [(f"{st}_gr{i}", 8, 512) for i in range(2)]
            out += [(f"{st}_ro{i}", 16, 256) for i in range(4)]
            out += [(f"{st}_dt", 8, 32)]
            for g in range(4):
                out += [(f"{st}_xs{g}", 8, 512), (f"{st}_bc{g}", 8, 256), (f"{st}_z{g}", 8, 512)]
            out += [(f"{st}_gs{i}", 8, 512) for i in range(2)]
            out += [(f"{st}_so{i}", 16, 256) for i in range(4)]
            out += [(f"{st}_wo{i}", 8, 512) for i in range(2)]
        if st in ("ffn0", "ffn1"):
            out += [(f"{st}_gu{i}", 8, 512) for i in range(11)]
            out += [(f"{st}_dn{i}", 4 if i < 5 else 2, 1024) for i in range(6)]
        if st == "fin":
            out += [("fin_w", 1, 1024)]
    return out


def const_table(stages):
    n = {"even": 1184, "odd": 1152, "hyb0": 2008, "hyb1": 2008}
    return [(s + "_c", n[s]) for s in stages if s in n]


class Eng:

    def __init__(self, name, sem):
        self.name, self.sem, self.n, self.q, self.seen = name, sem, 0, [], {}
        self.open = False

    def wait(self, *toks):
        for t in toks:
            if t is None:
                continue
            sem, v = t
            if v > self.seen.get(id(sem), 0):
                self.seen[id(sem)] = v
                self.q.append((0, sem, v))

    def op(self, fn, w=(), chain=True, inc=True):
        self.wait(*w)
        if chain:
            self.wait((self.sem, self.n))
        if inc:
            self.n += 1
        self.open = not inc
        self.q.append((1, fn, inc))
        return (self.sem, self.n)

    def dma(self, out, in_, sem, w=()):
        self.wait(*w)
        self.q.append((2, out, in_, sem))

    @property
    def last(self):
        assert not self.open, self.name
        return (self.sem, self.n)

    def branch(self, flag, least, sub):
        self.q.append((3, flag, least, sub))

    def emit(self, eng):
        for e in self.q:
            if e[0] == 3:
                with eng.If(eng.value_load(e[1], min_val=0, max_val=1 << 20) > e[2]):
                    e[3].emit(eng)
            elif e[0] == 0:
                eng.wait_ge(e[1], e[2])
            elif e[0] == 1:
                r = e[1](eng)
                if e[2]:
                    r.then_inc(self.sem, 1)
            else:
                eng.dma_start(e[1], e[2]).then_inc(e[3], 16)


class Vec(Eng):
    def tt(self, out, a, b, op, w=()):
        return self.op(lambda e: e.tensor_tensor(out, a, b, op), w)

    def ts(self, out, a, s1, s2, op0, op1=None, w=()):
        if op1 is None:
            return self.op(lambda e: e.tensor_scalar(out, a, s1, None, op0), w)
        return self.op(lambda e: e.tensor_scalar(out, a, s1, s2, op0, op1), w)

    def stt(self, out, a, s, b, op0, op1, w=(), accum=None):
        if accum is None:
            return self.op(lambda e: e.scalar_tensor_tensor(out=out, in0=a, scalar=s, in1=b, op0=op0, op1=op1), w)
        return self.op(lambda e: e.scalar_tensor_tensor(out=out, in0=a, scalar=s, in1=b, op0=op0, op1=op1,
                                                        accum_out=accum), w)

    def cp(self, out, a, w=()):
        return self.op(lambda e: e.tensor_copy(out, a), w)

    def set(self, out, v, w=()):
        return self.op(lambda e: e.memset(out, v), w)

    def scan(self, out, d0, d1, init, op0, op1, w=()):
        return self.op(lambda e: e.tensor_tensor_scan(out, d0, d1, init, op0, op1), w)

    def red(self, out, a, op, w=()):
        return self.op(lambda e: e.tensor_reduce(out, a, AX.X, op), w)

    def rcp(self, out, a, w=()):
        return self.op(lambda e: e.reciprocal(out, a), w)


class Sca(Eng):
    def act(self, out, a, f, w=(), bias=0.0, scale=1.0):
        return self.op(lambda e: e.activation(out, a, f, bias=bias, scale=scale), w)

    def cp(self, out, a, w=()):
        return self.op(lambda e: e.activation(out, a, ACT.Copy), w)


class Ten(Eng):
    def mm(self, out, l, r, start, stop, w=(), inc=False):
        return self.op(lambda e: e.matmul(out, l, r, start=start, stop=stop), w, chain=False, inc=inc)

    def tr(self, out, a, ident, w=(), inc=False):
        return self.op(lambda e: e.transpose(out, a, ident), w, chain=False, inc=inc)


def program(nc, Wd, Pd, x_in, out_d, stages):
    ctx = ExitStack()
    with ctx:
        def sb(name, n):
            return ctx.enter_context(nc.sbuf_tensor(name, [128, n], F32))

        def sem(name):
            return ctx.enter_context(nc.semaphore(name))

        ring = sb("ring", NSLOT * SLOT)
        X = sb("x", 2048)[:, :].rearrange("p (t d) -> p t d", t=2)
        HT = sb("ht", 2048)[:, :].rearrange("p (k t) -> p k t", k=8)
        PP = sb("pp", NP)
        GS = sb("gs", 128)
        CS_T = sb("cst", 2008)
        FLAG = ctx.enter_context(nc.sbuf_tensor("flag", [128, 2], mybir.dt.int32))
        NA = 20992
        AR = sb("arena", NA)
        ps = ctx.enter_context(nc.psum_tensor("ps", [128, 8, 512], F32))

        V = Vec("v", sem("s_v"))
        A = Sca("a", sem("s_a"))
        PE = Ten("pe", sem("s_pe"))
        SP = Eng("sp", sem("s_sp"))
        s_slot = [sem(f"s_slot{i}") for i in range(NSLOT)]
        s_in = sem("s_in")
        s_over = [[sem(f"s_over{l}{n}") for n in ("v", "a", "pe", "dma")] for l in range(2)]
        s_const = sem("s_const")
        G = Eng("g", sem("s_g"))
        s_out = sem("s_out")

        def par(name, i=0, n=1):
            at = PT[name][0]
            return PP[:, at + i:at + i + n]

        ident, ones, ones64 = par("ident", 0, 128), par("ones", 0, 128), par("ones64", 0, 128)

        chunks = chunk_table(stages)
        offs, at = [], 0
        for _, k, n in chunks:
            offs.append(at)
            at += 128 * k * n
        st = {"take": 0, "sent": 0}
        freed = {}

        coffs, cn = {}, at
        for name, n in const_table(stages):
            coffs[name] = (cn, n)
            cn += 128 * n

        def consts(name):
            o, n = coffs[name]
            if st.get("cname") == name:
                return CS_T[:, 0:n], (s_const, 16 * st["consts"])
            st["cname"] = name
            st["consts"] = st.get("consts", 0) + 1
            G.dma(CS_T[:, 0:n], Wd[o:o + 128 * n].rearrange("(p n) -> p n", p=128), s_const,
                  [V.last, A.last, PE.last])
            return CS_T[:, 0:n], (s_const, 16 * st["consts"])

        def send(w=()):
            i = st["sent"]
            if i >= len(chunks):
                return
            _, k, n = chunks[i]
            s = i % NSLOT
            SP.dma(ring[:, s * SLOT:s * SLOT + k * n],
                   Wd[offs[i]:offs[i] + 128 * k * n].rearrange("(p n) -> p n", p=128), s_slot[s], w)
            st["sent"] += 1

        class Chunk:
            def __init__(self, i):
                name, k, n = chunks[i]
                s = i % NSLOT
                self.i = i
                self.ap = ring[:, s * SLOT:s * SLOT + k * n].rearrange("p (k n) -> p k n", k=k)
                self.tok = (s_slot[s], 16 * (i // NSLOT + 1))

            def free(self, *toks):
                freed[self.i] = toks
                while st["sent"] - NSLOT in freed and st["sent"] < len(chunks):
                    send(freed[st["sent"] - NSLOT])

        def take(name):
            i = st["take"]
            assert chunks[i][0] == name, (chunks[i], name)
            st["take"] += 1
            return Chunk(i)

        SP.dma(PP[:, :], Pd, s_in)
        SP.dma(X, x_in.rearrange("(t p) d -> p t d", p=128), s_in)
        for _ in range(NSLOT):
            send()
        tin = (s_in, 32)
        for e in (V, A, PE):
            e.wait(tin)

        free_banks = [(b, ()) for b in range(8)]

        def bank():
            b, toks = free_banks.pop(0)
            PE.wait(*toks)
            return b, ps[:, b, :]

        def rel(b, *toks):
            free_banks.append((b, toks))

        ar = {"at": 0}

        def buf(*shape):
            n = int(np.prod(shape))
            a = ar["at"]
            ar["at"] += n
            assert ar["at"] <= NA, ar["at"]
            v = AR[:, a:a + n]
            if len(shape) == 2:
                return v.rearrange("p (a b) -> p a b", a=shape[0])
            if len(shape) == 3:
                return v.rearrange("p (a b c) -> p a b c", a=shape[0], b=shape[1])
            return v

        def fence():
            toks = [V.last, A.last, PE.last]
            for e in (V, A, PE):
                e.wait(*toks)

        def phase():
            fence()
            ar["at"] = 0

        def bc(v, shape):
            return v.broadcast_to(list(shape))

        def norm_T(gname):
            sq, xn, ss = buf(2, 1024), buf(2, 1024), buf(4)
            for t in range(2):
                V.stt(sq[:, t, :], X[:, t, :], 1.0, X[:, t, :], ALU.mult, ALU.mult, accum=ss[:, t:t + 1])
            t1 = A.act(ss[:, 2:4], ss[:, 0:2], ACT.Ln, [V.last], bias=par("eps6"), scale=1.0 / 1024)
            t2 = A.act(ss[:, 0:2], ss[:, 2:4], ACT.Exp, scale=-0.5)
            tx = [V.ts(xn[:, t, :], X[:, t, :], ss[:, t:t + 1], None, ALU.mult, w=[t2]) for t in range(2)]
            for k in range(0, 8, 2):
                b, p = bank()
                for kk in (k, k + 1):
                    for t in range(2):
                        tp = PE.tr(p[:, (kk - k) * 256 + t * 128:(kk - k) * 256 + t * 128 + 128],
                                   xn[:, t, kk * 128:(kk + 1) * 128], ident, [tx[t]],
                                   inc=(kk == k + 1 and t == 1))
                if k % 4 == 0:
                    V.ts(HT[:, k, :], p[:, 0:256], par(gname, k), None, ALU.mult, w=[tp])
                    e0 = V.ts(HT[:, k + 1, :], p[:, 256:512], par(gname, k + 1), None, ALU.mult)
                    rel(b, e0)
                else:
                    A.act(HT[:, k, :], p[:, 0:256], ACT.Copy, [tp], scale=par(gname, k))
                    e1 = A.act(HT[:, k + 1, :], p[:, 256:512], ACT.Copy, scale=par(gname, k + 1))
                    rel(b, e1)
            return xn

        def proj_T(c, cols, rhs, K, w=()):
            b, p = bank()
            for n, c0 in enumerate(cols):
                for k in range(K):
                    t = PE.mm(p[:, n * 256:(n + 1) * 256], c.ap[:, k, c0:c0 + 128], rhs[:, k, :],
                              k == 0, k == K - 1, [c.tok, *w], inc=(k == K - 1 and n == len(cols) - 1))
            return b, p, t

        def proj_tok(c, lhs, K, t, c0, n, w=(), p=None, start=True, stop=True, kl=0):
            if p is None:
                b, p = bank()
            else:
                b, p = p
            for k in range(K):
                tk = PE.mm(p[:, 0:n], lhs[:, kl + k, t * 128:(t + 1) * 128], c.ap[:, k, c0:c0 + n],
                           start and k == 0, stop and k == K - 1, [c.tok, *w], inc=(k == K - 1))
            return b, p, tk

        def out_proj(names, lhs, w):
            for i, name in enumerate(names):
                c = take(name)
                for t in range(2):
                    b, p, tk = proj_tok(c, lhs, 8, t, 0, 512, w)
                    xs = X[:, t, i * 512:(i + 1) * 512]
                    rel(b, V.tt(xs, p, xs, ALU.add, [tk]))
                c.free(tk)

        def even():
            phase()
            consts("even_c")
            norm_T("g_even")
            phase()
            M = buf(14, 256)
            LD, AA, GG, KK = (buf(4, 256) for _ in range(4))
            OT, YT = buf(8, 256), buf(4, 256)
            base = ar["at"]
            U = buf(18, 256)
            cv, tcst = consts("even_c")
            for i in range(5):
                c = take(f"even_in{i}")
                for j in range(0, 4 if i < 4 else 2, 2):
                    b, p, tk = proj_T(c, [j * 128, j * 128 + 128], HT, 8)
                    f = i * 4 + j
                    rel(b, A.cp(U[:, f:f + 2, :], p.rearrange("p (a b) -> p a b", a=2), [tk]))
                c.free(tk)
            lora = take("lora")
            t0 = A.last
            V.tt(M[:, :, 1:256], U[:, 0:14, 0:255], U[:, 0:14, 1:256], ALU.subtract, [t0])
            V.ts(M[:, :, 0:1], U[:, 0:14, 0:1], -1.0, None, ALU.mult)
            for f in range(14):
                V.stt(M[:, f, :], M[:, f, :], par("mu", f), U[:, f, :], ALU.mult, ALU.add)
            tm = V.last
            ta = A.act(U[:, 0:1, :], M[:, 12:13, :], ACT.Tanh, [tm])
            tg = A.act(U[:, 1:2, :], M[:, 13:14, :], ACT.Sigmoid)
            W0, W1 = U[:, 2:6, :], U[:, 6:10, :]
            src, dst = U[:, 14:18, :], W0
            for lv in range(4):
                s = 1 << lv
                g0 = lv
                V.tt(dst[:, g0:4, s:256], src[:, g0:4, s:256], src[:, g0:4, 0:256 - s], ALU.add, [ta, tg])
                V.cp(dst[:, g0:4, 0:s], src[:, g0:4, 0:s])
                V.ts(U[:, 10 + lv, :], dst[:, lv, :], 1.0 / (2 << lv), None, ALU.mult)
                src, dst = dst, (W1 if dst is W0 else W0)
            PD = U[:, 10:14, :]
            V.tt(PD[:, :, 0:16], PD[:, :, 0:16], cv[:, 1088:1152].rearrange("p (a b) -> p a b", a=4), ALU.mult,
                 [tcst])
            V.tt(PD, PD, U[:, 14:18, :], ALU.subtract)
            tpd = V.last
            for g in range(0, 4, 2):
                b, p = bank()
                for gg in range(2):
                    tk = PE.mm(p[:, gg * 256:(gg + 1) * 256], lora.ap[:, 2, (g + gg) * 128:(g + gg + 1) * 128],
                               PD[:, g + gg, :], True, True, [tpd, lora.tok], inc=(gg == 1))
                for gg in range(2):
                    e = V.ts(OT[:, 4 + g + gg, :], p[:, gg * 256:(gg + 1) * 256], par("pool_scale", g + gg), None,
                             ALU.mult, w=[tk])
                rel(b, e)
            for j in range(0, 4, 2):
                bw, pw = bank()
                ba, pa = bank()
                bg, pg = bank()
                for i in range(2):
                    cs = slice((j + i) * 128, (j + i + 1) * 128)
                    o = slice(i * 256, (i + 1) * 256)
                    tw = PE.mm(pw[:, o], lora.ap[0:64, 0, cs], U[0:64, 0, :], True, True, [ta], inc=(i == 1))
                    tg2 = PE.mm(pg[:, o], lora.ap[:, 1, cs], U[:, 1, :], True, True, [tg], inc=(i == 1))
                for i in range(2):
                    cs = slice((j + i) * 128, (j + i + 1) * 128)
                    o = slice(i * 256, (i + 1) * 256)
                    tq = PE.mm(pa[:, o], lora.ap[64:128, 0, cs], M[64:128, 12, :], True, True, [tm], inc=(i == 1))
                for i in range(2):
                    o = slice(i * 256, (i + 1) * 256)
                    e1 = A.act(LD[:, j + i, :], pw[:, o], ACT.Sigmoid, [tw], bias=par("w0", j + i))
                    e2 = A.act(AA[:, j + i, :], pa[:, o], ACT.Sigmoid, [tq], bias=par("a0", j + i))
                e3 = A.cp(GG[:, j:j + 2, :], pg.rearrange("p (a b) -> p a b", a=2), [tg2])
                rel(bw, e1)
                rel(ba, e2)
                rel(bg, e3)
            lora.free(PE.last)
            V.ts(LD, LD, -math.exp(-0.5), None, ALU.mult, w=[A.last])
            R, K2, VV = M[:, 0:4, :], M[:, 4:8, :], M[:, 8:12, :]
            TMP, TM2 = U[:, 2:6, :], U[:, 6:10, :]
            for j in range(4):
                V.ts(KK[:, j, :], K2[:, j, :], par("k_k", j), None, ALU.mult)
            tk = V.tt(TMP, KK, KK, ALU.mult, [PE.last])
            for j in range(0, 4, 2):
                b, p = bank()
                for i in range(2):
                    t = PE.mm(p[:, i * 256:(i + 1) * 256], ones64, TMP[:, j + i, :], True, True, [tk], inc=(i == 1))
                rel(b, V.ts(TM2[:, j:j + 2, :], p.rearrange("p (a b) -> p a b", a=2), 1e-24, None, ALU.max, w=[t]))
            t = A.act(TM2, TM2, ACT.Sqrt, [V.last])
            V.rcp(TM2, TM2, [t])
            V.tt(KK, KK, TM2, ALU.mult)
            for j in range(4):
                V.ts(TMP[:, j, :], AA[:, j, :], 1.0, par("k_a", j), ALU.subtract, ALU.mult, w=[PE.last])
            V.stt(K2, TMP, 1.0, K2, ALU.add, ALU.mult)
            for j in range(4):
                V.stt(TMP[:, j, :], R[:, j, :], par("r_k", j), K2[:, j, :], ALU.mult, ALU.mult)
            tk = V.last
            BON = OT[:, 0:4, :]
            for j in range(0, 4, 2):
                b, p = bank()
                for i in range(2):
                    t = PE.mm(p[:, i * 256:(i + 1) * 256], ones64, TMP[:, j + i, :], True, True, [tk], inc=(i == 1))
                rel(b, V.tt(BON[:, j:j + 2, :], p.rearrange("p (a b) -> p a b", a=2), VV[:, j:j + 2, :], ALU.mult, [t]))
            fence()

            ar["at"] = base
            XX = buf(4, 128)
            xf = XX.rearrange("p c n -> p (c n)")
            CU, PI = xf[:, 0:256], xf[:, 256:512]
            PT_, PV = (buf(256) for _ in range(2))
            ah, bh, kh, rh, bp, kp = (buf(256) for _ in range(6))
            Bs = [buf(512) for _ in range(14)]
            VS = buf(4, 64)
            LRB, LRK = (M[:, i, :].rearrange("p (c n) -> p c n", c=4) for i in (12, 13))
            BS, QS, CS, SS = (v.rearrange("p (c n) -> p c n", c=4) for v in (bp, PV, kp, bh))
            mB, mDT, mD, mO, mL = (cv[:, i * 128:(i + 1) * 128] for i in range(5))
            mR, i2 = cv[:, 640:704], cv[:, 704:768]
            ones1 = cv[:, 1152:1153]

            def c4(v):
                return v.rearrange("p (c n) -> p c n", c=4)

            def bd(dst, src, mask, w=()):
                for _ in range(1):
                    d = dst.rearrange("p (c h n) -> p c h n", c=4, h=2)
                    s4 = src.unsqueeze(2).broadcast_to([128, 4, 2, 64])
                    m4 = mask.rearrange("p (h n) -> p h n", h=2).unsqueeze(1).broadcast_to([128, 4, 2, 64])
                    return V.tt(d, s4, m4, ALU.mult, w)

            def mul(p, l, r, n, w, more=()):
                pairs = [(l, r), *more]
                for c in range(4):
                    for i, (ll, rr) in enumerate(pairs):
                        last = i == len(pairs) - 1
                        t = PE.mm(p[:, c * n:(c + 1) * n], ll.rearrange("p (c n) -> p c n", c=4)[:, c, :], rr[:, c, :],
                                  i == 0, last, w, inc=(last and c == 3))
                return t

            for hp in range(4):
                fence()
                for c in range(4):
                    s = slice(c * 64, (c + 1) * 64)
                    V.scan(CU[:, s], bc(ones1, [128, 64]), LD[:, hp, s], 0.0, ALU.mult, ALU.add)
                V.tt(PV, CU, LD[:, hp, :], ALU.subtract)
                tv = V.last
                A.act(PT_, CU, ACT.Exp, [tv])
                A.act(PI, CU, ACT.Exp, scale=-1.0)
                te = A.act(PV, PV, ACT.Exp)
                V.stt(ah, KK[:, hp, :], -1.0, PV, ALU.mult, ALU.mult, [te])
                V.tt(bh, KK[:, hp, :], AA[:, hp, :], ALU.mult)
                V.tt(bh, bh, PI, ALU.mult)
                V.tt(kh, K2[:, hp, :], PI, ALU.mult)
                V.tt(rh, R[:, hp, :], PT_, ALU.mult)
                PC = c4(PT_)[:, :, 63:64]
                V.tt(c4(bp), c4(bh), bc(PC, [128, 4, 64]), ALU.mult)
                V.tt(c4(kp), c4(kh), bc(PC, [128, 4, 64]), ALU.mult)
                srcs = [c4(bh), c4(kh), c4(ah), c4(VV[:, hp, :]), c4(bp), c4(kp)]
                for i, s in enumerate(srcs):
                    bd(Bs[i], s, mB)
                tb = V.last
                bF, kF, aF, vF, bPF, kPF = Bs[0:6]
                D, DT, O, LK, Vb, Bb, Kb = Bs[6:13]
                I2 = [i2] * 4

                def tr_all(p, l, w):
                    for c in range(4):
                        t = PE.mm(p[:, c * 64:(c + 1) * 64], l.rearrange("p (c n) -> p c n", c=4)[:, c, :], i2,
                                  True, True, w, inc=(c == 3))
                    return t

                b0, p0 = bank()
                b1, p1 = bank()
                b2, p2 = bank()
                b3, p3 = bank()
                b4, p4 = bank()
                LabT, Lab = c4(p0[:, 0:256]), c4(p0[:, 256:512])
                t1 = mul(p0[:, 0:256], bF, c4(ah), 64, [tb])
                t2 = mul(p0[:, 256:512], aF, c4(bh), 64, [tb])
                t3 = mul(p1[:, 0:256], kF, c4(ah), 64, [tb])
                t4 = mul(p1[:, 256:512], bF, c4(rh), 64, [tb])
                t5 = mul(p2[:, 0:256], kF, c4(rh), 64, [tb])
                t6 = tr_all(p2[:, 256:512], vF, [tb])
                t7 = tr_all(p3[:, 0:256], bPF, [tb])
                t8 = tr_all(p3[:, 256:512], kPF, [tb])
                t9 = tr_all(p4[:, 0:256], aF, [tb])
                bd(DT, LabT, mDT, [t2])
                bd(D, Lab, mD, [t2])
                bd(O, Lab, mO)
                rel(b0, V.last)
                bd(LK, c4(p1[:, 0:256]), mL, [t4])
                mR4 = mR.unsqueeze(1).broadcast_to([128, 4, 64])
                rel(b1, V.tt(LRB, c4(p1[:, 256:512]), mR4, ALU.mult, [t4]))
                V.tt(LRK, c4(p2[:, 0:256]), mR4, ALU.mult, [t6])
                V.cp(VS, c4(p2[:, 256:512]), [t6])
                rel(b2, bd(Vb, c4(p2[:, 256:512]), mB))
                V.cp(BS, c4(p3[:, 0:256]), [t8])
                bd(Bb, c4(p3[:, 0:256]), mB)
                rel(b3, bd(Kb, c4(p3[:, 256:512]), mB, [t8]))
                rel(b4, V.cp(XX[:, :, 0:64], c4(p4[:, 0:256]), [t9]))
                tx = V.last
                b, p = bank()
                t = mul(p[:, 0:256], LK, VS, 64, [tx])
                rel(b, V.cp(XX[:, :, 64:128], c4(p[:, 0:256]), [t]))
                D2, D2T, D4, D4T, D8, ET = Bs[0:6]
                idb = ident.unsqueeze(1).broadcast_to([128, 4, 128])
                V.tt(c4(ET), c4(DT), idb, ALU.add, [t9])

                def sq(dst, l, r, w=(), add=None):
                    b, p = bank()
                    t = mul(p, l, c4(r), 128, [V.last, A.last])
                    if add is None:
                        e = A.cp(dst, p, [t])
                    else:
                        e = V.tt(dst, p, add, ALU.add, [t])
                    rel(b, e)

                sq(D2, DT, D)
                sq(D2T, D, DT)
                sq(D4, D2T, D2)
                sq(D4T, D2, D2T)
                sq(ET, D2, ET, add=ET)
                sq(D8, D4T, D4)
                sq(ET, D4, ET, add=ET)
                sq(ET, D8, ET, add=ET)
                G, G2T, GT = Bs[0], Bs[1], Bs[2]
                fence()
                sq(G, ET, O)
                sq(GT, O, ET)
                sq(G2T, G, GT)
                for i, l in enumerate((ET, G2T, GT)):
                    b, p = bank()
                    t = mul(p, l, XX, 128, [V.last, A.last])
                    rel(b, V.tt(xf, p, xf, ALU.add, [t]) if i else V.cp(xf, p, [t]))
                M1, M2, AT, ST = Bs[3], Bs[4], Bs[5], Bs[13]
                bd(M1, XX[:, :, 0:64], mB)
                bd(M2, XX[:, :, 64:128], mB)
                tx = V.last
                MS = XX[:, :, 64:128]
                b, p = bank()
                t1 = mul(p[:, 0:256], M1, LRB, 64, [tx])
                t2 = mul(p[:, 256:512], M1, BS, 64, [tx])
                V.tt(QS, c4(p[:, 0:256]), c4(rh), ALU.add, [t2])
                V.tt(CS, i2.unsqueeze(1).broadcast_to([128, 4, 64]), bc(PC, [128, 4, 64]), ALU.mult)
                rel(b, V.tt(CS, c4(p[:, 256:512]), CS, ALU.add, [t2]))
                bd(AT, CS, mB)
                b, p = bank()
                t = mul(p[:, 0:256], Bb, MS, 64, [tx], more=[(Kb, VS)])
                rel(b, V.cp(CS, c4(p[:, 0:256]), [t]))
                V.cp(SS[:, 0, :], CS[:, 0, :])
                for c in range(1, 3):
                    b, p = bank()
                    t = PE.mm(p[:, 0:64], c4(AT)[:, c, :], SS[:, c - 1, :], True, True, [V.last], inc=True)
                    rel(b, V.tt(SS[:, c, :], p[:, 0:64], CS[:, c, :], ALU.add, [t]))
                V.set(SS[:, 3, :], 0.0)
                bd(ST, SS, mB)
                tx = V.last
                b, p = bank()
                for c in range(4):
                    o = p[:, c * 64:(c + 1) * 64]
                    PE.mm(o, c4(M2)[:, c, :], LRB[:, c, :], True, False, [tx])
                    t = PE.mm(o, c4(Vb)[:, c, :], LRK[:, c, :], False, c == 0, inc=(c == 0))
                    if c:
                        t = PE.mm(o, c4(ST)[:, c - 1, :], QS[:, c, :], False, True, inc=True)
                rel(b, V.cp(YT[:, hp, :], p[:, 0:256], [t]))
            fence()
            ar["at"] = base
            Y2, RS = buf(4, 256), buf(4, 256)
            for j in range(0, 4, 2):
                b, p = bank()
                for i in range(2):
                    t = PE.mm(p[:, i * 256:(i + 1) * 256], ones64, YT[:, j + i, :], True, True, [V.last], inc=(i == 1))
                pv = p.rearrange("p (a b) -> p a b", a=2)
                rel(b, V.stt(YT[:, j:j + 2, :], pv, -1.0 / 64, YT[:, j:j + 2, :], ALU.mult, ALU.add, [t]))
            tk = V.tt(Y2, YT, YT, ALU.mult)
            for j in range(0, 4, 2):
                b, p = bank()
                for i in range(2):
                    t = PE.mm(p[:, i * 256:(i + 1) * 256], ones64, Y2[:, j + i, :], True, True, [tk], inc=(i == 1))
                rel(b, A.act(RS[:, j:j + 2, :], p.rearrange("p (a b) -> p a b", a=2), ACT.Ln, [t],
                             bias=par("epsln"), scale=1.0 / 64))
            t = A.act(RS, RS, ACT.Exp, scale=-0.5)
            V.tt(YT, YT, RS, ALU.mult, [t])
            for j in range(4):
                V.ts(YT[:, j, :], YT[:, j, :], par("ln_g", j), par("ln_b", j), ALU.mult, ALU.add)
            V.tt(YT, YT, BON, ALU.add)
            t = V.tt(OT[:, 0:4, :], YT, GG, ALU.mult)
            out_proj(["even_out0", "even_out1"], OT, [t])

        def over(l, G, flag):
            names = s_over[l]
            V2, A2, P2 = Vec("v2", names[0]), Sca("a2", names[1]), Ten("pe2", names[2])
            S2 = Eng("sp2", None)
            toks = [V.last, A.last, PE.last]
            for e in (V2, A2, P2, S2):
                e.wait(*toks)
            W3 = AR[:, 0:3 * SLOT]
            sg = AR[:, 3 * SLOT:3 * SLOT + 1024].rearrange("p (a b) -> p a b", a=4)
            hi = AR[:, 3 * SLOT + 1024:3 * SLOT + 2048].rearrange("p (a b) -> p a b", a=4)
            wg = W3[:, 0:SLOT].rearrange("p (k n) -> p k n", k=8)
            wu = W3[:, SLOT:2 * SLOT].rearrange("p (k n) -> p k n", k=8)
            wd = W3[:, 2 * SLOT:3 * SLOT].rearrange("p (k n) -> p k n", k=4)
            first = [i for i, c in enumerate(chunks) if c[0] == f"moe{l}_g0_0"][0]
            tp = tv = None
            for e in range(NE):
                q, j = e // 4, e % 4
                S2.wait(tp)
                for part, dst in ((0, wg), (4, wu), (8, wd)):
                    for c in range(4):
                        o = offs[first + 12 * q + part + c]
                        src = Wd[o:o + 128 * SLOT].rearrange("(p k n) -> p k n", p=128, k=8 if part < 8 else 4)
                        if part < 8:
                            S2.dma(dst[:, 2 * c:2 * c + 2, :], src[:, j::4, :], names[3])
                        else:
                            S2.dma(dst[:, c, :], src[:, j, :], names[3])
                td = (names[3], 16 * 12 * (e + 1))
                for i in range(4):
                    for k in range(8):
                        P2.mm(ps[:, i, 0:256], wg[:, k, i * 128:(i + 1) * 128], HT[:, k, :], k == 0, k == 7, [td, tv])
                    for k in range(8):
                        t = P2.mm(ps[:, 4 + i, 0:256], wu[:, k, i * 128:(i + 1) * 128], HT[:, k, :], k == 0, k == 7,
                                  inc=(k == 7))
                a = A2.act(sg, ps[:, 0:4, 0:256], ACT.Silu, [t, tv])
                v = V2.tt(hi, ps[:, 4:8, 0:256], sg, ALU.mult, [t, a])
                for n in range(2):
                    for t in range(2):
                        b = 2 * n + t
                        for k in range(4):
                            tp = P2.mm(ps[:, b, :], hi[:, k, t * 128:(t + 1) * 128], wd[:, k, n * 512:(n + 1) * 512],
                                       k == 0, k == 3, [v, a], inc=(k == 3))
                for n in range(2):
                    for t in range(2):
                        xs = X[:, t, n * 512:(n + 1) * 512]
                        tv = V2.stt(xs, ps[:, 2 * n + t, :], G[:, t, e:e + 1], xs, ALU.mult, ALU.add, [tp])
            for e in (V2, A2, P2, S2):
                e.wait(V2.last, A2.last, P2.last)
            for e, s2 in ((V, V2), (A, A2), (PE, P2), (SP, S2)):
                e.branch(flag, 0, s2)

        def moe(stg, l):
            phase()
            nxt = stages[stages.index(stg) + 1:][:1]
            if nxt and nxt[0] + "_c" in coffs:
                consts(nxt[0] + "_c")
            XN = norm_T(f"g_{stg}")
            hd = [V.last, A.last]
            L = buf(2, 36)
            EX, MG, CM = buf(2, 4), buf(2, 4), buf(2, 4)
            PR = buf(2, 4, 8)
            EL, M1, M2, C8, W8 = (buf(2, 8) for _ in range(5))
            s1 = [buf(2, 1) for _ in range(8)]
            Gf, Sf, POS, GO = (buf(2, 32) for _ in range(4))
            G, SE = (v.rearrange("p t (g j) -> p t g j", g=4) for v in (Gf, Sf))
            c = take(stg + "_r")
            for t in range(2):
                b, p, tk = proj_tok(c, HT, 8, t, 0, 36, hd)
                rel(b, V.tt(L[:, t, :], p[:, 0:36], par(f"rb{l}", 0, 36), ALU.add, [tk]))
            c.free(tk)

            def first(mask, cum, n):
                for t in range(2):
                    V.scan(cum[:, t, :], mask[:, t, :], mask[:, t, :], 0.0, ALU.max, ALU.max)
                V.cp(mask[:, :, 0:1], cum[:, :, 0:1])
                V.tt(mask[:, :, 1:n], cum[:, :, 1:n], cum[:, :, 0:n - 1], ALU.subtract)

            def spread(dst, w):
                for t in range(2):
                    V.tt(dst[:, t], MG[:, t, :].unsqueeze(2).broadcast_to([128, 4, 8]),
                         w[:, t, :].unsqueeze(1).broadcast_to([128, 4, 8]), ALU.mult)

            gm, gw, e1, e2, p2, den, g1, g2 = s1
            V.red(gm, L[:, :, 0:4], ALU.max)
            V.tt(EX, L[:, :, 0:4], bc(gm, [128, 2, 4]), ALU.subtract)
            V.ts(MG, EX, 0.0, None, ALU.is_ge)
            t = A.act(EX, EX, ACT.Exp, [V.last])
            first(MG, CM, 4)
            V.tt(PR, L[:, :, 4:36].rearrange("p t (g j) -> p t g j", g=4),
                 MG.unsqueeze(3).broadcast_to([128, 2, 4, 8]), ALU.mult)
            V.red(EL, PR.rearrange("p t g j -> p t j g"), ALU.add)
            V.red(e1, EL, ALU.max)
            V.tt(EL, EL, bc(e1, [128, 2, 8]), ALU.subtract)
            V.ts(M1, EL, 0.0, None, ALU.is_ge)
            first(M1, C8, 8)
            V.stt(EL, M1, -1e30, EL, ALU.mult, ALU.add)
            V.red(e2, EL, ALU.max)
            t = A.act(p2, e2, ACT.Exp, [V.last])
            V.tt(M2, EL, bc(e2, [128, 2, 8]), ALU.is_ge)
            first(M2, C8, 8)
            V.tt(W8, M1, M2, ALU.add)
            spread(SE, W8)
            tse = V.last
            tri = par("tri", 0, 128)
            b, p = bank()
            PE.mm(p[:, 0:32], tri, Sf[:, 0, :], True, True, [tse])
            PE.mm(p[:, 32:64], ones, Sf[:, 0, :], True, False)
            PE.mm(p[:, 32:64], tri, Sf[:, 1, :], False, True)
            PE.mm(p[:, 64:96], ones, Sf[:, 0, :], True, False)
            tk = PE.mm(p[:, 64:96], ones, Sf[:, 1, :], False, True, inc=True)
            V.red(gw, EX, ALU.add, [t])
            V.rcp(gw, gw)
            V.ts(den, p2, 1.0, None, ALU.add)
            V.rcp(den, den)
            V.tt(g1, gw, den, ALU.mult)
            V.tt(g2, g1, p2, ALU.mult)
            V.tt(M1, M1, bc(g1, [128, 2, 8]), ALU.mult)
            V.tt(M2, M2, bc(g2, [128, 2, 8]), ALU.mult)
            V.tt(W8, M1, M2, ALU.add)
            spread(G, W8)
            V.tt(POS, p[:, 0:64].rearrange("p (t e) -> p t e", t=2), Sf, ALU.mult, [tk])
            V.red(e1[:, 0, :], p[:, 64:96], ALU.max)
            rel(b, V.last)
            V.ts(e1[:, 0, :], e1[:, 0, :], float(CAP), 0.0, ALU.subtract, ALU.max)
            V.cp(FLAG[:, l:l + 1], e1[:, 0, :])
            V.ts(GO, POS, CAP + 0.5, None, ALU.is_ge)
            V.tt(GO, GO, Gf, ALU.mult)
            V.ts(POS, POS, 1.0, None, ALU.subtract)
            S = buf(2, NE * CAP)
            for t in range(2):
                ts_ = V.tt(S[:, t, :].rearrange("p (e c) -> p e c", c=CAP),
                           POS[:, t, :].unsqueeze(2).broadcast_to([128, NE, CAP]),
                           par("iota", 0, CAP).unsqueeze(1).broadcast_to([128, NE, CAP]), ALU.is_equal)
            XG = buf(8, NE * CAP)
            for n in range(2):
                for k in range(8):
                    b, p = bank()
                    for t in range(2):
                        tk = PE.mm(p, XN[:, t, k * 128:(k + 1) * 128], S[:, t, n * 512:(n + 1) * 512], t == 0, t == 1,
                                   [ts_], inc=(t == 1))
                    dst = XG[:, k, n * 512:(n + 1) * 512]
                    if k % 2:
                        rel(b, A.act(dst, p, ACT.Copy, [tk], scale=par(f"g_{stg}", k)))
                    else:
                        rel(b, V.ts(dst, p, par(f"g_{stg}", k), None, ALU.mult, w=[tk]))
            tx = [V.last, A.last]
            for t in range(2):
                v = S[:, t, :].rearrange("p (e c) -> p e c", c=CAP)
                ts_ = V.tt(v, v, Gf[:, t, :].unsqueeze(2).broadcast_to([128, NE, CAP]), ALU.mult, [PE.last])
            SG = [buf(512) for _ in range(2)]
            HI = [buf(512) for _ in range(2)]
            HTr = [buf(4, 128) for _ in range(2)]
            SC = [buf(2, 128) for _ in range(2)]
            YS = [buf(2, 512) for _ in range(2)]
            done = [None, None]
            for q in range(NE // 4):
                u = q % 2
                sg, hi, htr, sc, ys = SG[u], HI[u], HTr[u], SC[u], YS[u]
                res = []
                for part in "gu":
                    b, p = bank()
                    for c in range(4):
                        ck = take(f"{stg}_{part}{q}_{c}")
                        for kk in range(2):
                            for j in range(4):
                                k = 2 * c + kk
                                tk = PE.op(lambda e, p=p, j=j, k=k, q=q, w=ck.ap[:, kk * 4 + j, :]: e.matmul(
                                    p[32 * j:32 * j + 32, :], XG[:, k, (4 * q + j) * CAP:(4 * q + j + 1) * CAP], w,
                                    start=(k == 0), stop=(k == 7)),
                                    [ck.tok, *tx], chain=False, inc=(kk == 1 and j == 3))
                        ck.free(tk)
                    res.append((b, p, tk))
                b, p, tk = res[0]
                a = A.act(sg, p, ACT.Silu, [tk, done[u]])
                rel(b, a)
                b, p, tk = res[1]
                v = V.tt(hi, p, sg, ALU.mult, [tk, a])
                rel(b, v)
                b, p = bank()
                for t in range(2):
                    tk = PE.tr(p[:, t * 128:(t + 1) * 128], S[:, t, q * 128:(q + 1) * 128], ident, [ts_], inc=(t == 1))
                a2 = A.cp(sc, p[:, 0:256].rearrange("p (a b) -> p a b", a=2), [tk, done[u]])
                rel(b, a2)
                b, p = bank()
                for k in range(4):
                    tk = PE.tr(p[:, k * 128:(k + 1) * 128], hi[:, k * 128:(k + 1) * 128], ident, [v], inc=(k == 3))
                v = V.cp(htr, p.rearrange("p (a b) -> p a b", a=4), [tk, done[u]])
                rel(b, v)
                b0, p0 = bank()
                b1, p1 = bank()
                for k in range(4):
                    ck = take(f"{stg}_d{q}_{k}")
                    for n, p in ((0, p0), (1, p1)):
                        for j in range(4):
                            tk = PE.op(lambda e, p=p, j=j, k=k, n=n, w=ck.ap[:, j, n * 512:(n + 1) * 512], h=htr: e.matmul(
                                p[32 * j:32 * j + 32, :], h[:, k, j * CAP:(j + 1) * CAP], w,
                                start=(k == 0), stop=(k == 3)),
                                [ck.tok, v], chain=False, inc=(n == 1 and j == 3))
                    ck.free(tk)
                a = A.cp(ys[:, 0, :], p0, [tk, done[u]])
                v = V.cp(ys[:, 1, :], p1, [tk, done[u]])
                rel(b0, a)
                rel(b1, v)
                for n, w in ((0, a), (1, v)):
                    for t in range(2):
                        b, p = bank()
                        tk = PE.mm(p, sc[:, t, :], ys[:, n, :], True, True, [w, a2], inc=True)
                        xs = X[:, t, n * 512:(n + 1) * 512]
                        rel(b, V.tt(xs, p, xs, ALU.add, [tk]))
                done[u] = tk
            GOk = GS[:, l * 64:(l + 1) * 64].rearrange("p (t e) -> p t e", t=2)
            V.cp(GOk, GO)
            fence()
            over(l, GOk, FLAG[0:1, l:l + 1])

        def odd():
            phase()
            norm_T("g_odd")
            phase()
            cv, tcst = consts("odd_c")
            cosT, sinT, cmask = cv[:, 0:256], cv[:, 256:512], cv[:, 512:768]
            RT, trow = cv[:, 768:896], cv[:, 896:1152]
            OT = buf(8, 256)
            U5 = buf(4, 256)
            base = ar["at"]
            QK = buf(8, 256)
            VT = buf(2, 512)
            for i in range(2):
                c = take(f"odd_in{i}")
                for j in (0, 2):
                    b, p, tk = proj_T(c, [j * 128, j * 128 + 128], HT, 8)
                    rel(b, A.cp(QK[:, i * 4 + j:i * 4 + j + 2, :], p.rearrange("p (a b) -> p a b", a=2), [tk]))
                c.free(tk)
            c = take("odd_in2")
            for t in range(2):
                b, p, tk = proj_tok(c, HT, 8, t, 0, 512)
                rel(b, A.cp(VT[:, t, :], p, [tk]))
            c.free(tk)
            c = take("odd_in3")
            for j in (0, 2):
                b, p, tk = proj_T(c, [j * 128, j * 128 + 128], HT, 8)
                rel(b, A.cp(U5[:, j:j + 2, :], p.rearrange("p (a b) -> p a b", a=2), [tk]))
            c.free(tk)
            SQ = buf(8, 256)
            RS = buf(8, 256)
            lm = buf(8)
            lp = par("lam", 0, 256).rearrange("p (a b) -> p a b", a=4)
            V.tt(SQ[:, 0:1, 0:64], lp[:, 0:1, :], lp[:, 1:2, :], ALU.mult)
            V.tt(SQ[:, 1:2, 0:64], lp[:, 2:3, :], lp[:, 3:4, :], ALU.mult)
            V.red(lm[:, 0:2], SQ[:, 0:2, 0:64], ALU.add)
            t = A.act(lm[:, 2:4], lm[:, 0:2], ACT.Exp, [V.last])
            V.tt(lm[:, 4:5], lm[:, 3:4], lm[:, 2:3], ALU.subtract, [t])
            lam_init = 0.8 - 0.6 * math.exp(-0.3)
            V.ts(lm[:, 4:5], lm[:, 4:5], lam_init, None, ALU.subtract)
            nlam = lm[:, 4:5]
            t = V.tt(SQ, QK, QK, ALU.mult)
            for j in range(0, 8, 2):
                b, p = bank()
                for i in range(2):
                    tk = PE.mm(p[:, i * 256:(i + 1) * 256], ones64, SQ[:, j + i, :], True, True, [t], inc=(i == 1))
                rel(b, A.act(RS[:, j:j + 2, :], p.rearrange("p (a b) -> p a b", a=2), ACT.Ln, [tk],
                             bias=par("eps6"), scale=1.0 / 64))
            t = A.act(RS, RS, ACT.Exp, scale=-0.5)
            V.stt(QK[:, 0:4, :], QK[:, 0:4, :], par("qn"), RS[:, 0:4, :], ALU.mult, ALU.mult, [t])
            t = V.stt(QK[:, 4:8, :], QK[:, 4:8, :], par("kn"), RS[:, 4:8, :], ALU.mult, ALU.mult)
            V.wait(tcst)
            for j in range(0, 8, 2):
                b, p = bank()
                for i in range(2):
                    tk = PE.mm(p[:, i * 256:(i + 1) * 256], RT, QK[:, j + i, :], True, True, [t, tcst], inc=(i == 1))
                rel(b, V.tt(SQ[:, j:j + 2, :], p.rearrange("p (a b) -> p a b", a=2),
                            sinT.unsqueeze(1).broadcast_to([128, 2, 256]), ALU.mult, [tk]))
            V.tt(QK, QK, cosT.unsqueeze(1).broadcast_to([128, 8, 256]), ALU.mult, [PE.last])
            tq = V.tt(QK, QK, SQ, ALU.add)
            PR = [buf(2, 256) for _ in range(2)]
            AT = [buf(2, 256) for _ in range(2)]
            mx, sm = buf(32), buf(32)
            av = [None, None]
            YO = RS[:, 0:4, :]
            for h in range(4):
                for q in range(2):
                    nk = (q + 1) * 128
                    pr = PR[q]
                    for m in range(2):
                        ix = h * 4 + q * 2 + m
                        b, p = bank()
                        tk = PE.mm(p[:, 0:nk], QK[m * 64:(m + 1) * 64, h, q * 128:(q + 1) * 128],
                                   QK[m * 64:(m + 1) * 64, 4 + h, 0:nk], True, True, [tq], inc=True)
                        rel(b, V.stt(pr[:, m, 0:nk], p[:, 0:nk], 0.125, cmask[:, 256 - nk:256], ALU.mult, ALU.add,
                                     [tk, PE.last]))
                        V.red(mx[:, ix:ix + 1], pr[:, m, 0:nk], ALU.max)
                        V.ts(mx[:, ix:ix + 1], mx[:, ix:ix + 1], -1.0, None, ALU.mult)
                        ta = A.act(pr[:, m, 0:nk], pr[:, m, 0:nk], ACT.Exp, [V.last], bias=mx[:, ix:ix + 1])
                        V.red(sm[:, ix:ix + 1], pr[:, m, 0:nk], ALU.add, [ta])
                        V.rcp(sm[:, ix:ix + 1], sm[:, ix:ix + 1])
                    V.tt(sm[:, ix:ix + 1], sm[:, ix:ix + 1], nlam, ALU.mult)
                    V.ts(pr[:, 0, 0:nk], pr[:, 0, 0:nk], sm[:, ix - 1:ix], None, ALU.mult)
                    t = V.stt(pr[:, 0, 0:nk], pr[:, 1, 0:nk], sm[:, ix:ix + 1], pr[:, 0, 0:nk], ALU.mult, ALU.add)
                    b, p = bank()
                    for kb in range(q + 1):
                        tk = PE.tr(p[:, kb * 128:(kb + 1) * 128], pr[:, 0, kb * 128:(kb + 1) * 128], ident, [t],
                                   inc=(kb == q))
                    at = AT[h % 2]
                    e = A.cp(at[:, 0:q + 1, q * 128:(q + 1) * 128], p[:, 0:nk].rearrange("p (a b) -> p a b", a=q + 1),
                             [tk, av[h % 2]])
                    rel(b, e)
                b, p = bank()
                PE.mm(p[:, 0:256], VT[:, 0, h * 128:(h + 1) * 128], at[:, 0, :], True, False, [e])
                tk = PE.mm(p[:, 128:256], VT[:, 1, h * 128:(h + 1) * 128], at[:, 1, 128:256], False, True, inc=True)
                av[h % 2] = tk
                rel(b, A.cp(YO[:, h, :], p[:, 0:256], [tk, V.last]))
            t = V.tt(SQ[:, 0:4, :], YO, YO, ALU.mult, [A.last, PE.last])
            R2 = SQ[:, 4:8, :]
            for j in range(0, 4, 2):
                b, p = bank()
                for i in range(2):
                    tk = PE.mm(p[:, i * 256:(i + 1) * 256], ones, SQ[:, j + i, :], True, True, [t], inc=(i == 1))
                rel(b, A.act(R2[:, j:j + 2, :], p.rearrange("p (a b) -> p a b", a=2), ACT.Ln, [tk],
                             bias=par("eps5"), scale=1.0 / 128))
            t = A.act(R2, R2, ACT.Exp, scale=-0.5)
            V.stt(OT[:, 0:4, :], YO, 1.0 - lam_init, R2, ALU.mult, ALU.mult, [t])
            V.ts(OT[:, 0:4, :], OT[:, 0:4, :], par("subln"), None, ALU.mult)
            fence()

            ar["at"] = base
            cB, cC = take("s5_B"), take("s5_C")
            sB = cB.ap[:, 0, :].rearrange("p (r i n) -> p r i n", r=2, i=16)
            sC = cC.ap[:, 0, :].rearrange("p (r i n) -> p r i n", r=2, i=16)
            s16 = [buf(16) for _ in range(14)]
            lr, st_, rho, th, ph, kf, sn, cs, nr, ni, de, cr, ci, tp = s16
            V.ts(lr, par("s5_re", 0, 16), -1e-4, None, ALU.min)
            li = par("s5_im", 0, 16)
            t = A.act(st_, par("s5_ls", 0, 16), ACT.Exp)
            V.tt(rho, lr, st_, ALU.mult, [t])
            t = A.act(rho, rho, ACT.Exp, [V.last])
            V.tt(th, li, st_, ALU.mult)
            MAGIC = 12582912.0
            C1, C2, C3 = 6.28125, 0.0019350051879882812, 3.0199159819568e-07

            def reduce2pi(dst, src, k):
                V.ts(k, src, 1.0 / (2 * math.pi), MAGIC, ALU.mult, ALU.add)
                V.ts(k, k, MAGIC, None, ALU.subtract)
                V.stt(dst, k, -C1, src, ALU.mult, ALU.add)
                V.stt(dst, k, -C2, dst, ALU.mult, ALU.add)
                V.stt(dst, k, -C3, dst, ALU.mult, ALU.add)
                return V.ts(dst, dst, 3.1415925, -3.1415925, ALU.min, ALU.max)

            def sincos(sn, cs, r, tmp, w):
                t1 = V.stt(tmp, r, -1.0, r, ALU.mult, ALU.max, w)
                A.act(sn, r, ACT.Sin, [t1])
                return A.act(cs, tmp, ACT.Sin, bias=par("hpi"), scale=-1.0)

            t = reduce2pi(ph, th, kf)
            t = sincos(sn, cs, ph, tp, [t])
            V.tt(nr, rho, cs, ALU.mult, [t])
            V.ts(nr, nr, 1.0, None, ALU.subtract)
            V.tt(ni, rho, sn, ALU.mult)
            V.tt(de, lr, lr, ALU.mult)
            V.tt(tp, li, li, ALU.mult)
            V.tt(de, de, tp, ALU.add)
            V.rcp(de, de)
            V.tt(cr, nr, lr, ALU.mult)
            V.tt(tp, ni, li, ALU.mult)
            V.tt(cr, cr, tp, ALU.add)
            V.tt(cr, cr, de, ALU.mult)
            V.tt(ci, ni, lr, ALU.mult)
            V.tt(tp, nr, li, ALU.mult)
            V.tt(ci, ci, tp, ALU.subtract)
            V.tt(ci, ci, de, ALU.mult)
            Y5 = buf(4, 256)
            AG, KF = buf(4, 256), buf(4, 256)
            SN, CS_, BR, BI, ZR, ZI, TA, TB = (buf(4, 256) for _ in range(8))
            for q in range(4):
                for i in range(4):
                    V.ts(AG[:, i, :], trow, ph[:, q * 4 + i:q * 4 + i + 1], None, ALU.mult, w=[A.last, PE.last])
                t = reduce2pi(AG, AG, KF)
                tsc = sincos(SN, CS_, AG, TA, [t])
                tb = None
                for part, dst in ((0, BR), (1, BI)):
                    for j in (0, 2):
                        b, p = bank()
                        for i in range(2):
                            tk = PE.mm(p[:, i * 256:(i + 1) * 256], sB[:, part, q * 4 + j + i, :], U5[:, q, :],
                                       True, True, [cB.tok], inc=(i == 1))
                        tb = A.cp(dst[:, j:j + 2, :], p.rearrange("p (a b) -> p a b", a=2), [tk])
                        rel(b, tb)
                for i in range(4):
                    n = q * 4 + i
                    V.ts(TA[:, i, :], BI[:, i, :], ci[:, n:n + 1], None, ALU.mult, w=[tb])
                    V.ts(TB[:, i, :], BI[:, i, :], cr[:, n:n + 1], None, ALU.mult)
                    V.stt(TB[:, i, :], BR[:, i, :], ci[:, n:n + 1], TB[:, i, :], ALU.mult, ALU.add)
                    V.stt(TA[:, i, :], BR[:, i, :], cr[:, n:n + 1], TA[:, i, :], ALU.mult, ALU.subtract)
                V.tt(BR, TA, CS_, ALU.mult)
                V.tt(BI, TB, SN, ALU.mult)
                V.tt(BR, BR, BI, ALU.add)
                V.tt(BI, TB, CS_, ALU.mult)
                V.tt(TA, TA, SN, ALU.mult)
                V.tt(BI, BI, TA, ALU.subtract)
                for i in range(4):
                    r = bc(rho[:, q * 4 + i:q * 4 + i + 1], [128, 256])
                    V.scan(ZR[:, i, :], r, BR[:, i, :], 0.0, ALU.mult, ALU.add)
                    V.scan(ZI[:, i, :], r, BI[:, i, :], 0.0, ALU.mult, ALU.add)
                V.tt(TA, ZR, CS_, ALU.mult)
                V.tt(TB, ZI, SN, ALU.mult)
                V.tt(BR, TA, TB, ALU.subtract)
                V.tt(TA, ZR, SN, ALU.mult)
                V.tt(TB, ZI, CS_, ALU.mult)
                V.stt(BI, TA, -1.0, TB, ALU.mult, ALU.subtract)
                b, p = bank()
                for i in range(4):
                    PE.mm(p[:, 0:256], sC[:, 0, q * 4 + i, :], BR[:, i, :], i == 0, False, [V.last, cC.tok])
                    tk = PE.mm(p[:, 0:256], sC[:, 1, q * 4 + i, :], BI[:, i, :], False, i == 3, inc=(i == 3))
                rel(b, V.stt(Y5[:, q, :], U5[:, q, :], par("s5_d", q), p[:, 0:256], ALU.mult, ALU.add, [tk]))
            cB.free(PE.last)
            cC.free(PE.last)
            glu = take("glu")
            c0 = math.sqrt(2.0 / math.pi)
            V.tt(TA, Y5, Y5, ALU.mult, [A.last])
            V.ts(TA, TA, 0.044715 * c0, c0, ALU.mult, ALU.add)
            V.tt(TA, TA, Y5, ALU.mult)
            t = A.act(TA, TA, ACT.Tanh, [V.last])
            V.ts(TA, TA, 0.5, 0.5, ALU.mult, ALU.add, w=[t])
            t = V.tt(Y5, Y5, TA, ALU.mult)
            for j in (0, 2):
                b, p, tk = proj_T(glu, [j * 128, j * 128 + 128], Y5, 4, [t])
                a = A.act(TB[:, j:j + 2, :], p.rearrange("p (a b) -> p a b", a=2), ACT.Sigmoid, [tk])
                rel(b, a)
            glu.free(tk)
            t = V.tt(OT[:, 4:8, :], Y5, TB, ALU.mult, [a])
            out_proj(["odd_out0", "odd_out1"], OT, [t])
            return

        def hyb(stg):
            phase()
            norm_T(f"g_{stg}")
            phase()
            cv, tcst = consts(stg + "_c")
            cosT, sinT, tri = cv[:, 0:256], cv[:, 256:512], cv[:, 512:768]
            dec = cv[:, 768:1792].rearrange("p (h n) -> p h n", h=4)
            o = 1792
            cw, cb_ = cv[:, o:o + 96], cv[:, o + 96:o + 120]
            dsk, nw = cv[:, o + 120:o + 136], cv[:, o + 136:o + 152]
            dtb, alog = cv[:, o + 152:o + 184], cv[:, o + 184:o + 216]
            YR, MG = buf(16, 256), buf(8, 256)
            base = ar["at"]
            for e in (V, A, PE):
                e.wait(tcst)
            QR, KR, T1, T2 = (buf(2, 256) for _ in range(4))
            VT, SG, Y, SQ = buf(2, 512), buf(4, 256), buf(4, 256), buf(4, 256)
            PTs = buf(384)
            RS = buf(256)

            def p2(p):
                return p.rearrange("p (a b) -> p a b", a=2)

            def gnorm(dst, col):
                t = V.tt(SQ, Y, Y, ALU.mult, [A.last, PE.last])
                b, p = bank()
                for i in range(4):
                    tk = PE.mm(p[:, 0:256], ones, SQ[:, i, :], i == 0, i == 3, [t], inc=(i == 3))
                a = A.act(RS, p[:, 0:256], ACT.Ln, [tk, V.last], bias=par("eps6"), scale=1.0 / 512)
                rel(b, a)
                return A.act(RS, RS, ACT.Exp, scale=-0.5)

            for h in range(4):
                cq, cvv, cg = take(f"{stg}_qk{h}"), take(f"{stg}_v{h}"), take(f"{stg}_g{h}")
                for which, dst, sc in ((0, QR, 1.0), (1, KR, 1.0 / 16)):
                    b, p, tk = proj_T(cq, [which * 256, which * 256 + 128], HT, 8)
                    V.stt(T1, p2(p), sc, cosT.unsqueeze(1).broadcast_to([128, 2, 256]), ALU.mult, ALU.mult, [tk])
                    rel(b, V.stt(T2, p2(p), sc, sinT.unsqueeze(1).broadcast_to([128, 2, 256]), ALU.mult, ALU.mult))
                    V.tt(dst[:, 0, :], T1[:, 0, :], T2[:, 1, :], ALU.subtract)
                    tr = V.tt(dst[:, 1, :], T2[:, 0, :], T1[:, 1, :], ALU.add)
                cq.free(tk)
                for t in range(2):
                    b, p, tk = proj_tok(cvv, HT, 8, t, 0, 512)
                    tv = A.cp(VT[:, t, :], p, [tk])
                    rel(b, tv)
                cvv.free(tk)
                for j in (0, 2):
                    b, p, tk = proj_T(cg, [j * 128, j * 128 + 128], HT, 8)
                    ts_ = A.act(SG[:, j:j + 2, :], p2(p), ACT.Silu, [tk, V.last])
                    rel(b, ts_)
                cg.free(tk)
                b, p = bank()
                for i in range(2):
                    PE.mm(p[:, 0:256], KR[:, i, 0:128], QR[:, i, :], i == 0, i == 1, [tr])
                for i in range(2):
                    tk = PE.mm(p[:, 256:384], KR[:, i, 128:256], QR[:, i, 128:256], i == 0, i == 1, inc=(i == 1))
                V.tt(PTs[:, 0:256], p[:, 0:256], dec[:, h, :], ALU.mult, [tk])
                tp = V.tt(PTs[:, 256:384], p[:, 256:384], dec[:, h, 0:128], ALU.mult)
                rel(b, tp)
                for j in (0, 2):
                    b, p = bank()
                    for i in range(2):
                        d = slice((j + i) * 128, (j + i + 1) * 128)
                        PE.mm(p[:, i * 256:(i + 1) * 256], VT[:, 0, d], PTs[:, 0:256], True, False, [tp, tv])
                        tk = PE.mm(p[:, i * 256 + 128:(i + 1) * 256], VT[:, 1, d], PTs[:, 256:384], False, True,
                                   inc=(i == 1))
                    rel(b, A.cp(Y[:, j:j + 2, :], p2(p), [tk, V.last]))
                tr = gnorm(None, None)
                V.tt(Y, Y, SG, ALU.mult, [ts_])
                V.tt(YR[:, 4 * h:4 * h + 4, :], Y, RS.unsqueeze(1).broadcast_to([128, 4, 256]), ALU.mult, [tr])
            fence()

            def merge(gn, on, first):
                for i in range(2):
                    c = take(f"{stg}_{gn}{i}")
                    for j in (0, 2):
                        b, p, tk = proj_T(c, [j * 128, j * 128 + 128], HT, 8)
                        ta = A.act(SGM[:, i * 4 + j:i * 4 + j + 2, :], p2(p), ACT.Sigmoid, [tk])
                        rel(b, ta)
                    c.free(tk)
                for i in range(4):
                    c = take(f"{stg}_{on}{i}")
                    b, p, tk = proj_T(c, [0, 128], YR, 16, [V.last])
                    c.free(tk)
                    sl = slice(2 * i, 2 * i + 2)
                    if first:
                        rel(b, V.tt(MG[:, sl, :], p2(p), SGM[:, sl, :], ALU.mult, [tk, ta]))
                    else:
                        rel(b, V.tt(SGM[:, sl, :], p2(p), SGM[:, sl, :], ALU.mult, [tk, ta]))
                        V.tt(MG[:, sl, :], MG[:, sl, :], SGM[:, sl, :], ALU.add)

            ar["at"] = base
            SGM = buf(8, 256)
            merge("gr", "ro", True)
            fence()
            ar["at"] = base
            UB = buf(6, 259)
            CV = buf(6, 256)
            XD = buf(2, 512)
            ZS, Y, SQ = buf(4, 256), buf(4, 256), buf(4, 256)
            CB = buf(384)
            SE = [buf(2, 384) for _ in range(2)]
            RS = buf(256)
            DTP, LA, NA_ = buf(2, 32), buf(2, 32), buf(2, 32)
            E1, E2, AE = buf(2, 32), buf(2, 32), buf(32)
            c = take(f"{stg}_dt")
            for t in range(2):
                b, p, tk = proj_tok(c, HT, 8, t, 0, 32)
                rel(b, V.tt(DTP[:, t, :], p[:, 0:32], dtb, ALU.add, [tk]))
            c.free(tk)
            V.stt(E1, DTP, -1.0, DTP, ALU.mult, ALU.max)
            A.act(E1, E1, ACT.Exp, [V.last], scale=-1.0)
            A.act(AE, alog, ACT.Exp)
            t = A.act(E1, E1, ACT.Ln, bias=par("one"))
            V.ts(E2, DTP, 0.0, None, ALU.max)
            V.tt(DTP, E1, E2, ALU.add, [t])
            t = V.stt(LA, DTP, -1.0, AE.unsqueeze(1).broadcast_to([128, 2, 32]), ALU.mult, ALU.mult)
            b, p = bank()
            PE.mm(p[:, 0:32], tri[:, 0:128], LA[:, 0, :], True, True, [t])
            PE.mm(p[:, 32:64], tri[:, 128:256], LA[:, 0, :], True, False)
            tk = PE.mm(p[:, 32:64], tri[:, 0:128], LA[:, 1, :], False, True, inc=True)
            rel(b, V.ts(NA_, p[:, 0:64].rearrange("p (a b) -> p a b", a=2), -1.0, None, ALU.mult, w=[tk]))
            V.set(UB[:, :, 0:3], 0.0)
            seu = [None, None]
            for g in range(4):
                cx, cbc, cz = take(f"{stg}_xs{g}"), take(f"{stg}_bc{g}"), take(f"{stg}_z{g}")
                tiles = [4 * g, 4 * g + 1, 4 * g + 2, 4 * g + 3, 16 + g, 20 + g]
                for n, (c, c0) in enumerate(((cx, 0), (cx, 256), (cbc, 0))):
                    b, p, tk = proj_T(c, [c0, c0 + 128], HT, 8)
                    rel(b, A.cp(UB[:, 2 * n:2 * n + 2, 3:259], p2(p), [tk, V.last]))
                    if n:
                        c.free(tk)
                for j in (0, 2):
                    b, p, tk = proj_T(cz, [j * 128, j * 128 + 128], HT, 8)
                    tz = A.act(ZS[:, j:j + 2, :], p2(p), ACT.Silu, [tk])
                    rel(b, tz)
                cz.free(tk)
                for n, f in enumerate(tiles):
                    V.ts(CV[:, n, :], UB[:, n, 0:256], cw[:, 4 * f:4 * f + 1], cb_[:, f:f + 1], ALU.mult, ALU.add,
                         w=[A.last, PE.last])
                    for i in range(1, 4):
                        V.stt(CV[:, n, :], UB[:, n, i:i + 256], cw[:, 4 * f + i:4 * f + i + 1], CV[:, n, :],
                              ALU.mult, ALU.add)
                tcv = A.act(CV, CV, ACT.Silu, [V.last])
                for t in range(2):
                    b, p = bank()
                    for i in range(4):
                        tk = PE.tr(p[:, i * 128:(i + 1) * 128], CV[:, i, t * 128:(t + 1) * 128], ident, [tcv],
                                   inc=(i == 3))
                    txd = V.tt(XD[:, t, :].rearrange("p (h n) -> p h n", h=8), p.rearrange("p (h n) -> p h n", h=8),
                               DTP[:, t, 8 * g:8 * g + 8].unsqueeze(2).broadcast_to([128, 8, 64]), ALU.mult, [tk])
                    rel(b, txd)
                b, p = bank()
                PE.mm(p[:, 0:256], CV[:, 4, 0:128], CV[:, 5, :], True, True)
                tk = PE.mm(p[:, 256:384], CV[:, 4, 128:256], CV[:, 5, 128:256], True, True, inc=True)
                V.tt(CB[:, 0:256], p[:, 0:256], tri, ALU.mult, [tk])
                rel(b, V.tt(CB[:, 256:384], p[:, 256:384], tri[:, 0:128], ALU.mult))
                for hp in range(4):
                    se = SE[hp % 2]
                    b, p = bank()
                    for i in range(2):
                        hh = 8 * g + 2 * hp + i
                        PE.mm(p[:, i * 256:(i + 1) * 256], LA[:, 0, hh:hh + 1].broadcast_to([128, 128]), tri, True, False)
                        tk = PE.mm(p[:, i * 256 + 128:(i + 1) * 256], LA[:, 1, hh:hh + 1].broadcast_to([128, 128]),
                                   tri[:, 0:128], False, True, inc=(i == 1))
                    for i in range(2):
                        hh = 8 * g + 2 * hp + i
                        V.ts(se[:, i, 0:256], p[:, i * 256:(i + 1) * 256], NA_[:, 0, hh:hh + 1], 0.0, ALU.add, ALU.min,
                             w=[tk, seu[hp % 2]])
                        e = V.ts(se[:, i, 256:384], p[:, i * 256 + 128:(i + 1) * 256], NA_[:, 1, hh:hh + 1], 0.0,
                                 ALU.add, ALU.min)
                    rel(b, e)
                    t = A.act(se, se, ACT.Exp, [e])
                    t = V.tt(se, se, CB.unsqueeze(1).broadcast_to([128, 2, 384]), ALU.mult, [t])
                    b, p = bank()
                    for i in range(2):
                        xc = slice((2 * hp + i) * 64, (2 * hp + i + 1) * 64)
                        o2 = p[i * 64:(i + 1) * 64, :]
                        PE.mm(o2[:, 0:256], XD[:, 0, xc], se[:, i, 0:256], True, False, [t])
                        tk = PE.mm(o2[:, 128:256], XD[:, 1, xc], se[:, i, 256:384], False, True, inc=(i == 1))
                    seu[hp % 2] = tk
                    rel(b, V.stt(Y[:, hp, :], CV[:, hp, :], dsk[:, 4 * g + hp:4 * g + hp + 1], p[:, 0:256],
                                 ALU.mult, ALU.add, [tk]))
                V.tt(Y, Y, ZS, ALU.mult, [tz])
                tr = gnorm(None, None)
                V.tt(Y, Y, RS.unsqueeze(1).broadcast_to([128, 4, 256]), ALU.mult, [tr])
                for i in range(4):
                    V.ts(YR[:, 4 * g + i, :], Y[:, i, :], nw[:, 4 * g + i:4 * g + i + 1], None, ALU.mult)
            fence()
            ar["at"] = base
            SGM = buf(8, 256)
            merge("gs", "so", False)
            out_proj([f"{stg}_wo0", f"{stg}_wo1"], MG, [V.last])

        def ffn(stg):
            phase()
            nxt = stages[stages.index(stg) + 1:][:1]
            if nxt and nxt[0] + "_c" in coffs:
                consts(nxt[0] + "_c")
            norm_T(f"g_{stg}")
            hd = [V.last, A.last]
            H = buf(22, 256)
            SG = [buf(2, 256) for _ in range(2)]
            ht = []
            for i in range(11):
                c = take(f"{stg}_gu{i}")
                b, p, tk = proj_T(c, [0, 128], HT, 8, hd)
                b2, pu, tk2 = proj_T(c, [256, 384], HT, 8)
                c.free(tk2)
                sg = SG[i % 2]
                a = A.act(sg, p.rearrange("p (a b) -> p a b", a=2), ACT.Silu, [tk, ht[i - 2] if i > 1 else None])
                rel(b, a)
                v = V.tt(H[:, 2 * i:2 * i + 2, :], pu.rearrange("p (a b) -> p a b", a=2), sg, ALU.mult, [tk2, a])
                ht.append(v)
                rel(b2, v)
            acc = {(t, n): bank() for t in range(2) for n in range(2)}
            for i in range(6):
                c = take(f"{stg}_dn{i}")
                K = 4 if i < 5 else 2
                for t in range(2):
                    for n in range(2):
                        for k in range(K):
                            last = i == 5 and k == K - 1
                            tk = PE.mm(acc[t, n][1], H[:, 4 * i + k, t * 128:(t + 1) * 128],
                                       c.ap[:, k, n * 512:(n + 1) * 512], i == 0 and k == 0, last,
                                       [c.tok, ht[2 * i], ht[min(2 * i + 1, 10)]], inc=(k == K - 1))
                        if i == 5:
                            xs = X[:, t, n * 512:(n + 1) * 512]
                            rel(acc[t, n][0], V.tt(xs, acc[t, n][1], xs, ALU.add, [tk]))
                c.free(tk)

        def fin():
            phase()
            c = take("fin_w")
            sq, ss = buf(2, 1024), buf(4)
            for t in range(2):
                V.stt(sq[:, t, :], X[:, t, :], 1.0, X[:, t, :], ALU.mult, ALU.mult, accum=ss[:, t:t + 1])
            A.act(ss[:, 2:4], ss[:, 0:2], ACT.Ln, [V.last], bias=par("eps6"), scale=1.0 / 1024)
            t2 = A.act(ss[:, 0:2], ss[:, 2:4], ACT.Exp, scale=-0.5)
            for t in range(2):
                V.stt(X[:, t, :], X[:, t, :], ss[:, t:t + 1], c.ap[:, 0, :], ALU.mult, ALU.mult, [t2, c.tok])

        for s in stages:
            if s == "even":
                even()
            elif s in ("moe0", "moe1"):
                moe(s, int(s[-1]))
            elif s == "odd":
                odd_start = st["take"]
                odd()
            elif s.startswith("hyb"):
                hyb(s)
            elif s.startswith("ffn"):
                ffn(s)
            else:
                fin()
        SP.dma(out_d.rearrange("(t p) d -> p t d", p=128), X, s_out, [V.last])
        SP.wait((s_out, 16))

        block = ctx.enter_context(nc.Block())

        @block.sync
        def _(eng):
            SP.emit(eng)

        @block.scalar
        def _(eng):
            A.emit(eng)

        @block.vector
        def _(eng):
            V.emit(eng)

        @block.gpsimd
        def _(eng):
            G.emit(eng)

        @block.tensor
        def _(eng):
            PE.emit(eng)


def rows(w):
    return w.reshape(-1, 128, w.shape[1]).transpose(1, 0, 2)


def cols(v):
    return v.reshape(-1, 128).T


def brow(v):
    return np.broadcast_to(v.reshape(1, -1), (128, v.size))


def pack_chunk(name, inp):
    f = np.float32
    if name == "even_c":
        o = np.zeros((128, 1184), f)
        h, r = np.arange(128) // 64, np.arange(128) % 64
        same = h[:, None] == h[None, :]
        R, Cc = r[:, None], r[None, :]
        blk = (R // 16) == (Cc // 16)
        o[:, 0:128] = same
        o[:, 128:256] = same & (R < Cc) & blk
        o[:, 256:384] = same & (Cc < R) & blk
        o[:, 384:512] = same & (Cc < R) & ~blk
        o[:, 512:640] = same & (R < Cc)
        o[:, 640:704] = R <= np.arange(64)[None, :]
        o[:, 704:768] = R == np.arange(64)[None, :]
        for g, w in enumerate((2, 4, 8, 16)):
            o[:, 1088 + 16 * g:1104 + 16 * g] = w / np.minimum(np.arange(1, 17), w)
        o[:, 1152] = 1.0
        return o
    if name.startswith("even_in"):
        i = int(name[-1])
        return rows(inp["even_w_in"][0][:, i * 512:min((i + 1) * 512, 2304)])
    if name == "lora":
        o = np.zeros((128, 3, 512), f)
        o[0:64, 0] = inp["rw_w2"][0]
        o[64:128, 0] = inp["rw_a2"][0]
        o[:, 1] = inp["rw_g2"][0]
        o[:, 2] = inp["pool_w"][0].transpose(1, 0, 2).reshape(128, 512)
        return o
    if name.startswith("even_out"):
        i = int(name[-1])
        return rows(inp["even_w_out"][0][:, i * 512:(i + 1) * 512])
    if name.startswith("moe"):
        l = int(name[3])
        if name.endswith("_r"):
            return rows(np.concatenate([inp["moe_w_group"][l], inp["moe_w_expert"][l]], axis=1))
        q, c = (int(v) for v in name[6:].split("_"))
        w = inp[{"g": "moe_w_gate", "u": "moe_w_up", "d": "moe_w_down"}[name[5]]][l, 4 * q:4 * q + 4]
        if name[5] == "d":
            return w[:, c * 128:(c + 1) * 128].transpose(1, 0, 2)
        return w[:, c * 256:(c + 1) * 256].reshape(4, 2, 128, 512).transpose(2, 1, 0, 3)
    if name == "odd_c":
        o = np.zeros((128, 1152), f)
        inv = (10000.0 ** (-np.arange(0, 64, 2, dtype=f) / f(64))).astype(f)
        ang = np.arange(T, dtype=f)[None, :] * inv[np.arange(128) % 32][:, None]
        o[:, 0:256] = np.cos(ang)
        o[:, 256:512] = np.sin(ang)
        q = np.arange(128)
        o[:, 640:768] = np.where(q[:, None] >= q[None, :], 0.0, -1e30)
        for m in range(128):
            d = m % 64
            if d < 32:
                o[m + 32, 768 + m] = -1.0
            else:
                o[m - 32, 768 + m] = 1.0
        o[:, 896:1152] = np.arange(256)
        return o
    if name.startswith("odd_in"):
        i = int(name[-1])
        return rows(inp["odd_w_in"][0][:, i * 512:(i + 1) * 512])
    if name.startswith("odd_out"):
        i = int(name[-1])
        return rows(inp["odd_w_out"][0][:, i * 512:(i + 1) * 512])
    if name in ("s5_B", "s5_C"):
        o = np.zeros((128, 2, 16, 128), f)
        for r, part in enumerate(("re", "im")):
            m = inp[("s5_b_" if name == "s5_B" else "s5_c_") + part][0]
            for g in range(32):
                i, gg = g // 2, g % 2
                ch, s = 32 * (i % 4) + 16 * gg, 64 * gg
                if name == "s5_B":
                    o[ch:ch + 16, r, i, s:s + 64] = m[g].T
                else:
                    o[s:s + 64, r, i, ch:ch + 16] = m[g].T
        return o
    if name == "glu":
        return rows(inp["s5_w_glu"][0])
    if name.startswith("hyb"):
        l, key = int(name[3]), name[5:]
        w = inp["w_in_2"][l]
        if key == "c":
            o = np.zeros((128, 2008), f)
            inv = (10000.0 ** (-np.arange(128, dtype=f) / f(128))).astype(f)
            ang = np.arange(T, dtype=f)[None, :] * inv[:, None]
            o[:, 0:256] = np.cos(ang)
            o[:, 256:512] = np.sin(ang)
            j, i = np.arange(128)[:, None], np.arange(256)[None, :]
            o[:, 512:768] = j <= i
            for h in range(4):
                lg = math.log(1.0 - 2.0 ** (-5.0 - h))
                o[:, 768 + 256 * h:1024 + 256 * h] = np.where(j <= i, np.exp(lg * np.maximum(i - j, 0)), 0.0)
            at = 1792
            o[:, at:at + 96] = inp["conv_w_2"][l].reshape(4, 24, 128).transpose(2, 1, 0).reshape(128, 96)
            o[:, at + 96:at + 120] = cols(inp["conv_b_2"][l])
            o[:, at + 120:at + 136] = cols(np.repeat(inp["d_skip_2"][l], 64))
            o[:, at + 136:at + 152] = cols(inp["ssd_norm_w_2"][l])
            o[:, at + 152:at + 184] = brow(inp["dt_bias_2"][l])
            o[:, at + 184:at + 216] = brow(inp["a_log_2"][l])
            return o
        if key == "dt":
            return rows(w[:, 11264:11296])
        n = int(key[-1])
        k = key[:-1]
        if k == "qk":
            return rows(np.concatenate([w[:, n * 256:(n + 1) * 256], w[:, 1024 + n * 256:1024 + (n + 1) * 256]], 1))
        if k == "bc":
            return rows(np.concatenate([w[:, 10240 + n * 128:10368 + n * 128], w[:, 10752 + n * 128:10880 + n * 128]], 1))
        starts = {"v": 2048, "g": 4096, "z": 6144, "xs": 8192, "gr": 11296, "gs": 12320}
        if k in starts:
            a = starts[k] + n * 512
            return rows(w[:, a:a + 512])
        if k == "ro":
            return rows(inp["ret_out_2"][l][:, n * 256:(n + 1) * 256])
        if k == "so":
            return rows(inp["ssd_out_2"][l][:, n * 256:(n + 1) * 256])
        return rows(inp["w_o_2"][l][:, n * 512:(n + 1) * 512])
    if name.startswith("ffn"):
        l, key = int(name[3]), name[5:]
        if key.startswith("gu"):
            n = int(key[2:])
            w = inp["w_gate_up_2"][l]
            return rows(np.concatenate([w[:, n * 256:(n + 1) * 256], w[:, 2816 + n * 256:2816 + (n + 1) * 256]], 1))
        n = int(key[2:])
        return rows(inp["w_down_2"][l][n * 512:min((n + 1) * 512, 2816)])
    return brow(inp["final_norm_w_2"])


def pack_params(inp):
    o = np.zeros((128, NP), np.float32)

    def put(name, v):
        at, n = PT[name]
        o[:, at:at + n] = v

    for l in range(2):
        put(("g_even", "g_odd")[l], cols(inp["norm_mix_g"][l]))
        put(f"g_moe{l}", cols(inp["norm_ffn_g"][l]))
        put(f"g_hyb{l}", cols(inp["norm_mix_w_2"][l]))
        put(f"g_ffn{l}", cols(inp["norm_ffn_w_2"][l]))
        put(f"rb{l}", brow(np.concatenate([inp["moe_b_group"][l], inp["moe_b_expert"][l]])))
    for name, key in (("mu", "rw_mu"), ("w0", "rw_w0"), ("a0", "rw_a0"), ("k_k", "rw_k_k"), ("k_a", "rw_k_a"),
                      ("r_k", "rw_r_k"), ("ln_g", "rw_ln_g"), ("ln_b", "rw_ln_b"), ("pool_scale", "pool_scale"),
                      ("s5_d", "s5_d"), ("subln", "da_subln")):
        put(name, cols(inp[key][0].reshape(-1)))
    put("qn", cols(np.concatenate([inp["da_q_norm"][0]] * 2)))
    put("kn", cols(np.concatenate([inp["da_k_norm"][0]] * 2)))
    for name, key in (("s5_re", "s5_a_re"), ("s5_im", "s5_a_im"), ("s5_ls", "s5_log_step")):
        put(name, cols(inp[key][0].reshape(-1)))
    put("lam", brow(np.concatenate([inp[f"da_lam_{k}"][0] for k in ("q1", "k1", "q2", "k2")])))
    put("eps6", 1e-6)
    put("eps5", 1e-5)
    put("epsln", 64e-5)
    put("one", 1.0)
    put("hpi", math.pi / 2)
    put("ident", np.eye(128))
    put("ones", 1.0)
    r = np.arange(128)
    put("tri", r[:, None] <= r[None, :])
    put("iota", np.arange(32))
    r = np.arange(128) // 64
    put("ones64", r[:, None] == r[None, :])
    return o


def kernel(**inputs):
    import numpy as _np
    import concourse.bacc as _bacc
    from concourse import mybir as _mybir
    from concourse.bass_utils import run_bass_kernel_spmd as _run

    inputs = {k: _np.asarray(v) for k, v in inputs.items()}
    table = chunk_table(STAGES) + [(name, 1, n) for name, n in const_table(STAGES)]
    W = _np.empty((sum(128 * k * n for _, k, n in table),), _np.float32)
    at = 0
    for name, k, n in table:
        size = 128 * k * n
        W[at:at + size].reshape(128, k, n)[...] = pack_chunk(name, inputs).reshape(128, k, n)
        at += size
    arrays = {"w_dram": W, "p_dram": pack_params(inputs), "x_dram": _np.ascontiguousarray(inputs["x"][0])}
    nc = _bacc.Bacc("TRN2", target_bir_lowering=False, num_devices=1)
    args = [nc.dram_tensor(k, a.shape, _mybir.dt.float32, kind="ExternalInput").ap() for k, a in arrays.items()]
    out = nc.dram_tensor("out_dram", (T, 1024), _mybir.dt.float32, kind="ExternalOutput").ap()
    program(nc, args[0], args[1], args[2], out, STAGES)
    r = _run(nc, [arrays], core_ids=[0])
    return r.results[0]["out_dram"].reshape(1, T, 1024)
```

```python
import math
from contextlib import ExitStack

import numpy as np

import concourse.bass as bass
from concourse import mybir
from concourse.alu_op_type import AluOpType as ALU

F32 = mybir.dt.float32
ACT = mybir.ActivationFunctionType
AX = mybir.AxisListType
T = 256
NSLOT = 6
SLOT = 4096
NE = 32
STAGES = ["even", "moe0", "odd", "moe1", "hyb0", "ffn0", "hyb1", "ffn1", "fin"]

PCOLS = [
    ("g_even", 8), ("g_moe0", 8), ("g_odd", 8), ("g_moe1", 8), ("g_hyb0", 8), ("g_ffn0", 8),
    ("g_hyb1", 8), ("g_ffn1", 8), ("mu", 14), ("w0", 4), ("a0", 4), ("k_k", 4), ("k_a", 4),
    ("r_k", 4), ("ln_g", 4), ("ln_b", 4), ("pool_scale", 4), ("qn", 1), ("kn", 1), ("subln", 1),
    ("s5_re", 16), ("s5_im", 16), ("s5_ls", 16), ("s5_d", 4), ("lam", 256), ("rb0", 36),
    ("rb1", 36), ("eps6", 1), ("eps5", 1), ("epsln", 1), ("one", 1), ("hpi", 1), ("ident", 128), ("ones", 128),
    ("ones64", 128), ("tri", 128), ("iota", 32),
]
CAP = 32


def pcol_table():
    at, out = 0, {}
    for name, n in PCOLS:
        out[name] = (at, n)
        at += n
    return out, at


PT, NP = pcol_table()


def chunk_table(stages):
    out = []
    for st in stages:
        if st == "even":
            out += [(f"even_in{i}", 8, 512 if i < 4 else 256) for i in (3, 4)]
            out += [("lora", 3, 512)]
            out += [(f"even_in{i}", 8, 512) for i in (1, 0, 2)]
            out += [("even_out0", 8, 512), ("even_out1", 8, 512)]
        if st in ("moe0", "moe1"):
            out += [(st + "_r", 8, 36)]
            for q in range(NE // 4):
                out += [(f"{st}_g{q}_{c}", 8, 512) for c in range(4)]
                out += [(f"{st}_u{q}_{c}", 8, 512) for c in range(4)]
                out += [(f"{st}_d{q}_{c}", 4, 1024) for c in range(4)]
        if st == "odd":
            out += [("odd_in3", 8, 512), ("s5_C", 1, 1024), ("s5_B", 1, 4096)]
            out += [(f"odd_in{i}", 8, 512) for i in range(3)]
            out += [("glu", 4, 512)]
            out += [("odd_out0", 8, 512), ("odd_out1", 8, 512)]
        if st in ("hyb0", "hyb1"):
            for h in range(4):
                out += [(f"{st}_qk{h}", 8, 512), (f"{st}_v{h}", 8, 512), (f"{st}_g{h}", 8, 512)]
            out += [(f"{st}_gr{i}", 8, 512) for i in range(2)]
            out += [(f"{st}_ro{i}", 16, 256) for i in range(4)]
            out += [(f"{st}_dt", 8, 32)]
            for g in range(4):
                out += [(f"{st}_xs{g}", 8, 512), (f"{st}_bc{g}", 8, 256), (f"{st}_z{g}", 8, 512)]
            out += [(f"{st}_gs{i}", 8, 512) for i in range(2)]
            out += [(f"{st}_so{i}", 16, 256) for i in range(4)]
            out += [(f"{st}_wo{i}", 8, 512) for i in range(2)]
        if st in ("ffn0", "ffn1"):
            out += [(f"{st}_gu{i}", 8, 512) for i in range(11)]
            out += [(f"{st}_dn{i}", 4 if i < 5 else 2, 1024) for i in range(6)]
        if st == "fin":
            out += [("fin_w", 1, 1024)]
    return out


def const_table(stages):
    n = {"even": 1184, "odd": 1152, "hyb0": 2008, "hyb1": 2008}
    return [(s + "_c", n[s]) for s in stages if s in n]


class Eng:

    def __init__(self, name, sem):
        self.name, self.sem, self.n, self.q, self.seen = name, sem, 0, [], {}
        self.open = False

    def wait(self, *toks):
        for t in toks:
            if t is None:
                continue
            sem, v = t
            if v > self.seen.get(id(sem), 0):
                self.seen[id(sem)] = v
                self.q.append((0, sem, v))

    def op(self, fn, w=(), chain=True, inc=True):
        self.wait(*w)
        if chain:
            self.wait((self.sem, self.n))
        if inc:
            self.n += 1
        self.open = not inc
        self.q.append((1, fn, inc))
        return (self.sem, self.n)

    def dma(self, out, in_, sem, w=()):
        self.wait(*w)
        self.q.append((2, out, in_, sem))

    @property
    def last(self):
        assert not self.open, self.name
        return (self.sem, self.n)

    def branch(self, flag, least, sub):
        self.q.append((3, flag, least, sub))

    def emit(self, eng):
        for e in self.q:
            if e[0] == 3:
                with eng.If(eng.value_load(e[1], min_val=0, max_val=1 << 20) > e[2]):
                    e[3].emit(eng)
            elif e[0] == 0:
                eng.wait_ge(e[1], e[2])
            elif e[0] == 1:
                r = e[1](eng)
                if e[2]:
                    r.then_inc(self.sem, 1)
            else:
                eng.dma_start(e[1], e[2]).then_inc(e[3], 16)


class Vec(Eng):
    def tt(self, out, a, b, op, w=()):
        return self.op(lambda e: e.tensor_tensor(out, a, b, op), w)

    def ts(self, out, a, s1, s2, op0, op1=None, w=()):
        if op1 is None:
            return self.op(lambda e: e.tensor_scalar(out, a, s1, None, op0), w)
        return self.op(lambda e: e.tensor_scalar(out, a, s1, s2, op0, op1), w)

    def stt(self, out, a, s, b, op0, op1, w=(), accum=None):
        if accum is None:
            return self.op(lambda e: e.scalar_tensor_tensor(out=out, in0=a, scalar=s, in1=b, op0=op0, op1=op1), w)
        return self.op(lambda e: e.scalar_tensor_tensor(out=out, in0=a, scalar=s, in1=b, op0=op0, op1=op1,
                                                        accum_out=accum), w)

    def cp(self, out, a, w=()):
        return self.op(lambda e: e.tensor_copy(out, a), w)

    def set(self, out, v, w=()):
        return self.op(lambda e: e.memset(out, v), w)

    def scan(self, out, d0, d1, init, op0, op1, w=()):
        return self.op(lambda e: e.tensor_tensor_scan(out, d0, d1, init, op0, op1), w)

    def red(self, out, a, op, w=()):
        return self.op(lambda e: e.tensor_reduce(out, a, AX.X, op), w)

    def rcp(self, out, a, w=()):
        return self.op(lambda e: e.reciprocal(out, a), w)


class Sca(Eng):
    def act(self, out, a, f, w=(), bias=0.0, scale=1.0):
        return self.op(lambda e: e.activation(out, a, f, bias=bias, scale=scale), w)

    def cp(self, out, a, w=()):
        return self.op(lambda e: e.activation(out, a, ACT.Copy), w)


class Ten(Eng):
    def mm(self, out, l, r, start, stop, w=(), inc=False):
        return self.op(lambda e: e.matmul(out, l, r, start=start, stop=stop), w, chain=False, inc=inc)

    def tr(self, out, a, ident, w=(), inc=False):
        return self.op(lambda e: e.transpose(out, a, ident), w, chain=False, inc=inc)


def program(nc, Wd, Pd, x_in, out_d, stages):
    ctx = ExitStack()
    with ctx:
        def sb(name, n):
            return ctx.enter_context(nc.sbuf_tensor(name, [128, n], F32))

        def sem(name):
            return ctx.enter_context(nc.semaphore(name))

        ring = sb("ring", NSLOT * SLOT)
        X = sb("x", 2048)[:, :].rearrange("p (t d) -> p t d", t=2)
        HT = sb("ht", 2048)[:, :].rearrange("p (k t) -> p k t", k=8)
        PP = sb("pp", NP)
        GS = sb("gs", 128)
        CS_T = sb("cst", 2008)
        FLAG = ctx.enter_context(nc.sbuf_tensor("flag", [128, 2], mybir.dt.int32))
        NA = 20992
        AR = sb("arena", NA)
        ps = ctx.enter_context(nc.psum_tensor("ps", [128, 8, 512], F32))

        V = Vec("v", sem("s_v"))
        A = Sca("a", sem("s_a"))
        PE = Ten("pe", sem("s_pe"))
        SP = Eng("sp", sem("s_sp"))
        s_slot = [sem(f"s_slot{i}") for i in range(NSLOT)]
        s_in = sem("s_in")
        s_over = [[sem(f"s_over{l}{n}") for n in ("v", "a", "pe", "dma")] for l in range(2)]
        s_const = sem("s_const")
        G = Vec("g", sem("s_g"))
        s_out = sem("s_out")

        def par(name, i=0, n=1):
            at = PT[name][0]
            return PP[:, at + i:at + i + n]

        ident, ones, ones64 = par("ident", 0, 128), par("ones", 0, 128), par("ones64", 0, 128)

        chunks = chunk_table(stages)
        offs, at = [], 0
        for _, k, n in chunks:
            offs.append(at)
            at += 128 * k * n
        st = {"take": 0, "sent": 0}
        freed = {}

        coffs, cn = {}, at
        for name, n in const_table(stages):
            coffs[name] = (cn, n)
            cn += 128 * n

        def consts(name):
            o, n = coffs[name]
            if st.get("cname") == name:
                return CS_T[:, 0:n], (s_const, 16 * st["consts"])
            st["cname"] = name
            st["consts"] = st.get("consts", 0) + 1
            G.dma(CS_T[:, 0:n], Wd[o:o + 128 * n].rearrange("(p n) -> p n", p=128), s_const,
                  [V.last, A.last, PE.last])
            return CS_T[:, 0:n], (s_const, 16 * st["consts"])

        def send(w=()):
            i = st["sent"]
            if i >= len(chunks):
                return
            _, k, n = chunks[i]
            s = i % NSLOT
            SP.dma(ring[:, s * SLOT:s * SLOT + k * n],
                   Wd[offs[i]:offs[i] + 128 * k * n].rearrange("(p n) -> p n", p=128), s_slot[s], w)
            st["sent"] += 1

        class Chunk:
            def __init__(self, i):
                name, k, n = chunks[i]
                s = i % NSLOT
                self.i = i
                self.ap = ring[:, s * SLOT:s * SLOT + k * n].rearrange("p (k n) -> p k n", k=k)
                self.tok = (s_slot[s], 16 * (i // NSLOT + 1))

            def free(self, *toks):
                freed[self.i] = toks
                while st["sent"] - NSLOT in freed and st["sent"] < len(chunks):
                    send(freed[st["sent"] - NSLOT])

        def take(name):
            i = st["take"]
            assert chunks[i][0] == name, (chunks[i], name)
            st["take"] += 1
            return Chunk(i)

        SP.dma(PP[:, :], Pd, s_in)
        SP.dma(X, x_in.rearrange("(t p) d -> p t d", p=128), s_in)
        for _ in range(NSLOT):
            send()
        tin = (s_in, 32)
        for e in (V, A, PE):
            e.wait(tin)

        free_banks = [(b, ()) for b in range(8)]

        def bank():
            b, toks = free_banks.pop(0)
            PE.wait(*toks)
            return b, ps[:, b, :]

        def rel(b, *toks):
            free_banks.append((b, toks))

        ar = {"at": 0}

        def buf(*shape):
            n = int(np.prod(shape))
            a = ar["at"]
            ar["at"] += n
            assert ar["at"] <= NA, ar["at"]
            v = AR[:, a:a + n]
            if len(shape) == 2:
                return v.rearrange("p (a b) -> p a b", a=shape[0])
            if len(shape) == 3:
                return v.rearrange("p (a b c) -> p a b c", a=shape[0], b=shape[1])
            return v

        def fence():
            toks = [V.last, A.last, PE.last, G.last]
            for e in (V, A, PE, G):
                e.wait(*toks)

        def phase():
            fence()
            ar["at"] = 0

        def bc(v, shape):
            return v.broadcast_to(list(shape))

        def weave(*parts):
            parts = list(parts)
            while parts:
                parts = [g for g in parts if next(g, 1) is None]

        def norm_T(gname):
            sq, xn, ss = buf(2, 1024), buf(2, 1024), buf(4)
            for t in range(2):
                V.stt(sq[:, t, :], X[:, t, :], 1.0, X[:, t, :], ALU.mult, ALU.mult, accum=ss[:, t:t + 1])
            t1 = A.act(ss[:, 2:4], ss[:, 0:2], ACT.Ln, [V.last], bias=par("eps6"), scale=1.0 / 1024)
            t2 = A.act(ss[:, 0:2], ss[:, 2:4], ACT.Exp, scale=-0.5)
            tx = [V.ts(xn[:, t, :], X[:, t, :], ss[:, t:t + 1], None, ALU.mult, w=[t2]) for t in range(2)]
            for k in range(0, 8, 2):
                b, p = bank()
                for kk in (k, k + 1):
                    for t in range(2):
                        tp = PE.tr(p[:, (kk - k) * 256 + t * 128:(kk - k) * 256 + t * 128 + 128],
                                   xn[:, t, kk * 128:(kk + 1) * 128], ident, [tx[t]],
                                   inc=(kk == k + 1 and t == 1))
                if k % 4 == 0:
                    V.ts(HT[:, k, :], p[:, 0:256], par(gname, k), None, ALU.mult, w=[tp])
                    e0 = V.ts(HT[:, k + 1, :], p[:, 256:512], par(gname, k + 1), None, ALU.mult)
                    rel(b, e0)
                else:
                    A.act(HT[:, k, :], p[:, 0:256], ACT.Copy, [tp], scale=par(gname, k))
                    e1 = A.act(HT[:, k + 1, :], p[:, 256:512], ACT.Copy, scale=par(gname, k + 1))
                    rel(b, e1)
            return xn

        def proj_T(c, cols, rhs, K, w=()):
            b, p = bank()
            for n, c0 in enumerate(cols):
                for k in range(K):
                    t = PE.mm(p[:, n * 256:(n + 1) * 256], c.ap[:, k, c0:c0 + 128], rhs[:, k, :],
                              k == 0, k == K - 1, [c.tok, *w], inc=(k == K - 1 and n == len(cols) - 1))
            return b, p, t

        def proj_T_g(c, cols, rhs, K, w=()):
            b, p = bank()
            for n, c0 in enumerate(cols):
                if n:
                    yield
                for k in range(K):
                    t = PE.mm(p[:, n * 256:(n + 1) * 256], c.ap[:, k, c0:c0 + 128], rhs[:, k, :],
                              k == 0, k == K - 1, [c.tok, *w], inc=(k == K - 1))
            return b, p, t

        def proj_tok(c, lhs, K, t, c0, n, w=(), p=None, start=True, stop=True, kl=0):
            if p is None:
                b, p = bank()
            else:
                b, p = p
            for k in range(K):
                tk = PE.mm(p[:, 0:n], lhs[:, kl + k, t * 128:(t + 1) * 128], c.ap[:, k, c0:c0 + n],
                           start and k == 0, stop and k == K - 1, [c.tok, *w], inc=(k == K - 1))
            return b, p, tk

        def out_proj(names, lhs, w):
            for i, name in enumerate(names):
                c = take(name)
                for t in range(2):
                    b, p, tk = proj_tok(c, lhs, 8, t, 0, 512, w)
                    xs = X[:, t, i * 512:(i + 1) * 512]
                    rel(b, V.tt(xs, p, xs, ALU.add, [tk]))
                c.free(tk)

        def even():
            phase()
            consts("even_c")
            norm_T("g_even")
            phase()
            M = buf(14, 256)
            LD, AA, GG, KK = (buf(4, 256) for _ in range(4))
            OT, YT = buf(8, 256), buf(4, 256)
            base = ar["at"]
            U = buf(18, 256)
            cv, tcst = consts("even_c")
            TMP, TM2 = buf(4, 256), buf(4, 256)
            R, K2, VV = M[:, 0:4, :], M[:, 4:8, :], M[:, 8:12, :]

            def p2(p):
                return p.rearrange("p (a b) -> p a b", a=2)

            def proj(i):
                c = take(f"even_in{i}")
                for j in range(0, 4 if i < 4 else 2, 2):
                    b, p, tk = proj_T(c, [j * 128, j * 128 + 128], HT, 8)
                    f = i * 4 + j
                    t = A.cp(U[:, f:f + 2, :], p2(p), [tk])
                    rel(b, t)
                    if f < 14:
                        V.tt(M[:, f:f + 2, 1:256], U[:, f:f + 2, 0:255], U[:, f:f + 2, 1:256], ALU.subtract, [t])
                        V.ts(M[:, f:f + 2, 0:1], U[:, f:f + 2, 0:1], -1.0, None, ALU.mult)
                        for g in (f, f + 1):
                            tm = V.stt(M[:, g, :], M[:, g, :], par("mu", g), U[:, g, :], ALU.mult, ALU.add)
                        last_mix[0] = tm
                c.free(tk)

            last_mix = [None]

            def head_sums(src, w, out):
                for j in (0, 2):
                    b, p = bank()
                    for i in range(2):
                        t = PE.mm(p[:, i * 256:(i + 1) * 256], ones64, src[:, j + i, :], True, True, w, inc=(i == 1))
                    rel(b, out(j, p2(p), t))

            proj(3)
            tm = last_mix[0]
            ta = A.act(U[:, 0:1, :], M[:, 12:13, :], ACT.Tanh, [tm])
            tg = A.act(U[:, 1:2, :], M[:, 13:14, :], ACT.Sigmoid)
            proj(4)
            tpl = A.last
            lora = take("lora")
            proj(1)
            for j in range(0, 4, 2):
                bw, pw = bank()
                ba, pa = bank()
                bg, pg = bank()
                for i in range(2):
                    cs = slice((j + i) * 128, (j + i + 1) * 128)
                    o = slice(i * 256, (i + 1) * 256)
                    tw = PE.mm(pw[:, o], lora.ap[0:64, 0, cs], U[0:64, 0, :], True, True, [ta, lora.tok], inc=(i == 1))
                    tg2 = PE.mm(pg[:, o], lora.ap[:, 1, cs], U[:, 1, :], True, True, [tg], inc=(i == 1))
                for i in range(2):
                    cs = slice((j + i) * 128, (j + i + 1) * 128)
                    o = slice(i * 256, (i + 1) * 256)
                    tq = PE.mm(pa[:, o], lora.ap[64:128, 0, cs], M[64:128, 12, :], True, True, [tm], inc=(i == 1))
                for i in range(2):
                    o = slice(i * 256, (i + 1) * 256)
                    e1 = A.act(LD[:, j + i, :], pw[:, o], ACT.Sigmoid, [tw], bias=par("w0", j + i))
                    e2 = A.act(AA[:, j + i, :], pa[:, o], ACT.Sigmoid, [tq], bias=par("a0", j + i))
                e3 = A.cp(GG[:, j:j + 2, :], p2(pg), [tg2])
                rel(bw, e1)
                rel(ba, e2)
                rel(bg, e3)
            tlora = PE.last
            for j in range(4):
                V.ts(KK[:, j, :], K2[:, j, :], par("k_k", j), None, ALU.mult)
            tk = V.tt(TMP, KK, KK, ALU.mult)
            V.ts(LD, LD, -math.exp(-0.5), None, ALU.mult, w=[e2])
            proj(0)
            head_sums(TMP, [tk], lambda j, p, t: V.ts(TM2[:, j:j + 2, :], p, 1e-24, None, ALU.max, w=[t]))
            tsq = A.act(TM2, TM2, ACT.Sqrt, [V.last])
            W0, W1, PD = YT, OT[:, 0:4, :], OT[:, 4:8, :]
            src, dst = U[:, 14:18, :], W0
            V.wait(tcst, tpl)
            for lv in range(4):
                s = 1 << lv
                V.tt(dst[:, lv:4, s:256], src[:, lv:4, s:256], src[:, lv:4, 0:256 - s], ALU.add)
                V.cp(dst[:, lv:4, 0:s], src[:, lv:4, 0:s])
                V.ts(PD[:, lv, :], dst[:, lv, :], 1.0 / (2 << lv), None, ALU.mult)
                src, dst = dst, (W1 if dst is W0 else W0)
            V.tt(PD[:, :, 0:16], PD[:, :, 0:16], cv[:, 1088:1152].rearrange("p (a b) -> p a b", a=4), ALU.mult)
            tpd = V.tt(PD, PD, U[:, 14:18, :], ALU.subtract)
            V.rcp(TM2, TM2, [tsq])
            V.tt(KK, KK, TM2, ALU.mult)
            for j in range(4):
                V.ts(TMP[:, j, :], AA[:, j, :], 1.0, par("k_a", j), ALU.subtract, ALU.mult, w=[PE.last, e2])
            V.stt(K2, TMP, 1.0, K2, ALU.add, ALU.mult)
            for j in range(4):
                tk = V.stt(TMP[:, j, :], R[:, j, :], par("r_k", j), K2[:, j, :], ALU.mult, ALU.mult)
            proj(2)
            for g in (0, 2):
                b, p = bank()
                for gg in range(2):
                    t = PE.mm(p[:, gg * 256:(gg + 1) * 256], lora.ap[:, 2, (g + gg) * 128:(g + gg + 1) * 128],
                              PD[:, g + gg, :], True, True, [tpd], inc=(gg == 1))
                for gg in range(2):
                    e = A.act(OT[:, 4 + g + gg, :], p[:, gg * 256:(gg + 1) * 256], ACT.Copy, [t],
                              scale=par("pool_scale", g + gg))
                rel(b, e)
            lora.free(t, tlora)
            BON = OT[:, 0:4, :]
            head_sums(TMP, [tk], lambda j, p, t: V.tt(BON[:, j:j + 2, :], p, VV[:, j:j + 2, :], ALU.mult, [t]))
            fence()

            ar["at"] = base
            XX = buf(4, 128)
            xf = XX.rearrange("p c n -> p (c n)")
            CU, PI = xf[:, 0:256], xf[:, 256:512]
            PT_, PV = (buf(256) for _ in range(2))
            AHRH = buf(2, 256)
            ah, rh = AHRH[:, 0, :], AHRH[:, 1, :]
            bh_at = ar["at"]
            bh = buf(256)
            i2_at = ar["at"]
            I2 = buf(64)
            kh, bp, kp = (buf(256) for _ in range(3))
            BB = buf(14, 512)
            Bs = [BB[:, i, :] for i in range(14)]
            VS = buf(4, 64)
            LRB, LRK = (M[:, i, :].rearrange("p (c n) -> p c n", c=4) for i in (12, 13))
            BS, QS, CS, SS = (v.rearrange("p (c n) -> p c n", c=4) for v in (bp, PV, kp, bh))
            mB, mDT, mD, mO, mL = (cv[:, i * 128:(i + 1) * 128] for i in range(5))
            mR, i2 = cv[:, 640:704], cv[:, 704:768]
            ones1 = cv[:, 1152:1153]
            V.cp(I2, i2)

            def c4(v):
                return v.rearrange("p (c n) -> p c n", c=4)

            def bd(dst, src, mask, w=()):
                nc_ = src.shape[1]
                s4 = src.unsqueeze(2).broadcast_to([128, nc_, 2, 64])
                m4 = mask.rearrange("p (h n) -> p h n", h=2).unsqueeze(1).broadcast_to([128, nc_, 2, 64])
                return V.tt(dst.rearrange("p c (h n) -> p c h n", h=2), s4, m4, ALU.mult, w)

            def pair(l, r, o, w, inc=False):
                for c in range(2):
                    t = PE.mm(o(c), l[:, c, :], r(c), True, True, w, inc=(inc and c == 1))
                return t

            def split(terms, o, w, inc=False):
                for h in range(2):
                    for c in range(len(terms)):
                        for i, (l, r) in enumerate(terms[c]):
                            end = i == len(terms[c]) - 1
                            t = PE.mm(o(c)[64 * h:64 * h + 64, :], l[:, 64 * h:64 * h + 64], r, i == 0, end, w,
                                      inc=(inc and end and h == 1 and c == len(terms) - 1))
                return t

            def half(hp, hf, tb):
                cs = slice(2 * hf, 2 * hf + 2)
                H_ = [c4(v)[:, cs, :] for v in Bs]
                bF, kF, aF, vF, bPF, kPF = H_[0:6]
                D, DT, O, LK, Vb, Bb, Kb = H_[6:13]

                def ar_(c):
                    return AHRH[:, :, (2 * hf + c) * 64:(2 * hf + c + 1) * 64]

                def bi(c):
                    at = bh_at + (2 * hf + c) * 64
                    d = i2_at - at
                    return AR[:, at:at + 2 * d].rearrange("p (x d) -> p x d", x=2)[:, :, 0:64]

                bA, pA = bank()
                bB, pB = bank()
                bC, pC = bank()
                pair(bF, ar_, lambda c: pA[:, c * 128:(c + 1) * 128].rearrange("p (x n) -> p x n", x=2), [tb])
                tA = pair(kF, ar_, lambda c: pA[:, 256 + c * 128:384 + c * 128].rearrange("p (x n) -> p x n", x=2), [tb],
                          True)
                yield
                pair(aF, bi, lambda c: pB[:, c * 128:(c + 1) * 128].rearrange("p (x n) -> p x n", x=2), [tb])
                split([[(vF[:, c, :], i2)] for c in range(2)], lambda c: pB[:, 256 + c * 64:320 + c * 64], [tb])
                tB = split([[(bPF[:, c, :], i2)] for c in range(2)], lambda c: pB[:, 384 + c * 64:448 + c * 64], [tb],
                           True)
                tC = split([[(kPF[:, c, :], i2)] for c in range(2)], lambda c: pC[:, c * 64:(c + 1) * 64], [tb], True)
                vA = pA.rearrange("p (m c x n) -> p m c x n", m=2, c=2, x=2)
                vB = pB[:, 0:256].rearrange("p (c x n) -> p c x n", c=2, x=2)
                bd(DT, vA[:, 0, :, 0, :], mDT, [tA])
                bd(D, vB[:, :, 0, :], mD, [tB])
                tD = V.last
                bd(LK, vA[:, 1, :, 0, :], mL)
                mR4 = mR.unsqueeze(1).broadcast_to([128, 2, 64])
                V.tt(LRB[:, cs, :], vA[:, 0, :, 1, :], mR4, ALU.mult)
                rel(bA, V.tt(LRK[:, cs, :], vA[:, 1, :, 1, :], mR4, ALU.mult))
                tV = V.cp(VS[:, cs, :], pB[:, 256:384].rearrange("p (c n) -> p c n", c=2))
                D2, D2T, D4, D4T, D8, ET = H_[0:6]
                bQ, pQ = bank()
                pair(DT, lambda c: D[:, c, :], lambda c: pQ[:, c * 128:(c + 1) * 128], [tD])
                tQ = pair(D, lambda c: DT[:, c, :], lambda c: pQ[:, 256 + c * 128:384 + c * 128], [tD], True)
                q = BB[:, 0:2, :].rearrange("p m (c n) -> p m c n", c=4)[:, :, cs, :]
                t2 = A.cp(q, pQ.rearrange("p (m c n) -> p m c n", m=2, c=2), [tQ, tC])
                rel(bQ, t2)
                bd(O, vB[:, :, 0, :], mO)
                V.cp(XX[:, cs, 0:64], vB[:, :, 1, :])
                bd(Vb, pB[:, 256:384].rearrange("p (c n) -> p c n", c=2), mB)
                V.cp(BS[:, cs, :], pB[:, 384:512].rearrange("p (c n) -> p c n", c=2))
                rel(bB, bd(Bb, pB[:, 384:512].rearrange("p (c n) -> p c n", c=2), mB))
                rel(bC, bd(Kb, pC[:, 0:128].rearrange("p (c n) -> p c n", c=2), mB, [tC]))
                idb = ident.unsqueeze(1).broadcast_to([128, 2, 128])
                tE = V.tt(ET, DT, idb, ALU.add)
                yield
                bQ, pQ = bank()
                tl = split([[(LK[:, c, :], VS[:, 2 * hf + c, :])] for c in range(2)],
                           lambda c: pQ[:, c * 64:(c + 1) * 64], [tV], True)
                rel(bQ, V.cp(XX[:, cs, 64:128], pQ[:, 0:128].rearrange("p (c n) -> p c n", c=2), [tl]))
                bQ, pQ = bank()
                t = pair(D2T, lambda c: D2[:, c, :], lambda c: pQ[:, c * 128:(c + 1) * 128], [t2], True)
                t4 = A.cp(D4, pQ[:, 0:256].rearrange("p (c n) -> p c n", c=2), [t])
                rel(bQ, t4)
                yield
                bQ, pQ = bank()
                de = BB[:, 1:9, :].rearrange("p (x m) (c n) -> p x m c n", x=2, c=4)[:, :, 0, cs, :]
                t = pair(D2, lambda c: de[:, :, c, :], lambda c: pQ[:, c * 256:(c + 1) * 256].rearrange(
                    "p (x n) -> p x n", x=2), [tE, t4], True)
                vQ = pQ.rearrange("p (c x n) -> p c x n", c=2, x=2)
                t4t = A.cp(D4T, vQ[:, :, 0, :], [t])
                tE = V.tt(ET, vQ[:, :, 1, :], ET, ALU.add, [t, t4t])
                rel(bQ, tE)
                yield
                bQ, pQ = bank()
                t = pair(D4T, lambda c: D4[:, c, :], lambda c: pQ[:, c * 128:(c + 1) * 128], [t4t], True)
                t8 = A.cp(D8, pQ[:, 0:256].rearrange("p (c n) -> p c n", c=2), [t])
                rel(bQ, t8)
                for l, tl in ((D4, tE), (D8, t8)):
                    bQ, pQ = bank()
                    t = pair(l, lambda c: ET[:, c, :], lambda c: pQ[:, c * 128:(c + 1) * 128], [tl, tE], True)
                    tE = V.tt(ET, pQ[:, 0:256].rearrange("p (c n) -> p c n", c=2), ET, ALU.add, [t])
                    rel(bQ, tE)
                    yield
                G, GT, G2T = H_[0], H_[2], H_[1]
                bQ, pQ = bank()
                bR, pR = bank()
                pair(ET, lambda c: O[:, c, :], lambda c: pQ[:, c * 128:(c + 1) * 128], [tE])
                tq = pair(ET, lambda c: XX[:, 2 * hf + c, :], lambda c: pQ[:, 256 + c * 128:384 + c * 128], [tE], True)
                tr_ = pair(O, lambda c: ET[:, c, :], lambda c: pR[:, c * 128:(c + 1) * 128], [tE], True)
                A.cp(G, pQ[:, 0:256].rearrange("p (c n) -> p c n", c=2), [tq])
                tg = A.last
                tg2 = A.cp(GT, pR[:, 0:256].rearrange("p (c n) -> p c n", c=2), [tr_])
                rel(bR, tg2)
                tx = V.cp(XX[:, cs, :], pQ[:, 256:512].rearrange("p (c n) -> p c n", c=2), [tq, tg])
                rel(bQ, tx)
                yield
                bQ, pQ = bank()
                t = pair(G, lambda c: GT[:, c, :], lambda c: pQ[:, c * 128:(c + 1) * 128], [tg2], True)
                t = A.cp(G2T, pQ[:, 0:256].rearrange("p (c n) -> p c n", c=2), [t])
                rel(bQ, t)
                yield
                for l, tl in ((G2T, t), (GT, tg2)):
                    bQ, pQ = bank()
                    t = pair(l, lambda c: XX[:, 2 * hf + c, :], lambda c: pQ[:, c * 128:(c + 1) * 128], [tl, tx], True)
                    tx = V.tt(XX[:, cs, :], pQ[:, 0:256].rearrange("p (c n) -> p c n", c=2), XX[:, cs, :], ALU.add, [t])
                    rel(bQ, tx)
                    yield
                M1, M2, AT = H_[3], H_[4], H_[5]
                tm = bd(M1, XX[:, cs, 0:64], mB)
                bQ, pQ = bank()
                split([[(M1[:, c, :], LRB[:, 2 * hf + c, :])] for c in range(2)], lambda c: pQ[:, c * 64:(c + 1) * 64],
                      [tm])
                split([[(M1[:, c, :], BS[:, 2 * hf + c, :])] for c in range(2)],
                      lambda c: pQ[:, 128 + c * 64:192 + c * 64], [tm])
                t = split([[(Bb[:, c, :], XX[:, 2 * hf + c, 64:128]), (Kb[:, c, :], VS[:, 2 * hf + c, :])]
                           for c in range(2)], lambda c: pQ[:, 256 + c * 64:320 + c * 64], [tm], True)
                bd(M2, XX[:, cs, 64:128], mB)
                V.tt(QS[:, cs, :], pQ[:, 0:128].rearrange("p (c n) -> p c n", c=2), c4(rh)[:, cs, :], ALU.add, [t])
                PCh = c4(PT_)[:, cs, 63:64]
                V.tt(CS[:, cs, :], i2.unsqueeze(1).broadcast_to([128, 2, 64]), bc(PCh, [128, 2, 64]), ALU.mult)
                V.tt(CS[:, cs, :], pQ[:, 128:256].rearrange("p (c n) -> p c n", c=2), CS[:, cs, :], ALU.add)
                bd(AT, CS[:, cs, :], mB)
                rel(bQ, V.cp(CS[:, cs, :], pQ[:, 256:384].rearrange("p (c n) -> p c n", c=2)))
                yield

            for hp in range(4):
                for e in (V, A):
                    e.wait(V.last, A.last, PE.last)
                for c in range(4):
                    s = slice(c * 64, (c + 1) * 64)
                    V.scan(CU[:, s], bc(ones1, [128, 64]), LD[:, hp, s], 0.0, ALU.mult, ALU.add)
                V.tt(PV, CU, LD[:, hp, :], ALU.subtract)
                tv = V.last
                te = A.act(PV, PV, ACT.Exp, [tv])
                te2 = A.act(PI, CU, ACT.Exp, scale=-1.0)
                te3 = A.act(PT_, CU, ACT.Exp)
                V.tt(bh, KK[:, hp, :], AA[:, hp, :], ALU.mult)
                V.stt(ah, KK[:, hp, :], -1.0, PV, ALU.mult, ALU.mult, [te])
                V.tt(bh, bh, PI, ALU.mult, [te2])
                V.tt(kh, K2[:, hp, :], PI, ALU.mult)
                V.tt(rh, R[:, hp, :], PT_, ALU.mult, [te3])
                PC = c4(PT_)[:, :, 63:64]
                for i, v in enumerate((bh, kh, ah)):
                    bd(c4(Bs[i]), c4(v), mB)
                bd(c4(Bs[3]), c4(VV[:, hp, :]), mB)
                V.tt(c4(bp), c4(bh), bc(PC, [128, 4, 64]), ALU.mult)
                bd(c4(Bs[4]), c4(bp), mB)
                V.tt(c4(kp), c4(kh), bc(PC, [128, 4, 64]), ALU.mult)
                bd(c4(Bs[5]), c4(kp), mB)
                tb = V.last
                weave(half(hp, 0, tb), half(hp, 1, tb))
                Vb, M2, AT, ST = (c4(Bs[i]) for i in (10, 4, 5, 13))
                V.cp(SS[:, 0, :], CS[:, 0, :])
                bd(ST[:, 0:1, :], SS[:, 0:1, :], mB)
                tst = [V.last]
                for c in range(1, 3):
                    b, p = bank()
                    t = split([[(AT[:, c, :], SS[:, c - 1, :])]], lambda _: p[:, 0:64], [V.last], True)
                    rel(b, V.tt(SS[:, c, :], p[:, 0:64], CS[:, c, :], ALU.add, [t]))
                    tst.append(bd(ST[:, c:c + 1, :], SS[:, c:c + 1, :], mB))
                for c in range(4):
                    terms = [(M2[:, c, :], LRB[:, c, :]), (Vb[:, c, :], LRK[:, c, :])]
                    if c:
                        terms.append((ST[:, c - 1, :], QS[:, c, :]))
                    if c % 2 == 0:
                        b, p = bank()
                    t = split([terms], lambda _: p[:, (c % 2) * 64:(c % 2) * 64 + 64], [tst[max(c - 1, 0)]], True)
                    if c % 2:
                        rel(b, A.cp(YT[:, hp, (c - 1) * 64:(c + 1) * 64], p[:, 0:128], [t]))
            fence()
            ar["at"] = base
            Y2, RS = buf(4, 256), buf(4, 256)
            for j in range(0, 4, 2):
                b, p = bank()
                for i in range(2):
                    t = PE.mm(p[:, i * 256:(i + 1) * 256], ones64, YT[:, j + i, :], True, True, [V.last], inc=(i == 1))
                pv = p.rearrange("p (a b) -> p a b", a=2)
                rel(b, V.stt(YT[:, j:j + 2, :], pv, -1.0 / 64, YT[:, j:j + 2, :], ALU.mult, ALU.add, [t]))
            tk = V.tt(Y2, YT, YT, ALU.mult)
            for j in range(0, 4, 2):
                b, p = bank()
                for i in range(2):
                    t = PE.mm(p[:, i * 256:(i + 1) * 256], ones64, Y2[:, j + i, :], True, True, [tk], inc=(i == 1))
                rel(b, A.act(RS[:, j:j + 2, :], p.rearrange("p (a b) -> p a b", a=2), ACT.Ln, [t],
                             bias=par("epsln"), scale=1.0 / 64))
            t = A.act(RS, RS, ACT.Exp, scale=-0.5)
            V.tt(YT, YT, RS, ALU.mult, [t])
            for j in range(4):
                V.ts(YT[:, j, :], YT[:, j, :], par("ln_g", j), par("ln_b", j), ALU.mult, ALU.add)
            V.tt(YT, YT, BON, ALU.add)
            t = V.tt(OT[:, 0:4, :], YT, GG, ALU.mult)
            out_proj(["even_out0", "even_out1"], OT, [t])

        def over(l, G, flag):
            names = s_over[l]
            V2, A2, P2 = Vec("v2", names[0]), Sca("a2", names[1]), Ten("pe2", names[2])
            S2 = Eng("sp2", None)
            toks = [V.last, A.last, PE.last]
            for e in (V2, A2, P2, S2):
                e.wait(*toks)
            W3 = AR[:, 0:3 * SLOT]
            sg = AR[:, 3 * SLOT:3 * SLOT + 1024].rearrange("p (a b) -> p a b", a=4)
            hi = AR[:, 3 * SLOT + 1024:3 * SLOT + 2048].rearrange("p (a b) -> p a b", a=4)
            wg = W3[:, 0:SLOT].rearrange("p (k n) -> p k n", k=8)
            wu = W3[:, SLOT:2 * SLOT].rearrange("p (k n) -> p k n", k=8)
            wd = W3[:, 2 * SLOT:3 * SLOT].rearrange("p (k n) -> p k n", k=4)
            first = [i for i, c in enumerate(chunks) if c[0] == f"moe{l}_g0_0"][0]
            tp = tv = None
            for e in range(NE):
                q, j = e // 4, e % 4
                S2.wait(tp)
                for part, dst in ((0, wg), (4, wu), (8, wd)):
                    for c in range(4):
                        o = offs[first + 12 * q + part + c]
                        src = Wd[o:o + 128 * SLOT].rearrange("(p k n) -> p k n", p=128, k=8 if part < 8 else 4)
                        if part < 8:
                            S2.dma(dst[:, 2 * c:2 * c + 2, :], src[:, j::4, :], names[3])
                        else:
                            S2.dma(dst[:, c, :], src[:, j, :], names[3])
                td = (names[3], 16 * 12 * (e + 1))
                for i in range(4):
                    for k in range(8):
                        P2.mm(ps[:, i, 0:256], wg[:, k, i * 128:(i + 1) * 128], HT[:, k, :], k == 0, k == 7, [td, tv])
                    for k in range(8):
                        t = P2.mm(ps[:, 4 + i, 0:256], wu[:, k, i * 128:(i + 1) * 128], HT[:, k, :], k == 0, k == 7,
                                  inc=(k == 7))
                a = A2.act(sg, ps[:, 0:4, 0:256], ACT.Silu, [t, tv])
                v = V2.tt(hi, ps[:, 4:8, 0:256], sg, ALU.mult, [t, a])
                for n in range(2):
                    for t in range(2):
                        b = 2 * n + t
                        for k in range(4):
                            tp = P2.mm(ps[:, b, :], hi[:, k, t * 128:(t + 1) * 128], wd[:, k, n * 512:(n + 1) * 512],
                                       k == 0, k == 3, [v, a], inc=(k == 3))
                for n in range(2):
                    for t in range(2):
                        xs = X[:, t, n * 512:(n + 1) * 512]
                        tv = V2.stt(xs, ps[:, 2 * n + t, :], G[:, t, e:e + 1], xs, ALU.mult, ALU.add, [tp])
            for e in (V2, A2, P2, S2):
                e.wait(V2.last, A2.last, P2.last)
            for e, s2 in ((V, V2), (A, A2), (PE, P2), (SP, S2)):
                e.branch(flag, 0, s2)

        def moe(stg, l):
            phase()
            nxt = stages[stages.index(stg) + 1:][:1]
            if nxt and nxt[0] + "_c" in coffs:
                consts(nxt[0] + "_c")
            XN = norm_T(f"g_{stg}")
            hd = [V.last, A.last]
            L = buf(2, 36)
            EX, MG, CM = buf(2, 4), buf(2, 4), buf(2, 4)
            PR = buf(2, 4, 8)
            EL, M1, M2, C8, W8 = (buf(2, 8) for _ in range(5))
            s1 = [buf(2, 1) for _ in range(8)]
            Gf, Sf, POS, GO = (buf(2, 32) for _ in range(4))
            G, SE = (v.rearrange("p t (g j) -> p t g j", g=4) for v in (Gf, Sf))
            c = take(stg + "_r")
            for t in range(2):
                b, p, tk = proj_tok(c, HT, 8, t, 0, 36, hd)
                rel(b, V.tt(L[:, t, :], p[:, 0:36], par(f"rb{l}", 0, 36), ALU.add, [tk]))
            c.free(tk)

            def first(mask, cum, n):
                for t in range(2):
                    V.scan(cum[:, t, :], mask[:, t, :], mask[:, t, :], 0.0, ALU.max, ALU.max)
                V.cp(mask[:, :, 0:1], cum[:, :, 0:1])
                V.tt(mask[:, :, 1:n], cum[:, :, 1:n], cum[:, :, 0:n - 1], ALU.subtract)

            def spread(dst, w):
                for t in range(2):
                    V.tt(dst[:, t], MG[:, t, :].unsqueeze(2).broadcast_to([128, 4, 8]),
                         w[:, t, :].unsqueeze(1).broadcast_to([128, 4, 8]), ALU.mult)

            gm, gw, e1, e2, p2, den, g1, g2 = s1
            V.red(gm, L[:, :, 0:4], ALU.max)
            V.tt(EX, L[:, :, 0:4], bc(gm, [128, 2, 4]), ALU.subtract)
            V.ts(MG, EX, 0.0, None, ALU.is_ge)
            t = A.act(EX, EX, ACT.Exp, [V.last])
            first(MG, CM, 4)
            V.tt(PR, L[:, :, 4:36].rearrange("p t (g j) -> p t g j", g=4),
                 MG.unsqueeze(3).broadcast_to([128, 2, 4, 8]), ALU.mult)
            V.red(EL, PR.rearrange("p t g j -> p t j g"), ALU.add)
            V.red(e1, EL, ALU.max)
            V.tt(EL, EL, bc(e1, [128, 2, 8]), ALU.subtract)
            V.ts(M1, EL, 0.0, None, ALU.is_ge)
            first(M1, C8, 8)
            V.stt(EL, M1, -1e30, EL, ALU.mult, ALU.add)
            V.red(e2, EL, ALU.max)
            t = A.act(p2, e2, ACT.Exp, [V.last])
            V.tt(M2, EL, bc(e2, [128, 2, 8]), ALU.is_ge)
            first(M2, C8, 8)
            V.tt(W8, M1, M2, ALU.add)
            spread(SE, W8)
            tse = V.last
            tri = par("tri", 0, 128)
            b, p = bank()
            PE.mm(p[:, 0:32], tri, Sf[:, 0, :], True, True, [tse])
            PE.mm(p[:, 32:64], ones, Sf[:, 0, :], True, False)
            PE.mm(p[:, 32:64], tri, Sf[:, 1, :], False, True)
            PE.mm(p[:, 64:96], ones, Sf[:, 0, :], True, False)
            tk = PE.mm(p[:, 64:96], ones, Sf[:, 1, :], False, True, inc=True)
            V.red(gw, EX, ALU.add, [t])
            V.rcp(gw, gw)
            V.ts(den, p2, 1.0, None, ALU.add)
            V.rcp(den, den)
            V.tt(g1, gw, den, ALU.mult)
            V.tt(g2, g1, p2, ALU.mult)
            V.tt(M1, M1, bc(g1, [128, 2, 8]), ALU.mult)
            V.tt(M2, M2, bc(g2, [128, 2, 8]), ALU.mult)
            V.tt(W8, M1, M2, ALU.add)
            spread(G, W8)
            V.tt(POS, p[:, 0:64].rearrange("p (t e) -> p t e", t=2), Sf, ALU.mult, [tk])
            V.red(e1[:, 0, :], p[:, 64:96], ALU.max)
            rel(b, V.last)
            V.ts(e1[:, 0, :], e1[:, 0, :], float(CAP), 0.0, ALU.subtract, ALU.max)
            V.cp(FLAG[:, l:l + 1], e1[:, 0, :])
            V.ts(GO, POS, CAP + 0.5, None, ALU.is_ge)
            V.tt(GO, GO, Gf, ALU.mult)
            V.ts(POS, POS, 1.0, None, ALU.subtract)
            S = buf(2, NE * CAP)
            for t in range(2):
                ts_ = V.tt(S[:, t, :].rearrange("p (e c) -> p e c", c=CAP),
                           POS[:, t, :].unsqueeze(2).broadcast_to([128, NE, CAP]),
                           par("iota", 0, CAP).unsqueeze(1).broadcast_to([128, NE, CAP]), ALU.is_equal)
            XG = buf(8, NE * CAP)
            for n in range(2):
                for k in range(8):
                    b, p = bank()
                    for t in range(2):
                        tk = PE.mm(p, XN[:, t, k * 128:(k + 1) * 128], S[:, t, n * 512:(n + 1) * 512], t == 0, t == 1,
                                   [ts_], inc=(t == 1))
                    dst = XG[:, k, n * 512:(n + 1) * 512]
                    if k % 2:
                        rel(b, A.act(dst, p, ACT.Copy, [tk], scale=par(f"g_{stg}", k)))
                    else:
                        rel(b, V.ts(dst, p, par(f"g_{stg}", k), None, ALU.mult, w=[tk]))
            tx = [V.last, A.last]
            for t in range(2):
                v = S[:, t, :].rearrange("p (e c) -> p e c", c=CAP)
                ts_ = V.tt(v, v, Gf[:, t, :].unsqueeze(2).broadcast_to([128, NE, CAP]), ALU.mult, [PE.last])
            SG = [buf(512) for _ in range(2)]
            HI = [buf(512) for _ in range(2)]
            HTr = [buf(4, 128) for _ in range(2)]
            SC = [buf(2, 128) for _ in range(2)]
            YS = [buf(2, 512) for _ in range(2)]
            done = [None, None]
            for q in range(NE // 4):
                u = q % 2
                sg, hi, htr, sc, ys = SG[u], HI[u], HTr[u], SC[u], YS[u]
                res = []
                for part in "gu":
                    b, p = bank()
                    for c in range(4):
                        ck = take(f"{stg}_{part}{q}_{c}")
                        for kk in range(2):
                            for j in range(4):
                                k = 2 * c + kk
                                tk = PE.op(lambda e, p=p, j=j, k=k, q=q, w=ck.ap[:, kk * 4 + j, :]: e.matmul(
                                    p[32 * j:32 * j + 32, :], XG[:, k, (4 * q + j) * CAP:(4 * q + j + 1) * CAP], w,
                                    start=(k == 0), stop=(k == 7)),
                                    [ck.tok, *tx], chain=False, inc=(kk == 1 and j == 3))
                        ck.free(tk)
                    res.append((b, p, tk))
                b, p, tk = res[0]
                a = A.act(sg, p, ACT.Silu, [tk, done[u]])
                rel(b, a)
                b, p, tk = res[1]
                v = V.tt(hi, p, sg, ALU.mult, [tk, a])
                rel(b, v)
                b, p = bank()
                for t in range(2):
                    tk = PE.tr(p[:, t * 128:(t + 1) * 128], S[:, t, q * 128:(q + 1) * 128], ident, [ts_], inc=(t == 1))
                a2 = A.cp(sc, p[:, 0:256].rearrange("p (a b) -> p a b", a=2), [tk, done[u]])
                rel(b, a2)
                b, p = bank()
                for k in range(4):
                    tk = PE.tr(p[:, k * 128:(k + 1) * 128], hi[:, k * 128:(k + 1) * 128], ident, [v], inc=(k == 3))
                v = V.cp(htr, p.rearrange("p (a b) -> p a b", a=4), [tk, done[u]])
                rel(b, v)
                b0, p0 = bank()
                b1, p1 = bank()
                for k in range(4):
                    ck = take(f"{stg}_d{q}_{k}")
                    for n, p in ((0, p0), (1, p1)):
                        for j in range(4):
                            tk = PE.op(lambda e, p=p, j=j, k=k, n=n, w=ck.ap[:, j, n * 512:(n + 1) * 512], h=htr: e.matmul(
                                p[32 * j:32 * j + 32, :], h[:, k, j * CAP:(j + 1) * CAP], w,
                                start=(k == 0), stop=(k == 3)),
                                [ck.tok, v], chain=False, inc=(n == 1 and j == 3))
                    ck.free(tk)
                a = A.cp(ys[:, 0, :], p0, [tk, done[u]])
                v = V.cp(ys[:, 1, :], p1, [tk, done[u]])
                rel(b0, a)
                rel(b1, v)
                for n, w in ((0, a), (1, v)):
                    for t in range(2):
                        b, p = bank()
                        tk = PE.mm(p, sc[:, t, :], ys[:, n, :], True, True, [w, a2], inc=True)
                        xs = X[:, t, n * 512:(n + 1) * 512]
                        rel(b, V.tt(xs, p, xs, ALU.add, [tk]))
                done[u] = tk
            GOk = GS[:, l * 64:(l + 1) * 64].rearrange("p (t e) -> p t e", t=2)
            V.cp(GOk, GO)
            fence()
            over(l, GOk, FLAG[0:1, l:l + 1])

        def odd():
            phase()
            norm_T("g_odd")
            phase()
            cv, tcst = consts("odd_c")
            cosT, sinT, cmask = cv[:, 0:256], cv[:, 256:512], cv[:, 512:768]
            RT, trow = cv[:, 768:896], cv[:, 896:1152]
            OT = buf(8, 256)
            U5 = buf(4, 256)
            QK, VT = buf(8, 256), buf(2, 512)
            SQ, RS = buf(4, 256), buf(4, 256)
            PRb = buf(4, 256)
            PR = [PRb[:, 0:2, :], PRb[:, 2:4, :]]
            AT = [buf(2, 256) for _ in range(2)]
            mx, sm, lm = buf(32), buf(32), buf(8)
            s16 = [buf(16) for _ in range(14)]
            Y5, AG, KF, SN, CS_, BR, BI, TA, TB = (buf(4, 256) for _ in range(9))
            lam_init = 0.8 - 0.6 * math.exp(-0.3)
            MAGIC = 12582912.0
            C1, C2, C3 = 6.28125, 0.0019350051879882812, 3.0199159819568e-07

            def p2(p):
                return p.rearrange("p (a b) -> p a b", a=2)

            c = take("odd_in3")
            for j in (0, 2):
                b, p, tk = proj_T(c, [j * 128, j * 128 + 128], HT, 8)
                tu = A.cp(U5[:, j:j + 2, :], p2(p), [tk])
                rel(b, tu)
            c.free(tk)
            lp = par("lam", 0, 256).rearrange("p (a b) -> p a b", a=4)
            V.tt(SQ[:, 0:1, 0:64], lp[:, 0:1, :], lp[:, 1:2, :], ALU.mult)
            V.tt(SQ[:, 1:2, 0:64], lp[:, 2:3, :], lp[:, 3:4, :], ALU.mult)
            V.red(lm[:, 0:2], SQ[:, 0:2, 0:64], ALU.add)
            t = A.act(lm[:, 2:4], lm[:, 0:2], ACT.Exp, [V.last])
            V.tt(lm[:, 4:5], lm[:, 3:4], lm[:, 2:3], ALU.subtract, [t])
            V.ts(lm[:, 4:5], lm[:, 4:5], lam_init, None, ALU.subtract)
            nlam = lm[:, 4:5]

            def attention():
                for i in range(2):
                    c = take(f"odd_in{i}")
                    for j in (0, 2):
                        b, p, tk = yield from proj_T_g(c, [j * 128, j * 128 + 128], HT, 8)
                        t = A.cp(QK[:, i * 4 + j:i * 4 + j + 2, :], p2(p), [tk])
                        rel(b, t)
                        yield
                    c.free(tk)
                    X4 = QK[:, 4 * i:4 * i + 4, :]
                    t = V.tt(SQ, X4, X4, ALU.mult, [t, PE.last])
                    yield
                    for j in (0, 2):
                        b, p = bank()
                        for ii in range(2):
                            tk = PE.mm(p[:, ii * 256:(ii + 1) * 256], ones64, SQ[:, j + ii, :], True, True, [t],
                                       inc=(ii == 1))
                        rel(b, A.act(RS[:, j:j + 2, :], p2(p), ACT.Ln, [tk, V.last], bias=par("eps6"), scale=1.0 / 64))
                    t = A.act(RS, RS, ACT.Exp, scale=-0.5)
                    t = V.stt(X4, X4, par("kn" if i else "qn"), RS, ALU.mult, ALU.mult, [t])
                    V.wait(tcst)
                    yield
                    for j in (0, 2):
                        b, p = bank()
                        for ii in range(2):
                            tk = PE.mm(p[:, ii * 256:(ii + 1) * 256], RT, X4[:, j + ii, :], True, True, [t, tcst],
                                       inc=(ii == 1))
                        rel(b, V.tt(SQ[:, j:j + 2, :], p2(p), sinT.unsqueeze(1).broadcast_to([128, 2, 256]), ALU.mult,
                                    [tk]))
                    V.tt(X4, X4, cosT.unsqueeze(1).broadcast_to([128, 4, 256]), ALU.mult, [PE.last])
                    tq = V.tt(X4, X4, SQ, ALU.add)
                c = take("odd_in2")
                for t in range(2):
                    b, p, tk = proj_tok(c, HT, 8, t, 0, 512)
                    rel(b, A.cp(VT[:, t, :], p, [tk]))
                    yield
                c.free(tk)
                av = [None, None]
                YO = SQ
                for h in range(4):
                    for q in range(2):
                        nk = (q + 1) * 128
                        pr = PR[q]
                        i0 = h * 4 + q * 2
                        for m in range(2):
                            b, p = bank()
                            tk = PE.mm(p[:, 0:nk], QK[m * 64:(m + 1) * 64, h, q * 128:(q + 1) * 128],
                                       QK[m * 64:(m + 1) * 64, 4 + h, 0:nk], True, True, [tq], inc=True)
                            rel(b, V.stt(pr[:, m, 0:nk], p[:, 0:nk], 0.125, cmask[:, 256 - nk:256], ALU.mult, ALU.add,
                                         [tk]))
                        V.red(mx[:, i0:i0 + 2], pr[:, :, 0:nk], ALU.max)
                        V.ts(mx[:, i0:i0 + 2], mx[:, i0:i0 + 2], -1.0, None, ALU.mult)
                        tv = V.last
                        yield
                        for m in range(2):
                            ta = A.act(pr[:, m, 0:nk], pr[:, m, 0:nk], ACT.Exp, [tv], bias=mx[:, i0 + m:i0 + m + 1])
                        V.red(sm[:, i0:i0 + 2], pr[:, :, 0:nk], ALU.add, [ta])
                        V.rcp(sm[:, i0:i0 + 2], sm[:, i0:i0 + 2])
                        V.tt(sm[:, i0 + 1:i0 + 2], sm[:, i0 + 1:i0 + 2], nlam, ALU.mult)
                        V.ts(pr[:, 0, 0:nk], pr[:, 0, 0:nk], sm[:, i0:i0 + 1], None, ALU.mult)
                        t = V.stt(pr[:, 0, 0:nk], pr[:, 1, 0:nk], sm[:, i0 + 1:i0 + 2], pr[:, 0, 0:nk], ALU.mult,
                                  ALU.add)
                        b, p = bank()
                        for kb in range(q + 1):
                            tk = PE.tr(p[:, kb * 128:(kb + 1) * 128], pr[:, 0, kb * 128:(kb + 1) * 128], ident, [t],
                                       inc=(kb == q))
                        at = AT[h % 2]
                        e = A.cp(at[:, 0:q + 1, q * 128:(q + 1) * 128],
                                 p[:, 0:nk].rearrange("p (a b) -> p a b", a=q + 1), [tk, av[h % 2]])
                        rel(b, e)
                        V.wait(tk)
                        yield
                    b, p = bank()
                    PE.mm(p[:, 0:256], VT[:, 0, h * 128:(h + 1) * 128], at[:, 0, :], True, False, [e])
                    tk = PE.mm(p[:, 128:256], VT[:, 1, h * 128:(h + 1) * 128], at[:, 1, 128:256], False, True, inc=True)
                    av[h % 2] = tk
                    rel(b, A.cp(YO[:, h, :], p[:, 0:256], [tk, V.last]))
                    yield
                t = V.tt(PRb, YO, YO, ALU.mult, [A.last, PE.last])
                for j in (0, 2):
                    b, p = bank()
                    for i in range(2):
                        tk = PE.mm(p[:, i * 256:(i + 1) * 256], ones, PRb[:, j + i, :], True, True, [t], inc=(i == 1))
                    rel(b, A.act(RS[:, j:j + 2, :], p2(p), ACT.Ln, [tk], bias=par("eps5"), scale=1.0 / 128))
                t = A.act(RS, RS, ACT.Exp, scale=-0.5)
                yield
                V.stt(OT[:, 0:4, :], YO, 1.0 - lam_init, RS, ALU.mult, ALU.mult, [t])
                V.ts(OT[:, 0:4, :], OT[:, 0:4, :], par("subln"), None, ALU.mult)

            lr, st_, rho, th, ph, kf, sn, cs, nr, ni, de, cr, ci, tp = s16

            def reduce2pi(dst, src, k):
                V.ts(k, src, 1.0 / (2 * math.pi), MAGIC, ALU.mult, ALU.add)
                V.ts(k, k, MAGIC, None, ALU.subtract)
                V.stt(dst, k, -C1, src, ALU.mult, ALU.add)
                V.stt(dst, k, -C2, dst, ALU.mult, ALU.add)
                V.stt(dst, k, -C3, dst, ALU.mult, ALU.add)
                return V.ts(dst, dst, 3.1415925, -3.1415925, ALU.min, ALU.max)

            def sincos(sn, cs, r, tmp, w):
                t1 = V.stt(tmp, r, -1.0, r, ALU.mult, ALU.max, w)
                A.act(sn, r, ACT.Sin, [t1])
                return A.act(cs, tmp, ACT.Sin, bias=par("hpi"), scale=-1.0)

            def s5():
                cC, cB = take("s5_C"), take("s5_B")
                sB = cB.ap[:, 0, :].rearrange("p (r i n) -> p r i n", r=2, i=16)
                sC = cC.ap[:, 0, :].rearrange("p (r i n) -> p r i n", r=2, i=16)
                V.ts(lr, par("s5_re", 0, 16), -1e-4, None, ALU.min)
                li = par("s5_im", 0, 16)
                t = A.act(st_, par("s5_ls", 0, 16), ACT.Exp)
                V.tt(rho, lr, st_, ALU.mult, [t])
                t = A.act(rho, rho, ACT.Exp, [V.last])
                V.tt(th, li, st_, ALU.mult)
                t = reduce2pi(ph, th, kf)
                t = sincos(sn, cs, ph, tp, [t])
                V.tt(nr, rho, cs, ALU.mult, [t])
                V.ts(nr, nr, 1.0, None, ALU.subtract)
                V.tt(ni, rho, sn, ALU.mult)
                V.tt(de, lr, lr, ALU.mult)
                V.tt(tp, li, li, ALU.mult)
                V.tt(de, de, tp, ALU.add)
                V.rcp(de, de)
                V.tt(cr, nr, lr, ALU.mult)
                V.tt(tp, ni, li, ALU.mult)
                V.tt(cr, cr, tp, ALU.add)
                V.tt(cr, cr, de, ALU.mult)
                V.tt(ci, ni, lr, ALU.mult)
                V.tt(tp, nr, li, ALU.mult)
                V.tt(ci, ci, tp, ALU.subtract)
                V.tt(ci, ci, de, ALU.mult)
                crb, cib = (v.unsqueeze(2).broadcast_to([128, 16, 32]) for v in (cr, ci))
                c_re, c_im = sC[:, 0], sC[:, 1]
                x1, x2, x3 = (v.rearrange("p a b -> p (a b)")[:, 0:512].rearrange("p (a b) -> p a b", a=16)
                              for v in (AG, KF, TA))
                V.tt(x1, c_re, cib, ALU.mult, [cC.tok])
                V.tt(x2, c_im, cib, ALU.mult)
                V.tt(x3, c_im, crb, ALU.mult)
                V.tt(c_re, c_re, crb, ALU.mult)
                V.tt(c_re, c_re, x2, ALU.subtract)
                tC = V.tt(c_im, x1, x3, ALU.add)
                tout = None
                for q in range(4):
                    for i in range(4):
                        V.ts(AG[:, i, :], trow, ph[:, q * 4 + i:q * 4 + i + 1], None, ALU.mult, w=[tcst, A.last])
                    t = reduce2pi(AG, AG, KF)
                    tsc = sincos(SN, CS_, AG, KF, [t])
                    yield
                    for part, dst in ((0, BR), (1, BI)):
                        for j in (0, 2):
                            b, p = bank()
                            for i in range(2):
                                tk = PE.mm(p[:, i * 256:(i + 1) * 256], sB[:, part, q * 4 + j + i, :], U5[:, q, :],
                                           True, True, [cB.tok, tu], inc=(i == 1))
                            tb = A.cp(dst[:, j:j + 2, :], p2(p), [tk, tout])
                            rel(b, tb)
                    yield
                    V.tt(TA, BR, CS_, ALU.mult, [tb, tsc])
                    G.tt(TB, BI, CS_, ALU.mult, [tb, tsc, V.last])
                    V.tt(AG, BI, SN, ALU.mult)
                    G.tt(KF, BR, SN, ALU.mult)
                    V.tt(TA, TA, AG, ALU.add)
                    tg = G.tt(TB, TB, KF, ALU.subtract)
                    yield
                    for i in range(4):
                        r = bc(rho[:, q * 4 + i:q * 4 + i + 1], [128, 256])
                        V.scan(TA[:, i, :], r, TA[:, i, :], 0.0, ALU.mult, ALU.add)
                    for i in range(4):
                        r = bc(rho[:, q * 4 + i:q * 4 + i + 1], [128, 256])
                        V.scan(TB[:, i, :], r, TB[:, i, :], 0.0, ALU.mult, ALU.add, [tg])
                    yield
                    tv = V.last
                    G.tt(AG, TB, SN, ALU.mult, [tv])
                    V.tt(BR, TA, CS_, ALU.mult)
                    V.tt(BI, TA, SN, ALU.mult)
                    V.tt(KF, TB, CS_, ALU.mult)
                    tg = G.last
                    V.stt(BI, BI, -1.0, KF, ALU.mult, ALU.subtract)
                    V.tt(BR, BR, AG, ALU.subtract, [tg])
                    yield
                    b, p = bank()
                    for part, xx in ((0, BR), (1, BI)):
                        for m in range(4):
                            tk = PE.mm(p[32 * m:32 * m + 32, 0:256], sC[:, part, q * 4 + m, :], xx[:, m, :],
                                       part == 0, part == 1, [V.last, tC], inc=(part == 1 and m == 3))
                    tout = tk
                    rel(b, V.stt(Y5[:, q, :], U5[:, q, :], par("s5_d", q), p[:, 0:256], ALU.mult, ALU.add, [tk]))
                    yield
                cC.free(tk)
                cB.free(tk)
                c0 = math.sqrt(2.0 / math.pi)
                V.tt(TA, Y5, Y5, ALU.mult)
                V.ts(TA, TA, 0.044715 * c0, c0, ALU.mult, ALU.add)
                V.tt(TA, TA, Y5, ALU.mult)
                t = A.act(TA, TA, ACT.Tanh, [V.last])
                yield
                V.ts(TA, TA, 0.5, 0.5, ALU.mult, ALU.add, w=[t])
                s5_out.append(V.tt(Y5, Y5, TA, ALU.mult))

            s5_out = []
            sg, ag = s5(), attention()
            next(sg)
            weave(ag, sg)
            t = s5_out[0]
            glu = take("glu")
            for j in (0, 2):
                b, p, tk = proj_T(glu, [j * 128, j * 128 + 128], Y5, 4, [t])
                a = A.act(TB[:, j:j + 2, :], p2(p), ACT.Sigmoid, [tk])
                rel(b, a)
            glu.free(tk)
            t = V.tt(OT[:, 4:8, :], Y5, TB, ALU.mult, [a])
            out_proj(["odd_out0", "odd_out1"], OT, [t])

        def hyb(stg):
            phase()
            norm_T(f"g_{stg}")
            phase()
            cv, tcst = consts(stg + "_c")
            cosT, sinT, tri = cv[:, 0:256], cv[:, 256:512], cv[:, 512:768]
            dec = cv[:, 768:1792].rearrange("p (h n) -> p h n", h=4)
            o = 1792
            cw, cb_ = cv[:, o:o + 96], cv[:, o + 96:o + 120]
            dsk, nw = cv[:, o + 120:o + 136], cv[:, o + 136:o + 152]
            dtb, alog = cv[:, o + 152:o + 184], cv[:, o + 184:o + 216]
            YR, MG = buf(16, 256), buf(8, 256)
            base = ar["at"]
            for e in (V, A, PE):
                e.wait(tcst)
            T1, T2 = buf(2, 256), buf(2, 256)
            QRs, KRs, VTs, SGs = ([buf(2, n) for _ in range(2)] for n in (256, 256, 512, 512))
            Y, SQ = buf(4, 256), buf(4, 256)
            PTs = buf(384)
            RS = buf(256)
            SGM = buf(8, 256)

            def p2(p):
                return p.rearrange("p (a b) -> p a b", a=2)

            def rstd(w=()):
                t = V.tt(SQ, Y, Y, ALU.mult, w)
                yield
                b, p = bank()
                for i in range(4):
                    tk = PE.mm(p[:, 0:256], ones, SQ[:, i, :], i == 0, i == 3, [t], inc=(i == 3))
                rel(b, A.act(RS, p[:, 0:256], ACT.Ln, [tk, V.last], bias=par("eps6"), scale=1.0 / 512))
                return A.act(RS, RS, ACT.Exp, scale=-0.5)

            ret = {}

            def ret_in(h):
                QR, KR, VT = QRs[h % 2], KRs[h % 2], VTs[h % 2]
                SG = SGs[h % 2].rearrange("p a (b c) -> p (a b) c", b=2)
                before = ret.get(("end", h - 2), [])
                c = take(f"{stg}_qk{h}")
                for which, dst, sc in ((0, QR, 1.0), (1, KR, 1.0 / 16)):
                    b, p, tk = yield from proj_T_g(c, [which * 256, which * 256 + 128], HT, 8)
                    V.stt(T1, p2(p), sc, cosT.unsqueeze(1).broadcast_to([128, 2, 256]), ALU.mult, ALU.mult,
                          [tk, *before])
                    rel(b, V.stt(T2, p2(p), sc, sinT.unsqueeze(1).broadcast_to([128, 2, 256]), ALU.mult, ALU.mult))
                    V.tt(dst[:, 0, :], T1[:, 0, :], T2[:, 1, :], ALU.subtract)
                    ret["r", h] = V.tt(dst[:, 1, :], T2[:, 0, :], T1[:, 1, :], ALU.add)
                    if which:
                        c.free(tk)
                    yield
                c = take(f"{stg}_v{h}")
                for t in range(2):
                    b, p, tk = proj_tok(c, HT, 8, t, 0, 512)
                    ret["v", h] = A.cp(VT[:, t, :], p, [tk, *before])
                    rel(b, A.last)
                    if t:
                        c.free(tk)
                    yield
                c = take(f"{stg}_g{h}")
                for j in (0, 2):
                    b, p, tk = yield from proj_T_g(c, [j * 128, j * 128 + 128], HT, 8)
                    ret["g", h] = A.act(SG[:, j:j + 2, :], p2(p), ACT.Silu, [tk, *before])
                    rel(b, A.last)
                    if j:
                        c.free(tk)
                    yield

            def ret_do(h):
                QR, KR, VT = QRs[h % 2], KRs[h % 2], VTs[h % 2]
                SG = SGs[h % 2].rearrange("p a (b c) -> p (a b) c", b=2)
                b, p = bank()
                for i in range(2):
                    PE.mm(p[:, 0:256], KR[:, i, 0:128], QR[:, i, :], i == 0, i == 1, [ret["r", h]])
                for i in range(2):
                    tk = PE.mm(p[:, 256:384], KR[:, i, 128:256], QR[:, i, 128:256], i == 0, i == 1, inc=(i == 1))
                V.tt(PTs[:, 0:256], p[:, 0:256], dec[:, h, :], ALU.mult, [tk])
                tp = V.tt(PTs[:, 256:384], p[:, 256:384], dec[:, h, 0:128], ALU.mult)
                rel(b, tp)
                yield
                for j in (0, 2):
                    b, p = bank()
                    for i in range(2):
                        d = slice((j + i) * 128, (j + i + 1) * 128)
                        PE.mm(p[:, i * 256:(i + 1) * 256], VT[:, 0, d], PTs[:, 0:256], True, False, [tp, ret["v", h]])
                        tk = PE.mm(p[:, i * 256 + 128:(i + 1) * 256], VT[:, 1, d], PTs[:, 256:384], False, True,
                                   inc=(i == 1))
                    rel(b, A.cp(Y[:, j:j + 2, :], p2(p), [tk, V.last]))
                tr = yield from rstd([A.last, PE.last])
                V.tt(Y, Y, SG, ALU.mult, [ret["g", h]])
                V.tt(YR[:, 4 * h:4 * h + 4, :], Y, RS.unsqueeze(1).broadcast_to([128, 4, 256]), ALU.mult, [tr])
                ret["end", h] = [V.last, PE.last]
                yield

            def gates(gn, dst, w=()):
                for i in range(2):
                    c = take(f"{stg}_{gn}{i}")
                    for j in (0, 2):
                        b, p, tk = yield from proj_T_g(c, [j * 128, j * 128 + 128], HT, 8)
                        ret["gate"] = A.act(dst[:, i * 4 + j:i * 4 + j + 2, :], p2(p), ACT.Sigmoid, [tk, *w])
                        rel(b, A.last)
                        if j:
                            c.free(tk)
                        yield

            def merge(on, SGM, first):
                ty = V.last
                for i in range(4):
                    c = take(f"{stg}_{on}{i}")
                    b, p, tk = proj_T(c, [0, 128], YR, 16, [ty])
                    c.free(tk)
                    sl = slice(2 * i, 2 * i + 2)
                    if first:
                        rel(b, V.tt(MG[:, sl, :], p2(p), SGM[:, sl, :], ALU.mult, [tk, ret["gate"]]))
                    else:
                        rel(b, V.tt(SGM[:, sl, :], p2(p), SGM[:, sl, :], ALU.mult, [tk, ret["gate"]]))
                        V.tt(MG[:, sl, :], MG[:, sl, :], SGM[:, sl, :], ALU.add)

            weave(ret_in(0))
            for h in range(3):
                weave(ret_in(h + 1), ret_do(h))
            weave(gates("gr", SGM), ret_do(3))
            merge("ro", SGM, True)
            fence()
            ar["at"] = base
            UB = buf(6, 259)
            CVs = [buf(6, 256) for _ in range(2)]
            XD = buf(2, 512)
            ZSs = [buf(4, 256) for _ in range(2)]
            Y, SQ = buf(4, 256), buf(4, 256)
            CB = buf(384)
            SE = [buf(2, 384) for _ in range(2)]
            RS = buf(256)
            DTP, LA, NA_ = buf(2, 32), buf(2, 32), buf(2, 32)
            E1, E2, AE = buf(2, 32), buf(2, 32), buf(32)
            SGM = AR[:, base:base + 2048].rearrange("p (a b) -> p a b", a=8)

            def dt_in():
                c = take(f"{stg}_dt")
                for t in range(2):
                    b, p, tk = proj_tok(c, HT, 8, t, 0, 32)
                    rel(b, V.tt(DTP[:, t, :], p[:, 0:32], dtb, ALU.add, [tk]))
                c.free(tk)
                V.stt(E1, DTP, -1.0, DTP, ALU.mult, ALU.max)
                A.act(E1, E1, ACT.Exp, [V.last], scale=-1.0)
                A.act(AE, alog, ACT.Exp)
                t = A.act(E1, E1, ACT.Ln, bias=par("one"))
                V.ts(E2, DTP, 0.0, None, ALU.max)
                V.tt(DTP, E1, E2, ALU.add, [t])
                t = V.stt(LA, DTP, -1.0, AE.unsqueeze(1).broadcast_to([128, 2, 32]), ALU.mult, ALU.mult)
                V.set(UB[:, :, 0:3], 0.0)
                yield
                b, p = bank()
                PE.mm(p[:, 0:32], tri[:, 0:128], LA[:, 0, :], True, True, [t])
                PE.mm(p[:, 32:64], tri[:, 128:256], LA[:, 0, :], True, False)
                tk = PE.mm(p[:, 32:64], tri[:, 0:128], LA[:, 1, :], False, True, inc=True)
                rel(b, V.ts(NA_, p[:, 0:64].rearrange("p (a b) -> p a b", a=2), -1.0, None, ALU.mult, w=[tk]))
                yield

            def ssd_in(g):
                CV, ZS = CVs[g % 2], ZSs[g % 2]
                before = ret.get(("send", g - 2), [])
                tiles = [4 * g, 4 * g + 1, 4 * g + 2, 4 * g + 3, 16 + g, 20 + g]
                c = take(f"{stg}_xs{g}")
                for n, c0 in enumerate((0, 256, 0)):
                    if n == 2:
                        c = take(f"{stg}_bc{g}")
                    b, p, tk = yield from proj_T_g(c, [c0, c0 + 128], HT, 8)
                    rel(b, A.cp(UB[:, 2 * n:2 * n + 2, 3:259], p2(p), [tk, *before, ret.get("conv")]))
                    ta = A.last
                    if n:
                        c.free(tk)
                    if n == 0:
                        V.wait(*before)
                    for m in (2 * n, 2 * n + 1):
                        f = tiles[m]
                        V.ts(CV[:, m, :], UB[:, m, 0:256], cw[:, 4 * f:4 * f + 1], cb_[:, f:f + 1], ALU.mult, ALU.add,
                             w=[ta])
                        for i in range(1, 4):
                            V.stt(CV[:, m, :], UB[:, m, i:i + 256], cw[:, 4 * f + i:4 * f + i + 1], CV[:, m, :],
                                  ALU.mult, ALU.add)
                    ret["conv"] = V.last
                    yield
                c = take(f"{stg}_z{g}")
                for j in (0, 2):
                    b, p, tk = yield from proj_T_g(c, [j * 128, j * 128 + 128], HT, 8)
                    ret["z", g] = A.act(ZS[:, j:j + 2, :], p2(p), ACT.Silu, [tk, *before])
                    rel(b, A.last)
                    if j:
                        c.free(tk)
                    else:
                        ret["cv", g] = A.act(CV, CV, ACT.Silu, [ret["conv"]])
                    yield

            def ssd_do(g):
                CV, ZS = CVs[g % 2], ZSs[g % 2]
                acs = {}

                def cum(hp):
                    b, p = bank()
                    for i in range(2):
                        hh = 8 * g + 2 * hp + i
                        PE.mm(p[:, i * 256:(i + 1) * 256], LA[:, 0, hh:hh + 1].broadcast_to([128, 128]), tri, True, False)
                        tk = PE.mm(p[:, i * 256 + 128:(i + 1) * 256], LA[:, 1, hh:hh + 1].broadcast_to([128, 128]),
                                   tri[:, 0:128], False, True, inc=(i == 1))
                    se = SE[hp % 2]
                    for i in range(2):
                        hh = 8 * g + 2 * hp + i
                        V.ts(se[:, i, 0:256], p[:, i * 256:(i + 1) * 256], NA_[:, 0, hh:hh + 1], 0.0, ALU.add, ALU.min,
                             w=[tk, ret.get(("se", hp % 2))])
                        e = V.ts(se[:, i, 256:384], p[:, i * 256 + 128:(i + 1) * 256], NA_[:, 1, hh:hh + 1], 0.0,
                                 ALU.add, ALU.min)
                    rel(b, e)
                    acs[hp] = A.act(se, se, ACT.Exp, [e])

                cum(0)
                for t in range(2):
                    b, p = bank()
                    for i in range(4):
                        tk = PE.tr(p[:, i * 128:(i + 1) * 128], CV[:, i, t * 128:(t + 1) * 128], ident, [ret["cv", g]],
                                   inc=(i == 3))
                    txd = V.tt(XD[:, t, :].rearrange("p (h n) -> p h n", h=8), p.rearrange("p (h n) -> p h n", h=8),
                               DTP[:, t, 8 * g:8 * g + 8].unsqueeze(2).broadcast_to([128, 8, 64]), ALU.mult, [tk])
                    rel(b, txd)
                b, p = bank()
                PE.mm(p[:, 0:256], CV[:, 4, 0:128], CV[:, 5, :], True, True)
                tk = PE.mm(p[:, 256:384], CV[:, 4, 128:256], CV[:, 5, 128:256], True, True, inc=True)
                V.tt(CB[:, 0:256], p[:, 0:256], tri, ALU.mult, [tk])
                rel(b, V.tt(CB[:, 256:384], p[:, 256:384], tri[:, 0:128], ALU.mult))
                yield
                for hp in range(4):
                    if hp < 3:
                        cum(hp + 1)
                    se = SE[hp % 2]
                    t = V.tt(se, se, CB.unsqueeze(1).broadcast_to([128, 2, 384]), ALU.mult, [acs[hp]])
                    yield
                    b, p = bank()
                    for i in range(2):
                        xc = slice((2 * hp + i) * 64, (2 * hp + i + 1) * 64)
                        o2 = p[i * 64:(i + 1) * 64, :]
                        PE.mm(o2[:, 0:256], XD[:, 0, xc], se[:, i, 0:256], True, False, [t])
                        tk = PE.mm(o2[:, 128:256], XD[:, 1, xc], se[:, i, 256:384], False, True, inc=(i == 1))
                    ret["se", hp % 2] = tk
                    rel(b, V.stt(Y[:, hp, :], CV[:, hp, :], dsk[:, 4 * g + hp:4 * g + hp + 1], p[:, 0:256],
                                 ALU.mult, ALU.add, [tk]))
                V.tt(Y, Y, ZS, ALU.mult, [ret["z", g]])
                tr = yield from rstd([PE.last])
                V.tt(Y, Y, RS.unsqueeze(1).broadcast_to([128, 4, 256]), ALU.mult, [tr])
                for i in range(4):
                    V.ts(YR[:, 4 * g + i, :], Y[:, i, :], nw[:, 4 * g + i:4 * g + i + 1], None, ALU.mult)
                ret["send", g] = [V.last, PE.last]
                yield

            weave(dt_in())
            weave(ssd_in(0))
            for g in range(3):
                weave(ssd_in(g + 1), ssd_do(g))
            weave(gates("gs", SGM, [ret["conv"], *ret["send", 2]]), ssd_do(3))
            merge("so", SGM, False)
            out_proj([f"{stg}_wo0", f"{stg}_wo1"], MG, [V.last])

        def ffn(stg):
            phase()
            nxt = stages[stages.index(stg) + 1:][:1]
            if nxt and nxt[0] + "_c" in coffs:
                consts(nxt[0] + "_c")
            norm_T(f"g_{stg}")
            hd = [V.last, A.last]
            H = buf(22, 256)
            SG = [buf(2, 256) for _ in range(2)]
            ht = []
            for i in range(11):
                c = take(f"{stg}_gu{i}")
                b, p, tk = proj_T(c, [0, 128], HT, 8, hd)
                b2, pu, tk2 = proj_T(c, [256, 384], HT, 8)
                c.free(tk2)
                sg = SG[i % 2]
                a = A.act(sg, p.rearrange("p (a b) -> p a b", a=2), ACT.Silu, [tk, ht[i - 2] if i > 1 else None])
                rel(b, a)
                v = V.tt(H[:, 2 * i:2 * i + 2, :], pu.rearrange("p (a b) -> p a b", a=2), sg, ALU.mult, [tk2, a])
                ht.append(v)
                rel(b2, v)
            acc = {(t, n): bank() for t in range(2) for n in range(2)}
            for i in range(6):
                c = take(f"{stg}_dn{i}")
                K = 4 if i < 5 else 2
                for t in range(2):
                    for n in range(2):
                        for k in range(K):
                            last = i == 5 and k == K - 1
                            tk = PE.mm(acc[t, n][1], H[:, 4 * i + k, t * 128:(t + 1) * 128],
                                       c.ap[:, k, n * 512:(n + 1) * 512], i == 0 and k == 0, last,
                                       [c.tok, ht[2 * i], ht[min(2 * i + 1, 10)]], inc=(k == K - 1))
                        if i == 5:
                            xs = X[:, t, n * 512:(n + 1) * 512]
                            rel(acc[t, n][0], V.tt(xs, acc[t, n][1], xs, ALU.add, [tk]))
                c.free(tk)

        def fin():
            phase()
            c = take("fin_w")
            sq, ss = buf(2, 1024), buf(4)
            for t in range(2):
                V.stt(sq[:, t, :], X[:, t, :], 1.0, X[:, t, :], ALU.mult, ALU.mult, accum=ss[:, t:t + 1])
            A.act(ss[:, 2:4], ss[:, 0:2], ACT.Ln, [V.last], bias=par("eps6"), scale=1.0 / 1024)
            t2 = A.act(ss[:, 0:2], ss[:, 2:4], ACT.Exp, scale=-0.5)
            for t in range(2):
                V.stt(X[:, t, :], X[:, t, :], ss[:, t:t + 1], c.ap[:, 0, :], ALU.mult, ALU.mult, [t2, c.tok])

        for s in stages:
            if s == "even":
                even()
            elif s in ("moe0", "moe1"):
                moe(s, int(s[-1]))
            elif s == "odd":
                odd_start = st["take"]
                odd()
            elif s.startswith("hyb"):
                hyb(s)
            elif s.startswith("ffn"):
                ffn(s)
            else:
                fin()
        SP.dma(out_d.rearrange("(t p) d -> p t d", p=128), X, s_out, [V.last])
        SP.wait((s_out, 16))

        block = ctx.enter_context(nc.Block())

        @block.sync
        def _(eng):
            SP.emit(eng)

        @block.scalar
        def _(eng):
            A.emit(eng)

        @block.vector
        def _(eng):
            V.emit(eng)

        @block.gpsimd
        def _(eng):
            G.emit(eng)

        @block.tensor
        def _(eng):
            PE.emit(eng)


def rows(w):
    return w.reshape(-1, 128, w.shape[1]).transpose(1, 0, 2)


def cols(v):
    return v.reshape(-1, 128).T


def brow(v):
    return np.broadcast_to(v.reshape(1, -1), (128, v.size))


def pack_chunk(name, inp):
    f = np.float32
    if name == "even_c":
        o = np.zeros((128, 1184), f)
        h, r = np.arange(128) // 64, np.arange(128) % 64
        same = h[:, None] == h[None, :]
        R, Cc = r[:, None], r[None, :]
        blk = (R // 16) == (Cc // 16)
        o[:, 0:128] = same
        o[:, 128:256] = same & (R < Cc) & blk
        o[:, 256:384] = same & (Cc < R) & blk
        o[:, 384:512] = same & (Cc < R) & ~blk
        o[:, 512:640] = same & (R < Cc)
        o[:, 640:704] = R <= np.arange(64)[None, :]
        o[:, 704:768] = R == np.arange(64)[None, :]
        for g, w in enumerate((2, 4, 8, 16)):
            o[:, 1088 + 16 * g:1104 + 16 * g] = w / np.minimum(np.arange(1, 17), w)
        o[:, 1152] = 1.0
        return o
    if name.startswith("even_in"):
        i = int(name[-1])
        return rows(inp["even_w_in"][0][:, i * 512:min((i + 1) * 512, 2304)])
    if name == "lora":
        o = np.zeros((128, 3, 512), f)
        o[0:64, 0] = inp["rw_w2"][0]
        o[64:128, 0] = inp["rw_a2"][0]
        o[:, 1] = inp["rw_g2"][0]
        o[:, 2] = inp["pool_w"][0].transpose(1, 0, 2).reshape(128, 512)
        return o
    if name.startswith("even_out"):
        i = int(name[-1])
        return rows(inp["even_w_out"][0][:, i * 512:(i + 1) * 512])
    if name.startswith("moe"):
        l = int(name[3])
        if name.endswith("_r"):
            return rows(np.concatenate([inp["moe_w_group"][l], inp["moe_w_expert"][l]], axis=1))
        q, c = (int(v) for v in name[6:].split("_"))
        w = inp[{"g": "moe_w_gate", "u": "moe_w_up", "d": "moe_w_down"}[name[5]]][l, 4 * q:4 * q + 4]
        if name[5] == "d":
            return w[:, c * 128:(c + 1) * 128].transpose(1, 0, 2)
        return w[:, c * 256:(c + 1) * 256].reshape(4, 2, 128, 512).transpose(2, 1, 0, 3)
    if name == "odd_c":
        o = np.zeros((128, 1152), f)
        inv = (10000.0 ** (-np.arange(0, 64, 2, dtype=f) / f(64))).astype(f)
        ang = np.arange(T, dtype=f)[None, :] * inv[np.arange(128) % 32][:, None]
        o[:, 0:256] = np.cos(ang)
        o[:, 256:512] = np.sin(ang)
        q = np.arange(128)
        o[:, 640:768] = np.where(q[:, None] >= q[None, :], 0.0, -1e30)
        for m in range(128):
            d = m % 64
            if d < 32:
                o[m + 32, 768 + m] = -1.0
            else:
                o[m - 32, 768 + m] = 1.0
        o[:, 896:1152] = np.arange(256)
        return o
    if name.startswith("odd_in"):
        i = int(name[-1])
        return rows(inp["odd_w_in"][0][:, i * 512:(i + 1) * 512])
    if name.startswith("odd_out"):
        i = int(name[-1])
        return rows(inp["odd_w_out"][0][:, i * 512:(i + 1) * 512])
    if name in ("s5_B", "s5_C"):
        o = np.zeros((128, 2, 16, 128 if name == "s5_B" else 32), f)
        for r, part in enumerate(("re", "im")):
            m = inp[("s5_b_" if name == "s5_B" else "s5_c_") + part][0]
            for g in range(32):
                i, gg = g // 2, g % 2
                ch, s = 16 * gg, 64 * gg
                if name == "s5_B":
                    ch += 32 * (i % 4)
                    o[ch:ch + 16, r, i, s:s + 64] = m[g].T
                else:
                    o[s:s + 64, r, i, ch:ch + 16] = m[g].T
        return o
    if name == "glu":
        return rows(inp["s5_w_glu"][0])
    if name.startswith("hyb"):
        l, key = int(name[3]), name[5:]
        w = inp["w_in_2"][l]
        if key == "c":
            o = np.zeros((128, 2008), f)
            inv = (10000.0 ** (-np.arange(128, dtype=f) / f(128))).astype(f)
            ang = np.arange(T, dtype=f)[None, :] * inv[:, None]
            o[:, 0:256] = np.cos(ang)
            o[:, 256:512] = np.sin(ang)
            j, i = np.arange(128)[:, None], np.arange(256)[None, :]
            o[:, 512:768] = j <= i
            for h in range(4):
                lg = math.log(1.0 - 2.0 ** (-5.0 - h))
                o[:, 768 + 256 * h:1024 + 256 * h] = np.where(j <= i, np.exp(lg * np.maximum(i - j, 0)), 0.0)
            at = 1792
            o[:, at:at + 96] = inp["conv_w_2"][l].reshape(4, 24, 128).transpose(2, 1, 0).reshape(128, 96)
            o[:, at + 96:at + 120] = cols(inp["conv_b_2"][l])
            o[:, at + 120:at + 136] = cols(np.repeat(inp["d_skip_2"][l], 64))
            o[:, at + 136:at + 152] = cols(inp["ssd_norm_w_2"][l])
            o[:, at + 152:at + 184] = brow(inp["dt_bias_2"][l])
            o[:, at + 184:at + 216] = brow(inp["a_log_2"][l])
            return o
        if key == "dt":
            return rows(w[:, 11264:11296])
        n = int(key[-1])
        k = key[:-1]
        if k == "qk":
            return rows(np.concatenate([w[:, n * 256:(n + 1) * 256], w[:, 1024 + n * 256:1024 + (n + 1) * 256]], 1))
        if k == "bc":
            return rows(np.concatenate([w[:, 10240 + n * 128:10368 + n * 128], w[:, 10752 + n * 128:10880 + n * 128]], 1))
        starts = {"v": 2048, "g": 4096, "z": 6144, "xs": 8192, "gr": 11296, "gs": 12320}
        if k in starts:
            a = starts[k] + n * 512
            return rows(w[:, a:a + 512])
        if k == "ro":
            return rows(inp["ret_out_2"][l][:, n * 256:(n + 1) * 256])
        if k == "so":
            return rows(inp["ssd_out_2"][l][:, n * 256:(n + 1) * 256])
        return rows(inp["w_o_2"][l][:, n * 512:(n + 1) * 512])
    if name.startswith("ffn"):
        l, key = int(name[3]), name[5:]
        if key.startswith("gu"):
            n = int(key[2:])
            w = inp["w_gate_up_2"][l]
            return rows(np.concatenate([w[:, n * 256:(n + 1) * 256], w[:, 2816 + n * 256:2816 + (n + 1) * 256]], 1))
        n = int(key[2:])
        return rows(inp["w_down_2"][l][n * 512:min((n + 1) * 512, 2816)])
    return brow(inp["final_norm_w_2"])


def pack_params(inp):
    o = np.zeros((128, NP), np.float32)

    def put(name, v):
        at, n = PT[name]
        o[:, at:at + n] = v

    for l in range(2):
        put(("g_even", "g_odd")[l], cols(inp["norm_mix_g"][l]))
        put(f"g_moe{l}", cols(inp["norm_ffn_g"][l]))
        put(f"g_hyb{l}", cols(inp["norm_mix_w_2"][l]))
        put(f"g_ffn{l}", cols(inp["norm_ffn_w_2"][l]))
        put(f"rb{l}", brow(np.concatenate([inp["moe_b_group"][l], inp["moe_b_expert"][l]])))
    for name, key in (("mu", "rw_mu"), ("w0", "rw_w0"), ("a0", "rw_a0"), ("k_k", "rw_k_k"), ("k_a", "rw_k_a"),
                      ("r_k", "rw_r_k"), ("ln_g", "rw_ln_g"), ("ln_b", "rw_ln_b"), ("pool_scale", "pool_scale"),
                      ("s5_d", "s5_d"), ("subln", "da_subln")):
        put(name, cols(inp[key][0].reshape(-1)))
    put("qn", cols(np.concatenate([inp["da_q_norm"][0]] * 2)))
    put("kn", cols(np.concatenate([inp["da_k_norm"][0]] * 2)))
    for name, key in (("s5_re", "s5_a_re"), ("s5_im", "s5_a_im"), ("s5_ls", "s5_log_step")):
        put(name, cols(inp[key][0].reshape(-1)))
    put("lam", brow(np.concatenate([inp[f"da_lam_{k}"][0] for k in ("q1", "k1", "q2", "k2")])))
    put("eps6", 1e-6)
    put("eps5", 1e-5)
    put("epsln", 64e-5)
    put("one", 1.0)
    put("hpi", math.pi / 2)
    put("ident", np.eye(128))
    put("ones", 1.0)
    r = np.arange(128)
    put("tri", r[:, None] <= r[None, :])
    put("iota", np.arange(32))
    r = np.arange(128) // 64
    put("ones64", r[:, None] == r[None, :])
    return o


def kernel(**inputs):
    import numpy as _np
    import concourse.bacc as _bacc
    from concourse import mybir as _mybir
    from concourse.bass_utils import run_bass_kernel_spmd as _run

    inputs = {k: _np.asarray(v) for k, v in inputs.items()}
    table = chunk_table(STAGES) + [(name, 1, n) for name, n in const_table(STAGES)]
    W = _np.empty((sum(128 * k * n for _, k, n in table),), _np.float32)
    at = 0
    for name, k, n in table:
        size = 128 * k * n
        W[at:at + size].reshape(128, k, n)[...] = pack_chunk(name, inputs).reshape(128, k, n)
        at += size
    arrays = {"w_dram": W, "p_dram": pack_params(inputs), "x_dram": _np.ascontiguousarray(inputs["x"][0])}
    nc = _bacc.Bacc("TRN2", target_bir_lowering=False, num_devices=1)
    args = [nc.dram_tensor(k, a.shape, _mybir.dt.float32, kind="ExternalInput").ap() for k, a in arrays.items()]
    out = nc.dram_tensor("out_dram", (T, 1024), _mybir.dt.float32, kind="ExternalOutput").ap()
    program(nc, args[0], args[1], args[2], out, STAGES)
    r = _run(nc, [arrays], core_ids=[0])
    return r.results[0]["out_dram"].reshape(1, T, 1024)
```

```python
import math
from contextlib import ExitStack

import numpy as np

import concourse.bass as bass
from concourse import mybir
from concourse.alu_op_type import AluOpType as ALU

F32 = mybir.dt.float32
F32R = mybir.dt.float32r
ACT = mybir.ActivationFunctionType
AX = mybir.AxisListType
T = 256
NSLOT = 6
FEW = 3
SLOT = 4096
NE = 32
STAGES = ["even", "moe0", "odd", "moe1", "hyb0", "ffn0", "hyb1", "ffn1", "fin"]

PCOLS = [
    ("g_even", 8), ("g_moe0", 8), ("g_odd", 8), ("g_moe1", 8), ("g_hyb0", 8), ("g_ffn0", 8),
    ("g_hyb1", 8), ("g_ffn1", 8), ("mu", 14), ("w0", 4), ("a0", 4), ("k_k", 4), ("k_a", 4),
    ("r_k", 4), ("ln_g", 4), ("ln_b", 4), ("pool_scale", 4), ("qn", 1), ("kn", 1), ("subln", 1),
    ("s5_re", 16), ("s5_im", 16), ("s5_ls", 16), ("s5_d", 4), ("lam", 256), ("rb0", 36),
    ("rb1", 36), ("eps6", 1), ("eps5", 1), ("epsln", 1), ("one", 1), ("hpi", 1), ("ident", 128), ("ones", 128),
    ("ones64", 128), ("tri", 128), ("iota", 32),
]
CAP = 32
AHEAD = 2


def pcol_table():
    at, out = 0, {}
    for name, n in PCOLS:
        out[name] = (at, n)
        at += n
    return out, at


PT, NP = pcol_table()


def chunk_table(stages):
    out = []
    for st in stages:
        if st == "even":
            out += [(f"even_in{i}", 8, 512 if i < 4 else 256) for i in (3, 4)]
            out += [("lora", 3, 512)]
            out += [(f"even_in{i}", 8, 512) for i in (1, 0, 2)]
            out += [("even_out0", 8, 512), ("even_out1", 8, 512)]
        if st in ("moe0", "moe1"):
            out += [(st + "_r", 8, 36)]
            for q in range(NE // 4):
                out += [(f"{st}_g{q}_{c}", 8, 512) for c in range(4)]
                out += [(f"{st}_u{q}_{c}", 8, 512) for c in range(4)]
                out += [(f"{st}_d{q}_{c}", 4, 1024) for c in range(4)]
        if st == "odd":
            out += [("odd_in3", 8, 512), ("s5_C", 1, 1024), ("s5_B", 1, 4096)]
            out += [(f"odd_in{i}", 8, 512) for i in range(3)]
            out += [("glu", 4, 512)]
            out += [("odd_out0", 8, 512), ("odd_out1", 8, 512)]
        if st in ("hyb0", "hyb1"):
            for h in range(4):
                out += [(f"{st}_qk{h}", 8, 512), (f"{st}_v{h}", 8, 512), (f"{st}_g{h}", 8, 512)]
            out += [(f"{st}_gr{i}", 8, 512) for i in range(2)]
            out += [(f"{st}_ro{i}", 16, 256) for i in range(4)]
            out += [(f"{st}_dt", 8, 32)]
            for g in range(4):
                out += [(f"{st}_xs{g}", 8, 512), (f"{st}_bc{g}", 8, 256), (f"{st}_z{g}", 8, 512)]
            out += [(f"{st}_gs{i}", 8, 512) for i in range(2)]
            out += [(f"{st}_so{i}", 16, 256) for i in range(4)]
            out += [(f"{st}_wo{i}", 8, 512) for i in range(2)]
        if st in ("ffn0", "ffn1"):
            out += [(f"{st}_gu{i}", 8, 512) for i in range(11)]
            out += [(f"{st}_dn{i}", 4 if i < 5 else 2, 1024) for i in range(6)]
        if st == "fin":
            out += [("fin_w", 1, 1024)]
    return out


def const_table(stages):
    n = {"even": 1184, "odd": 1152, "hyb0": 2008, "hyb1": 2008}
    return [(s + "_c", n[s]) for s in stages if s in n]


class Eng:

    def __init__(self, name, sem):
        self.name, self.sem, self.n, self.q, self.seen = name, sem, 0, [], {}
        self.open = False

    def wait(self, *toks):
        for t in toks:
            if t is None:
                continue
            sem, v = t
            if v > self.seen.get(id(sem), 0):
                self.seen[id(sem)] = v
                self.q.append((0, sem, v))

    def op(self, fn, w=(), chain=True, inc=True):
        self.wait(*w)
        if chain:
            self.wait((self.sem, self.n))
        if inc:
            self.n += 1
        self.open = not inc
        self.q.append((1, fn, inc))
        return (self.sem, self.n)

    def dma(self, out, in_, sem, w=()):
        self.wait(*w)
        self.q.append((2, out, in_, sem))

    @property
    def last(self):
        assert not self.open, self.name
        return (self.sem, self.n)

    def branch(self, flag, least, sub):
        self.q.append((3, flag, least, sub))

    def emit(self, eng):
        for e in self.q:
            if e[0] == 3:
                with eng.If(eng.value_load(e[1], min_val=0, max_val=1 << 20) > e[2]):
                    e[3].emit(eng)
            elif e[0] == 0:
                eng.wait_ge(e[1], e[2])
            elif e[0] == 1:
                r = e[1](eng)
                if e[2]:
                    r.then_inc(self.sem, 1)
            else:
                eng.dma_start(e[1], e[2]).then_inc(e[3], 16)


class Vec(Eng):
    def tt(self, out, a, b, op, w=(), chain=True):
        return self.op(lambda e: e.tensor_tensor(out, a, b, op), w, chain)

    def ts(self, out, a, s1, s2, op0, op1=None, w=(), chain=True):
        if op1 is None:
            return self.op(lambda e: e.tensor_scalar(out, a, s1, None, op0), w, chain)
        return self.op(lambda e: e.tensor_scalar(out, a, s1, s2, op0, op1), w, chain)

    def stt(self, out, a, s, b, op0, op1, w=(), accum=None, chain=True):
        if accum is None:
            return self.op(lambda e: e.scalar_tensor_tensor(out=out, in0=a, scalar=s, in1=b, op0=op0, op1=op1), w,
                           chain)
        return self.op(lambda e: e.scalar_tensor_tensor(out=out, in0=a, scalar=s, in1=b, op0=op0, op1=op1,
                                                        accum_out=accum), w)

    def cp(self, out, a, w=(), chain=True):
        return self.op(lambda e: e.tensor_copy(out, a), w, chain)

    def set(self, out, v, w=(), chain=True):
        return self.op(lambda e: e.memset(out, v), w, chain)

    def scan(self, out, d0, d1, init, op0, op1, w=(), chain=True):
        return self.op(lambda e: e.tensor_tensor_scan(out, d0, d1, init, op0, op1), w, chain)

    def red(self, out, a, op, w=(), chain=True):
        return self.op(lambda e: e.tensor_reduce(out, a, AX.X, op), w, chain)

    def rcp(self, out, a, w=(), chain=True):
        return self.op(lambda e: e.reciprocal(out, a), w, chain)


class Sca(Eng):
    def act(self, out, a, f, w=(), bias=0.0, scale=1.0, chain=True):
        return self.op(lambda e: e.activation(out, a, f, bias=bias, scale=scale), w, chain)

    def cp(self, out, a, w=(), chain=True):
        return self.op(lambda e: e.activation(out, a, ACT.Copy), w, chain)


class Ten(Eng):
    def mm(self, out, l, r, start, stop, w=(), inc=False):
        return self.op(lambda e: e.matmul(out, l, r, start=start, stop=stop), w, chain=False, inc=inc)

    def tr(self, out, a, ident, w=(), inc=False):
        return self.op(lambda e: e.transpose(out, a, ident), w, chain=False, inc=inc)


def program(nc, Wd, Pd, x_in, out_d, stages):
    ctx = ExitStack()
    with ctx:
        def sb(name, n):
            return ctx.enter_context(nc.sbuf_tensor(name, [128, n], F32))

        def sem(name):
            return ctx.enter_context(nc.semaphore(name))

        X = sb("x", 2048)[:, :].rearrange("p (t d) -> p t d", t=2)
        PP = sb("pp", NP)
        GS = sb("gs", 128)
        CS_T = sb("cst", 2008)
        FLAG = ctx.enter_context(nc.sbuf_tensor("flag", [128, 2], mybir.dt.int32))
        NA = 20992
        with nc.sbuf_tensor("arena", [128, NA], F32) as arena:
            AR = arena[:, :]
        AR32 = ctx.enter_context(nc.sbuf_tensor("arena32", [128, NA], F32R))
        ring = sb("ring", FEW * SLOT)
        with nc.sbuf_tensor("ring2", [128, (NSLOT - FEW) * SLOT + 2048], F32) as ring2:
            HT = ring2[:, (NSLOT - FEW) * SLOT:].rearrange("p (k t) -> p k t", k=8)
        R32 = ctx.enter_context(nc.sbuf_tensor("r32", [128, 12288], F32R))
        TMP = sb("tmp", 2048)
        HH, HL = (R32[:, i * 2048:(i + 1) * 2048].rearrange("p (k t) -> p k t", k=8) for i in range(2))
        WS = [[R32[:, i:i + 2048].rearrange("p (k n) -> p k n", k=8) for i in (j, j + 2048)]
              for j in (4096, 8192)]
        ps = ctx.enter_context(nc.psum_tensor("ps", [128, 8, 512], F32))

        V = Vec("v", sem("s_v"))
        A = Sca("a", sem("s_a"))
        PE = Ten("pe", sem("s_pe"))
        SP = Eng("sp", sem("s_sp"))
        s_slot = [sem(f"s_slot{i}") for i in range(NSLOT)]
        s_in = sem("s_in")
        s_over = [[sem(f"s_over{l}{n}") for n in ("v", "a", "pe", "dma")] for l in range(2)]
        s_const = sem("s_const")
        G = Vec("g", sem("s_g"))
        s_out = sem("s_out")

        def par(name, i=0, n=1):
            at = PT[name][0]
            return PP[:, at + i:at + i + n]

        ident, ones, ones64 = par("ident", 0, 128), par("ones", 0, 128), par("ones64", 0, 128)

        chunks = chunk_table(stages)
        offs, at = [], 0
        for _, k, n in chunks:
            offs.append(at)
            at += 128 * k * n
        st = {"take": 0, "sent": 0, "split": 0}
        freed = {}
        split_from = len(chunks)
        for i, (name, _, _) in reversed(list(enumerate(chunks))):
            if name[:3] in ("hyb", "ffn"):
                split_from = i
        slot_of, prev, nth, held = [], [], [], {}
        for i in range(len(chunks)):
            s = i % NSLOT if i < split_from else (i - split_from) % FEW
            slot_of.append(s)
            prev.append(held.get(s, (-1, 0))[0])
            nth.append(held.get(s, (-1, 0))[1] + 1)
            held[s] = (i, nth[-1])

        def slot_ap(i):
            _, k, n = chunks[i]
            s = slot_of[i]
            r, at = (ring, s) if s < FEW else (ring2, s - FEW)
            return r[:, at * SLOT:at * SLOT + k * n]

        coffs, cn = {}, at
        for name, n in const_table(stages):
            coffs[name] = (cn, n)
            cn += 128 * n

        def consts(name):
            o, n = coffs[name]
            if st.get("cname") == name:
                return CS_T[:, 0:n], (s_const, 16 * st["consts"])
            st["cname"] = name
            st["consts"] = st.get("consts", 0) + 1
            G.dma(CS_T[:, 0:n], Wd[o:o + 128 * n].rearrange("(p n) -> p n", p=128), s_const,
                  [V.last, A.last, PE.last])
            return CS_T[:, 0:n], (s_const, 16 * st["consts"])

        def send(w=()):
            i = st["sent"]
            _, k, n = chunks[i]
            SP.dma(slot_ap(i), Wd[offs[i]:offs[i] + 128 * k * n].rearrange("(p n) -> p n", p=128),
                   s_slot[slot_of[i]], w)
            st["sent"] += 1

        def sends():
            while st["sent"] < len(chunks) and (prev[st["sent"]] < 0 or prev[st["sent"]] in freed):
                send(freed.get(prev[st["sent"]], ()))

        class Chunk:
            def __init__(self, i):
                self.i = i
                self.ap = slot_ap(i).rearrange("p (k n) -> p k n", k=chunks[i][1])
                self.tok = (s_slot[slot_of[i]], 16 * nth[i])

            def free(self, *toks):
                freed[self.i] = toks
                sends()

        def take(name):
            i = st["take"]
            assert chunks[i][0] == name, (chunks[i], name)
            st["take"] += 1
            return Chunk(i)

        SP.dma(PP[:, :], Pd, s_in)
        SP.dma(X, x_in.rearrange("(t p) d -> p t d", p=128), s_in)
        sends()
        tin = (s_in, 32)
        for e in (V, A, PE):
            e.wait(tin)

        free_banks = [(b, ()) for b in range(8)]

        def bank():
            b, toks = free_banks.pop(0)
            PE.wait(*toks)
            return b, ps[:, b, :]

        def rel(b, *toks):
            free_banks.append((b, toks))

        ar = {"at": 0}

        def buf(*shape, of=AR):
            n = int(np.prod(shape))
            a = ar["at"]
            ar["at"] += n
            assert ar["at"] <= NA, ar["at"]
            v = of[:, a:a + n]
            if len(shape) == 2:
                return v.rearrange("p (a b) -> p a b", a=shape[0])
            if len(shape) == 3:
                return v.rearrange("p (a b c) -> p a b c", a=shape[0], b=shape[1])
            return v

        def fence():
            toks = [V.last, A.last, PE.last, G.last]
            for e in (V, A, PE, G):
                e.wait(*toks)

        def phase():
            fence()
            ar["at"] = 0

        def bc(v, shape):
            return v.broadcast_to(list(shape))

        def weave(*parts):
            parts = list(parts)
            while parts:
                parts = [g for g in parts if next(g, 1) is None]

        def rstd_x():
            sq, ss = buf(2, 1024), buf(4)
            A.act(ss[:, 3:4], par("one"), ACT.Sqrt)
            v = V.stt(sq[:, 0, :], X[:, 0, :], 1.0, X[:, 0, :], ALU.mult, ALU.mult, accum=ss[:, 0:1])
            A.op(lambda e: e.activation(sq[:, 1, :], X[:, 1, :], ACT.Square, accum_out=ss[:, 1:2]), chain=False)
            t = A.act(ss[:, 2:4], ss[:, 0:2], ACT.Sqrt, [v], bias=par("eps6"), scale=1.0 / 1024)
            return ss, V.rcp(ss[:, 0:2], ss[:, 2:4], [t])

        def norm_T(gname):
            ss, t2 = rstd_x()
            xn = buf(2, 1024)
            tx = [V.ts(xn[:, 0, :], X[:, 0, :], ss[:, 0:1], None, ALU.mult, w=[t2]),
                  A.act(xn[:, 1, :], X[:, 1, :], ACT.Copy, [t2], scale=ss[:, 1:2])]
            for k in range(0, 8, 2):
                b, p = bank()
                for kk in (k, k + 1):
                    for t in range(2):
                        tp = PE.tr(p[:, (kk - k) * 256 + t * 128:(kk - k) * 256 + t * 128 + 128],
                                   xn[:, t, kk * 128:(kk + 1) * 128], ident, [tx[t]],
                                   inc=(kk == k + 1 and t == 1))
                if k % 4 == 0:
                    V.ts(HT[:, k, :], p[:, 0:256], par(gname, k), None, ALU.mult, w=[tp])
                    e0 = V.ts(HT[:, k + 1, :], p[:, 256:512], par(gname, k + 1), None, ALU.mult)
                    rel(b, e0)
                else:
                    A.act(HT[:, k, :], p[:, 0:256], ACT.Copy, [tp], scale=par(gname, k))
                    e1 = A.act(HT[:, k + 1, :], p[:, 256:512], ACT.Copy, scale=par(gname, k + 1))
                    rel(b, e1)
            return xn

        def norm_HL(gname):
            ss, t2 = rstd_x()
            xn = buf(2, 1024)
            tx = [V.ts(xn[:, 0, :], X[:, 0, :], ss[:, 0:1], None, ALU.mult, w=[t2]),
                  A.act(xn[:, 1, :], X[:, 1, :], ACT.Copy, [t2], scale=ss[:, 1:2])]
            cut_to(tile_at[st["take"]] + AHEAD)
            for k in range(0, 8, 2):
                b, p = bank()
                for t in range(2):
                    for kk in (k, k + 1):
                        tp = PE.tr(p[:, (kk - k) * 256 + t * 128:(kk - k) * 256 + t * 128 + 128],
                                   xn[:, t, kk * 128:(kk + 1) * 128], ident, [tx[t]],
                                   inc=(kk == k + 1 and t == 1))
                for kk in (k, k + 1):
                    q = p[:, (kk - k) * 256:(kk - k) * 256 + 256]
                    ta = A.act(HH[:, kk, :], q, ACT.Copy, [tp], scale=par(gname, kk))
                for kk in (k, k + 1):
                    q = p[:, (kk - k) * 256:(kk - k) * 256 + 256]
                    tv = V.stt(HL[:, kk, :], q, par(gname, kk), HH[:, kk, :].bitcast(F32), ALU.mult, ALU.subtract, [ta])
                rel(b, tv)

        def pair(hi, lo, v, w=()):
            ta = A.act(hi, v, ACT.Copy, [V.last, *w])
            return V.tt(lo, v, hi.bitcast(F32), ALU.subtract, [ta, *w])

        def pair_half(hi, lo, v):
            ta = A.act(hi, v, ACT.Copy, [V.last], scale=0.5)
            return V.stt(lo, v, 0.5, hi.bitcast(F32), ALU.mult, ALU.subtract, [ta])

        def silu2(out, v, w=()):
            ta = A.act(out, v, ACT.Tanh, w, scale=0.5)
            return V.stt(out, out, 1.0, v, ALU.add, ALU.mult, [ta])

        tiles, tile_at = [], {}
        for i, (name, k, n) in enumerate(chunks):
            if name[:3] not in ("hyb", "ffn"):
                continue
            tile_at[i] = len(tiles)
            key = name[5:7]
            if key in ("ro", "so"):
                cs = [(slice(0, 16), slice(c, c + 128)) for c in (0, 128)]
            elif key == "wo":
                cs = [(slice(c, c + 4), slice(0, 512)) for c in (0, 4)]
            elif key == "dn":
                cs = [(slice(c, c + 2), slice(0, 1024)) for c in range(0, k, 2)]
            else:
                cs = [(slice(0, 8), slice(c, min(c + 128, n))) for c in range(0, n, 128)]
            for m, (ks, cc) in enumerate(cs):
                tiles.append((i, ks, cc, m == len(cs) - 1))
                if key in ("ro", "so", "wo", "dn", "dt"):
                    tiles.append(None)
        used, cut = {}, {}

        def parts(j):
            hi, lo = WS[j // 2 % 2]
            c = j % 2 * 128
            return hi[:, :, c:c + 128], lo[:, :, c:c + 128]

        def whole(j, k):
            at = 4096 * (1 + j // 2 % 2)
            return [R32[:, at + o:at + o + 2048].rearrange("p (k n) -> p k n", k=k) for o in (0, 2048)]

        def cut_to(j):
            while st["split"] <= j and st["split"] < len(tiles):
                s = st["split"]
                if tiles[s] is not None:
                    i, ks, cc, last = tiles[s]
                    c = Chunk(i)
                    w = c.ap[:, ks, cc]
                    k, n = w.shape[1], w.shape[2]
                    hi, lo = whole(s, k) if k * n == 2048 else parts(s)
                    free = [used.get(s - 4), used.get(s - 3) if k * n == 2048 else None]
                    ta = A.act(hi[:, :, 0:n], w, ACT.Copy, [c.tok, *free], chain=False)
                    cut[s] = V.tt(lo[:, :, 0:n], w, hi[:, :, 0:n].bitcast(F32), ALU.subtract, [ta, c.tok, *free],
                                  chain=False)
                    if last:
                        c.free(ta, cut[s])
                st["split"] += 1

        def take_cut(name):
            c = take(name)
            return tile_at[c.i]

        def mm_cut(out, j):
            for tk in mm_cut_g(out, j):
                pass
            return used[j]

        def mm_cut_g(out, j):
            cut_to(j + AHEAD)
            hi, lo = parts(j)
            for k in range(8):
                PE.mm(out, hi[:, k, :], HH[:, k, :], k == 0, False, [cut[j]])
                PE.mm(out, hi[:, k, :], HL[:, k, :], False, False)
                tk = PE.mm(out, lo[:, k, :], HH[:, k, :], False, k == 7, inc=(k in (3, 7)))
                if k == 3:
                    yield
            used[j] = tk
            cut_to(j + AHEAD + 1)

        def proj_cut_g(j, todo=(), fine=False):
            b, p = bank()
            for n in range(2):
                out = p[:, n * 256:(n + 1) * 256]
                if fine:
                    for _ in mm_cut_g(out, j + n):
                        if todo:
                            todo.pop(0)()
                        yield
                else:
                    mm_cut(out, j + n)
                if todo:
                    todo.pop(0)()
                if not n:
                    yield
            return b, p, used[j + 1]

        def pair_cut(out, j, t, n=256):
            cut_to(j + 1 + AHEAD)
            hi, lo = WS[j // 2 % 2]
            ts_ = slice(t * 128, (t + 1) * 128)
            for k in range(8):
                PE.mm(out, HH[:, k, ts_], hi[:, k, 0:n], k == 0, False, [cut[j], cut.get(j + 1) if n > 128 else None])
                PE.mm(out, HL[:, k, ts_], hi[:, k, 0:n], False, False)
                tk = PE.mm(out, HH[:, k, ts_], lo[:, k, 0:n], False, k == 7, inc=(k == 7))
            used[j] = used[j + 1] = tk
            cut_to(j + AHEAD + 1)
            return tk

        def proj_T(c, cols, rhs, K, w=()):
            b, p = bank()
            for n, c0 in enumerate(cols):
                for k in range(K):
                    t = PE.mm(p[:, n * 256:(n + 1) * 256], c.ap[:, k, c0:c0 + 128], rhs[:, k, :],
                              k == 0, k == K - 1, [c.tok, *w], inc=(k == K - 1 and n == len(cols) - 1))
            return b, p, t

        def proj_T_g(c, cols, rhs, K, w=()):
            b, p = bank()
            for n, c0 in enumerate(cols):
                if n:
                    yield
                for k in range(K):
                    t = PE.mm(p[:, n * 256:(n + 1) * 256], c.ap[:, k, c0:c0 + 128], rhs[:, k, :],
                              k == 0, k == K - 1, [c.tok, *w], inc=(k == K - 1))
            return b, p, t

        def proj_tok(c, lhs, K, t, c0, n, w=(), p=None, start=True, stop=True, kl=0):
            if p is None:
                b, p = bank()
            else:
                b, p = p
            for k in range(K):
                tk = PE.mm(p[:, 0:n], lhs[:, kl + k, t * 128:(t + 1) * 128], c.ap[:, k, c0:c0 + n],
                           start and k == 0, stop and k == K - 1, [c.tok, *w], inc=(k == K - 1))
            return b, p, tk

        def out_proj(names, lhs, w):
            for i, name in enumerate(names):
                c = take(name)
                for t in range(2):
                    b, p, tk = proj_tok(c, lhs, 8, t, 0, 512, w)
                    xs = X[:, t, i * 512:(i + 1) * 512]
                    rel(b, V.tt(xs, p, xs, ALU.add, [tk], chain=False))
                c.free(tk)

        def even():
            phase()
            consts("even_c")
            norm_T("g_even")
            phase()
            M = buf(14, 256)
            LD, AA, GG, KK = (buf(4, 256) for _ in range(4))
            OT, YT = buf(8, 256), buf(4, 256)
            base = ar["at"]
            U = buf(18, 256)
            cv, tcst = consts("even_c")
            TMP, TM2 = buf(4, 256), buf(4, 256)
            R, K2, VV = M[:, 0:4, :], M[:, 4:8, :], M[:, 8:12, :]

            def p2(p):
                return p.rearrange("p (a b) -> p a b", a=2)

            def proj(i):
                c = take(f"even_in{i}")
                for j in range(0, 4 if i < 4 else 2, 2):
                    b, p, tk = proj_T(c, [j * 128, j * 128 + 128], HT, 8)
                    f = i * 4 + j
                    t = A.cp(U[:, f:f + 2, :], p2(p), [tk], chain=False)
                    rel(b, t)
                    if f < 14:
                        V.tt(M[:, f:f + 2, 1:256], U[:, f:f + 2, 0:255], U[:, f:f + 2, 1:256], ALU.subtract, [t], chain=False)
                        V.ts(M[:, f:f + 2, 0:1], U[:, f:f + 2, 0:1], -1.0, None, ALU.mult, chain=False)
                        for g in (f, f + 1):
                            tm = V.stt(M[:, g, :], M[:, g, :], par("mu", g), U[:, g, :], ALU.mult, ALU.add)
                        last_mix[0] = tm
                c.free(tk)

            last_mix = [None]

            def head_sums(src, w, out):
                for j in (0, 2):
                    b, p = bank()
                    for i in range(2):
                        t = PE.mm(p[:, i * 256:(i + 1) * 256], ones64, src[:, j + i, :], True, True, w, inc=(i == 1))
                    rel(b, out(j, p2(p), t))

            proj(3)
            tm = last_mix[0]
            ta = A.act(U[:, 0:1, :], M[:, 12:13, :], ACT.Tanh, [tm], chain=False)
            tg = A.act(U[:, 1:2, :], M[:, 13:14, :], ACT.Sigmoid, chain=False)
            proj(4)
            tpl = A.last
            lora = take("lora")
            proj(1)
            for j in range(0, 4, 2):
                bw, pw = bank()
                ba, pa = bank()
                bg, pg = bank()
                for i in range(2):
                    cs = slice((j + i) * 128, (j + i + 1) * 128)
                    o = slice(i * 256, (i + 1) * 256)
                    tw = PE.mm(pw[:, o], lora.ap[0:64, 0, cs], U[0:64, 0, :], True, True, [ta, lora.tok], inc=(i == 1))
                    tg2 = PE.mm(pg[:, o], lora.ap[:, 1, cs], U[:, 1, :], True, True, [tg], inc=(i == 1))
                for i in range(2):
                    cs = slice((j + i) * 128, (j + i + 1) * 128)
                    o = slice(i * 256, (i + 1) * 256)
                    tq = PE.mm(pa[:, o], lora.ap[64:128, 0, cs], M[64:128, 12, :], True, True, [tm], inc=(i == 1))
                for i in range(2):
                    o = slice(i * 256, (i + 1) * 256)
                    e1 = A.act(LD[:, j + i, :], pw[:, o], ACT.Sigmoid, [tw], bias=par("w0", j + i), chain=False)
                    e2 = A.act(AA[:, j + i, :], pa[:, o], ACT.Sigmoid, [tq], bias=par("a0", j + i), chain=False)
                e3 = A.cp(GG[:, j:j + 2, :], p2(pg), [tg2], chain=False)
                rel(bw, e1)
                rel(ba, e2)
                rel(bg, e3)
            tlora = PE.last
            for j in range(4):
                V.ts(KK[:, j, :], K2[:, j, :], par("k_k", j), None, ALU.mult)
            tk = V.tt(TMP, KK, KK, ALU.mult)
            V.ts(LD, LD, -math.exp(-0.5), None, ALU.mult, w=[e2], chain=False)
            proj(0)
            head_sums(TMP, [tk], lambda j, p, t: V.ts(TM2[:, j:j + 2, :], p, 1e-24, None, ALU.max, w=[t], chain=False))
            tsq = A.act(TM2, TM2, ACT.Sqrt, [V.last], chain=False)
            W0, W1, PD = YT, OT[:, 0:4, :], OT[:, 4:8, :]
            src, dst = U[:, 14:18, :], W0
            V.wait(tcst, tpl)
            for lv in range(4):
                s = 1 << lv
                V.tt(dst[:, lv:4, s:256], src[:, lv:4, s:256], src[:, lv:4, 0:256 - s], ALU.add, chain=False)
                V.cp(dst[:, lv:4, 0:s], src[:, lv:4, 0:s], chain=False)
                V.ts(PD[:, lv, :], dst[:, lv, :], 1.0 / (2 << lv), None, ALU.mult)
                src, dst = dst, (W1 if dst is W0 else W0)
            V.tt(PD[:, :, 0:16], PD[:, :, 0:16], cv[:, 1088:1152].rearrange("p (a b) -> p a b", a=4), ALU.mult)
            tpd = V.tt(PD, PD, U[:, 14:18, :], ALU.subtract)
            V.rcp(TM2, TM2, [tsq], chain=False)
            V.tt(KK, KK, TM2, ALU.mult)
            for j in range(4):
                V.ts(TMP[:, j, :], AA[:, j, :], 1.0, par("k_a", j), ALU.subtract, ALU.mult, w=[PE.last, e2], chain=False)
            V.stt(K2, TMP, 1.0, K2, ALU.add, ALU.mult)
            for j in range(4):
                tk = V.stt(TMP[:, j, :], R[:, j, :], par("r_k", j), K2[:, j, :], ALU.mult, ALU.mult)
            proj(2)
            for g in (0, 2):
                b, p = bank()
                for gg in range(2):
                    t = PE.mm(p[:, gg * 256:(gg + 1) * 256], lora.ap[:, 2, (g + gg) * 128:(g + gg + 1) * 128],
                              PD[:, g + gg, :], True, True, [tpd], inc=(gg == 1))
                for gg in range(2):
                    e = A.act(OT[:, 4 + g + gg, :], p[:, gg * 256:(gg + 1) * 256], ACT.Copy, [t],
                              scale=par("pool_scale", g + gg), chain=False)
                rel(b, e)
            lora.free(t, tlora)
            BON = OT[:, 0:4, :]
            head_sums(TMP, [tk], lambda j, p, t: V.tt(BON[:, j:j + 2, :], p, VV[:, j:j + 2, :], ALU.mult, [t]))
            fence()

            ar["at"] = base
            XX = buf(4, 128)
            xf = XX.rearrange("p c n -> p (c n)")
            CU, PI = xf[:, 0:256], xf[:, 256:512]
            PT_, PV = (buf(256) for _ in range(2))
            AHRH = buf(2, 256)
            ah, rh = AHRH[:, 0, :], AHRH[:, 1, :]
            bh_at = ar["at"]
            bh = buf(256)
            i2_at = ar["at"]
            I2 = buf(64)
            kh, bp, kp = (buf(256) for _ in range(3))
            BB = buf(14, 512)
            Bs = [BB[:, i, :] for i in range(14)]
            VS = buf(4, 64)
            LRB, LRK = (M[:, i, :].rearrange("p (c n) -> p c n", c=4) for i in (12, 13))
            BS, QS, CS, SS = (v.rearrange("p (c n) -> p c n", c=4) for v in (bp, PV, kp, bh))
            mB, mDT, mD, mO, mL = (cv[:, i * 128:(i + 1) * 128] for i in range(5))
            mR, i2 = cv[:, 640:704], cv[:, 704:768]
            ones1 = cv[:, 1152:1153]
            V.cp(I2, i2, chain=False)

            def c4(v):
                return v.rearrange("p (c n) -> p c n", c=4)

            def bd(dst, src, mask, w=()):
                nc_ = src.shape[1]
                s4 = src.unsqueeze(2).broadcast_to([128, nc_, 2, 64])
                m4 = mask.rearrange("p (h n) -> p h n", h=2).unsqueeze(1).broadcast_to([128, nc_, 2, 64])
                return V.tt(dst.rearrange("p c (h n) -> p c h n", h=2), s4, m4, ALU.mult, w)

            def pair(l, r, o, w, inc=False):
                for c in range(2):
                    t = PE.mm(o(c), l[:, c, :], r(c), True, True, w, inc=(inc and c == 1))
                return t

            def split(terms, o, w, inc=False):
                for h in range(2):
                    for c in range(len(terms)):
                        for i, (l, r) in enumerate(terms[c]):
                            end = i == len(terms[c]) - 1
                            t = PE.mm(o(c)[64 * h:64 * h + 64, :], l[:, 64 * h:64 * h + 64], r, i == 0, end, w,
                                      inc=(inc and end and h == 1 and c == len(terms) - 1))
                return t

            def half(hp, hf, tb):
                cs = slice(2 * hf, 2 * hf + 2)
                H_ = [c4(v)[:, cs, :] for v in Bs]
                bF, kF, aF, vF, bPF, kPF = H_[0:6]
                D, DT, O, LK, Vb, Bb, Kb = H_[6:13]

                def ar_(c):
                    return AHRH[:, :, (2 * hf + c) * 64:(2 * hf + c + 1) * 64]

                def bi(c):
                    at = bh_at + (2 * hf + c) * 64
                    d = i2_at - at
                    return AR[:, at:at + 2 * d].rearrange("p (x d) -> p x d", x=2)[:, :, 0:64]

                bA, pA = bank()
                bB, pB = bank()
                bC, pC = bank()
                pair(bF, ar_, lambda c: pA[:, c * 128:(c + 1) * 128].rearrange("p (x n) -> p x n", x=2), [tb])
                tA = pair(kF, ar_, lambda c: pA[:, 256 + c * 128:384 + c * 128].rearrange("p (x n) -> p x n", x=2), [tb],
                          True)
                yield
                pair(aF, bi, lambda c: pB[:, c * 128:(c + 1) * 128].rearrange("p (x n) -> p x n", x=2), [tb])
                split([[(vF[:, c, :], i2)] for c in range(2)], lambda c: pB[:, 256 + c * 64:320 + c * 64], [tb])
                tB = split([[(bPF[:, c, :], i2)] for c in range(2)], lambda c: pB[:, 384 + c * 64:448 + c * 64], [tb],
                           True)
                tC = split([[(kPF[:, c, :], i2)] for c in range(2)], lambda c: pC[:, c * 64:(c + 1) * 64], [tb], True)
                vA = pA.rearrange("p (m c x n) -> p m c x n", m=2, c=2, x=2)
                vB = pB[:, 0:256].rearrange("p (c x n) -> p c x n", c=2, x=2)
                bd(DT, vA[:, 0, :, 0, :], mDT, [tA])
                bd(D, vB[:, :, 0, :], mD, [tB])
                tD = V.last
                bd(LK, vA[:, 1, :, 0, :], mL)
                mR4 = mR.unsqueeze(1).broadcast_to([128, 2, 64])
                V.tt(LRB[:, cs, :], vA[:, 0, :, 1, :], mR4, ALU.mult, chain=False)
                rel(bA, V.tt(LRK[:, cs, :], vA[:, 1, :, 1, :], mR4, ALU.mult, chain=False))
                tV = V.cp(VS[:, cs, :], pB[:, 256:384].rearrange("p (c n) -> p c n", c=2), chain=False)
                D2, D2T, D4, D4T, D8, ET = H_[0:6]
                bQ, pQ = bank()
                pair(DT, lambda c: D[:, c, :], lambda c: pQ[:, c * 128:(c + 1) * 128], [tD])
                tQ = pair(D, lambda c: DT[:, c, :], lambda c: pQ[:, 256 + c * 128:384 + c * 128], [tD], True)
                q = BB[:, 0:2, :].rearrange("p m (c n) -> p m c n", c=4)[:, :, cs, :]
                t2 = A.cp(q, pQ.rearrange("p (m c n) -> p m c n", m=2, c=2), [tQ, tC], chain=False)
                rel(bQ, t2)
                bd(O, vB[:, :, 0, :], mO)
                V.cp(XX[:, cs, 0:64], vB[:, :, 1, :], chain=False)
                bd(Vb, pB[:, 256:384].rearrange("p (c n) -> p c n", c=2), mB)
                V.cp(BS[:, cs, :], pB[:, 384:512].rearrange("p (c n) -> p c n", c=2), chain=False)
                rel(bB, bd(Bb, pB[:, 384:512].rearrange("p (c n) -> p c n", c=2), mB))
                rel(bC, bd(Kb, pC[:, 0:128].rearrange("p (c n) -> p c n", c=2), mB, [tC]))
                idb = ident.unsqueeze(1).broadcast_to([128, 2, 128])
                tE = V.tt(ET, DT, idb, ALU.add, chain=False)
                yield
                bQ, pQ = bank()
                tl = split([[(LK[:, c, :], VS[:, 2 * hf + c, :])] for c in range(2)],
                           lambda c: pQ[:, c * 64:(c + 1) * 64], [tV], True)
                rel(bQ, V.cp(XX[:, cs, 64:128], pQ[:, 0:128].rearrange("p (c n) -> p c n", c=2), [tl], chain=False))
                bQ, pQ = bank()
                t = pair(D2T, lambda c: D2[:, c, :], lambda c: pQ[:, c * 128:(c + 1) * 128], [t2], True)
                t4 = A.cp(D4, pQ[:, 0:256].rearrange("p (c n) -> p c n", c=2), [t], chain=False)
                rel(bQ, t4)
                yield
                bQ, pQ = bank()
                de = BB[:, 1:9, :].rearrange("p (x m) (c n) -> p x m c n", x=2, c=4)[:, :, 0, cs, :]
                t = pair(D2, lambda c: de[:, :, c, :], lambda c: pQ[:, c * 256:(c + 1) * 256].rearrange(
                    "p (x n) -> p x n", x=2), [tE, t4], True)
                vQ = pQ.rearrange("p (c x n) -> p c x n", c=2, x=2)
                t4t = A.cp(D4T, vQ[:, :, 0, :], [t], chain=False)
                tE = V.tt(ET, vQ[:, :, 1, :], ET, ALU.add, [t, t4t], chain=False)
                rel(bQ, tE)
                yield
                bQ, pQ = bank()
                t = pair(D4T, lambda c: D4[:, c, :], lambda c: pQ[:, c * 128:(c + 1) * 128], [t4t], True)
                t8 = A.cp(D8, pQ[:, 0:256].rearrange("p (c n) -> p c n", c=2), [t], chain=False)
                rel(bQ, t8)
                for l, tl in ((D4, tE), (D8, t8)):
                    bQ, pQ = bank()
                    t = pair(l, lambda c: ET[:, c, :], lambda c: pQ[:, c * 128:(c + 1) * 128], [tl, tE], True)
                    tE = V.tt(ET, pQ[:, 0:256].rearrange("p (c n) -> p c n", c=2), ET, ALU.add, [t], chain=False)
                    rel(bQ, tE)
                    yield
                G, GT, G2T = H_[0], H_[2], H_[1]
                bQ, pQ = bank()
                bR, pR = bank()
                pair(ET, lambda c: O[:, c, :], lambda c: pQ[:, c * 128:(c + 1) * 128], [tE])
                tq = pair(ET, lambda c: XX[:, 2 * hf + c, :], lambda c: pQ[:, 256 + c * 128:384 + c * 128], [tE], True)
                tr_ = pair(O, lambda c: ET[:, c, :], lambda c: pR[:, c * 128:(c + 1) * 128], [tE], True)
                A.cp(G, pQ[:, 0:256].rearrange("p (c n) -> p c n", c=2), [tq], chain=False)
                tg = A.last
                tg2 = A.cp(GT, pR[:, 0:256].rearrange("p (c n) -> p c n", c=2), [tr_], chain=False)
                rel(bR, tg2)
                tx = V.cp(XX[:, cs, :], pQ[:, 256:512].rearrange("p (c n) -> p c n", c=2), [tq, tg], chain=False)
                rel(bQ, tx)
                yield
                bQ, pQ = bank()
                t = pair(G, lambda c: GT[:, c, :], lambda c: pQ[:, c * 128:(c + 1) * 128], [tg2], True)
                t = A.cp(G2T, pQ[:, 0:256].rearrange("p (c n) -> p c n", c=2), [t], chain=False)
                rel(bQ, t)
                yield
                for l, tl in ((G2T, t), (GT, tg2)):
                    bQ, pQ = bank()
                    t = pair(l, lambda c: XX[:, 2 * hf + c, :], lambda c: pQ[:, c * 128:(c + 1) * 128], [tl, tx], True)
                    tx = V.tt(XX[:, cs, :], pQ[:, 0:256].rearrange("p (c n) -> p c n", c=2), XX[:, cs, :], ALU.add, [t], chain=False)
                    rel(bQ, tx)
                    yield
                M1, M2, AT = H_[3], H_[4], H_[5]
                tm = bd(M1, XX[:, cs, 0:64], mB)
                bQ, pQ = bank()
                split([[(M1[:, c, :], LRB[:, 2 * hf + c, :])] for c in range(2)], lambda c: pQ[:, c * 64:(c + 1) * 64],
                      [tm])
                split([[(M1[:, c, :], BS[:, 2 * hf + c, :])] for c in range(2)],
                      lambda c: pQ[:, 128 + c * 64:192 + c * 64], [tm])
                t = split([[(Bb[:, c, :], XX[:, 2 * hf + c, 64:128]), (Kb[:, c, :], VS[:, 2 * hf + c, :])]
                           for c in range(2)], lambda c: pQ[:, 256 + c * 64:320 + c * 64], [tm], True)
                bd(M2, XX[:, cs, 64:128], mB)
                V.tt(QS[:, cs, :], pQ[:, 0:128].rearrange("p (c n) -> p c n", c=2), c4(rh)[:, cs, :], ALU.add, [t], chain=False)
                PCh = c4(PT_)[:, cs, 63:64]
                V.tt(CS[:, cs, :], i2.unsqueeze(1).broadcast_to([128, 2, 64]), bc(PCh, [128, 2, 64]), ALU.mult, chain=False)
                V.tt(CS[:, cs, :], pQ[:, 128:256].rearrange("p (c n) -> p c n", c=2), CS[:, cs, :], ALU.add)
                bd(AT, CS[:, cs, :], mB)
                rel(bQ, V.cp(CS[:, cs, :], pQ[:, 256:384].rearrange("p (c n) -> p c n", c=2)))
                yield

            for hp in range(4):
                for e in (V, A):
                    e.wait(V.last, A.last, PE.last)
                for c in range(4):
                    s = slice(c * 64, (c + 1) * 64)
                    V.scan(CU[:, s], bc(ones1, [128, 64]), LD[:, hp, s], 0.0, ALU.mult, ALU.add, chain=False)
                V.tt(PV, CU, LD[:, hp, :], ALU.subtract)
                tv = V.last
                te = A.act(PV, PV, ACT.Exp, [tv], chain=False)
                te2 = A.act(PI, CU, ACT.Exp, scale=-1.0, chain=False)
                te3 = A.act(PT_, CU, ACT.Exp, chain=False)
                V.tt(bh, KK[:, hp, :], AA[:, hp, :], ALU.mult, chain=False)
                V.stt(ah, KK[:, hp, :], -1.0, PV, ALU.mult, ALU.mult, [te])
                V.tt(bh, bh, PI, ALU.mult, [te2], chain=False)
                V.tt(kh, K2[:, hp, :], PI, ALU.mult, chain=False)
                V.tt(rh, R[:, hp, :], PT_, ALU.mult, [te3], chain=False)
                PC = c4(PT_)[:, :, 63:64]
                for i, v in enumerate((bh, kh, ah)):
                    bd(c4(Bs[i]), c4(v), mB)
                bd(c4(Bs[3]), c4(VV[:, hp, :]), mB)
                V.tt(c4(bp), c4(bh), bc(PC, [128, 4, 64]), ALU.mult, chain=False)
                bd(c4(Bs[4]), c4(bp), mB)
                V.tt(c4(kp), c4(kh), bc(PC, [128, 4, 64]), ALU.mult, chain=False)
                bd(c4(Bs[5]), c4(kp), mB)
                tb = V.last
                weave(half(hp, 0, tb), half(hp, 1, tb))
                Vb, M2, AT, ST = (c4(Bs[i]) for i in (10, 4, 5, 13))
                V.cp(SS[:, 0, :], CS[:, 0, :], chain=False)
                bd(ST[:, 0:1, :], SS[:, 0:1, :], mB)
                tst = [V.last]
                for c in range(1, 3):
                    b, p = bank()
                    t = split([[(AT[:, c, :], SS[:, c - 1, :])]], lambda _: p[:, 0:64], [V.last], True)
                    rel(b, V.tt(SS[:, c, :], p[:, 0:64], CS[:, c, :], ALU.add, [t], chain=False))
                    tst.append(bd(ST[:, c:c + 1, :], SS[:, c:c + 1, :], mB))
                for c in range(4):
                    terms = [(M2[:, c, :], LRB[:, c, :]), (Vb[:, c, :], LRK[:, c, :])]
                    if c:
                        terms.append((ST[:, c - 1, :], QS[:, c, :]))
                    if c % 2 == 0:
                        b, p = bank()
                    t = split([terms], lambda _: p[:, (c % 2) * 64:(c % 2) * 64 + 64], [tst[max(c - 1, 0)]], True)
                    if c % 2:
                        rel(b, A.cp(YT[:, hp, (c - 1) * 64:(c + 1) * 64], p[:, 0:128], [t], chain=False))
            fence()
            ar["at"] = base
            Y2, RS = buf(4, 256), buf(4, 256)
            for j in range(0, 4, 2):
                b, p = bank()
                for i in range(2):
                    t = PE.mm(p[:, i * 256:(i + 1) * 256], ones64, YT[:, j + i, :], True, True, [V.last], inc=(i == 1))
                pv = p.rearrange("p (a b) -> p a b", a=2)
                rel(b, V.stt(YT[:, j:j + 2, :], pv, -1.0 / 64, YT[:, j:j + 2, :], ALU.mult, ALU.add, [t], chain=False))
            tk = V.tt(Y2, YT, YT, ALU.mult)
            for j in range(0, 4, 2):
                b, p = bank()
                for i in range(2):
                    t = PE.mm(p[:, i * 256:(i + 1) * 256], ones64, Y2[:, j + i, :], True, True, [tk], inc=(i == 1))
                rel(b, A.act(RS[:, j:j + 2, :], p.rearrange("p (a b) -> p a b", a=2), ACT.Ln, [t],
                             bias=par("epsln"), scale=1.0 / 64, chain=False))
            t = A.act(RS, RS, ACT.Exp, scale=-0.5)
            V.tt(YT, YT, RS, ALU.mult, [t], chain=False)
            for j in range(4):
                V.ts(YT[:, j, :], YT[:, j, :], par("ln_g", j), par("ln_b", j), ALU.mult, ALU.add)
            V.tt(YT, YT, BON, ALU.add)
            t = V.tt(OT[:, 0:4, :], YT, GG, ALU.mult)
            out_proj(["even_out0", "even_out1"], OT, [t])

        def over(l, G, flag):
            names = s_over[l]
            V2, A2, P2 = Vec("v2", names[0]), Sca("a2", names[1]), Ten("pe2", names[2])
            S2 = Eng("sp2", None)
            toks = [V.last, A.last, PE.last]
            for e in (V2, A2, P2, S2):
                e.wait(*toks)
            W3 = AR[:, 0:3 * SLOT]
            sg = AR[:, 3 * SLOT:3 * SLOT + 1024].rearrange("p (a b) -> p a b", a=4)
            hi = AR[:, 3 * SLOT + 1024:3 * SLOT + 2048].rearrange("p (a b) -> p a b", a=4)
            wg = W3[:, 0:SLOT].rearrange("p (k n) -> p k n", k=8)
            wu = W3[:, SLOT:2 * SLOT].rearrange("p (k n) -> p k n", k=8)
            wd = W3[:, 2 * SLOT:3 * SLOT].rearrange("p (k n) -> p k n", k=4)
            first = [i for i, c in enumerate(chunks) if c[0] == f"moe{l}_g0_0"][0]
            tp = tv = None
            for e in range(NE):
                q, j = e // 4, e % 4
                S2.wait(tp)
                for part, dst in ((0, wg), (4, wu), (8, wd)):
                    for c in range(4):
                        o = offs[first + 12 * q + part + c]
                        src = Wd[o:o + 128 * SLOT].rearrange("(p k n) -> p k n", p=128, k=8 if part < 8 else 4)
                        if part < 8:
                            S2.dma(dst[:, 2 * c:2 * c + 2, :], src[:, j::4, :], names[3])
                        else:
                            S2.dma(dst[:, c, :], src[:, j, :], names[3])
                td = (names[3], 16 * 12 * (e + 1))
                for i in range(4):
                    for k in range(8):
                        P2.mm(ps[:, i, 0:256], wg[:, k, i * 128:(i + 1) * 128], HT[:, k, :], k == 0, k == 7, [td, tv])
                    for k in range(8):
                        t = P2.mm(ps[:, 4 + i, 0:256], wu[:, k, i * 128:(i + 1) * 128], HT[:, k, :], k == 0, k == 7,
                                  inc=(k == 7))
                a = A2.act(sg, ps[:, 0:4, 0:256], ACT.Silu, [t, tv])
                v = V2.tt(hi, ps[:, 4:8, 0:256], sg, ALU.mult, [t, a])
                for n in range(2):
                    for t in range(2):
                        b = 2 * n + t
                        for k in range(4):
                            tp = P2.mm(ps[:, b, :], hi[:, k, t * 128:(t + 1) * 128], wd[:, k, n * 512:(n + 1) * 512],
                                       k == 0, k == 3, [v, a], inc=(k == 3))
                for n in range(2):
                    for t in range(2):
                        xs = X[:, t, n * 512:(n + 1) * 512]
                        tv = V2.stt(xs, ps[:, 2 * n + t, :], G[:, t, e:e + 1], xs, ALU.mult, ALU.add, [tp])
            for e in (V2, A2, P2, S2):
                e.wait(V2.last, A2.last, P2.last)
            for e, s2 in ((V, V2), (A, A2), (PE, P2), (SP, S2)):
                e.branch(flag, 0, s2)

        def moe(stg, l):
            phase()
            nxt = stages[stages.index(stg) + 1:][:1]
            if nxt and nxt[0] + "_c" in coffs:
                consts(nxt[0] + "_c")
            XN = norm_T(f"g_{stg}")
            hd = [V.last, A.last]
            L = buf(2, 36)
            EX, MG, CM = buf(2, 4), buf(2, 4), buf(2, 4)
            PR = buf(2, 4, 8)
            EL, M1, M2, C8, W8 = (buf(2, 8) for _ in range(5))
            s1 = [buf(2, 1) for _ in range(8)]
            Gf, Sf, POS, GO = (buf(2, 32) for _ in range(4))
            G, SE = (v.rearrange("p t (g j) -> p t g j", g=4) for v in (Gf, Sf))
            c = take(stg + "_r")
            for t in range(2):
                b, p, tk = proj_tok(c, HT, 8, t, 0, 36, hd)
                rel(b, V.tt(L[:, t, :], p[:, 0:36], par(f"rb{l}", 0, 36), ALU.add, [tk]))
            c.free(tk)

            def first(mask, cum, n):
                for t in range(2):
                    V.scan(cum[:, t, :], mask[:, t, :], mask[:, t, :], 0.0, ALU.max, ALU.max)
                V.cp(mask[:, :, 0:1], cum[:, :, 0:1])
                V.tt(mask[:, :, 1:n], cum[:, :, 1:n], cum[:, :, 0:n - 1], ALU.subtract)

            def spread(dst, w):
                for t in range(2):
                    V.tt(dst[:, t], MG[:, t, :].unsqueeze(2).broadcast_to([128, 4, 8]),
                         w[:, t, :].unsqueeze(1).broadcast_to([128, 4, 8]), ALU.mult)

            gm, gw, e1, e2, p2, den, g1, g2 = s1
            V.red(gm, L[:, :, 0:4], ALU.max)
            V.tt(EX, L[:, :, 0:4], bc(gm, [128, 2, 4]), ALU.subtract)
            V.ts(MG, EX, 0.0, None, ALU.is_ge)
            t = A.act(EX, EX, ACT.Exp, [V.last])
            first(MG, CM, 4)
            V.tt(PR, L[:, :, 4:36].rearrange("p t (g j) -> p t g j", g=4),
                 MG.unsqueeze(3).broadcast_to([128, 2, 4, 8]), ALU.mult)
            V.red(EL, PR.rearrange("p t g j -> p t j g"), ALU.add)
            V.red(e1, EL, ALU.max)
            V.tt(EL, EL, bc(e1, [128, 2, 8]), ALU.subtract)
            V.ts(M1, EL, 0.0, None, ALU.is_ge)
            first(M1, C8, 8)
            V.stt(EL, M1, -1e30, EL, ALU.mult, ALU.add)
            V.red(e2, EL, ALU.max)
            t = A.act(p2, e2, ACT.Exp, [V.last])
            V.tt(M2, EL, bc(e2, [128, 2, 8]), ALU.is_ge)
            first(M2, C8, 8)
            V.tt(W8, M1, M2, ALU.add)
            spread(SE, W8)
            tse = V.last
            tri = par("tri", 0, 128)
            b, p = bank()
            PE.mm(p[:, 0:32], tri, Sf[:, 0, :], True, True, [tse])
            PE.mm(p[:, 32:64], ones, Sf[:, 0, :], True, False)
            PE.mm(p[:, 32:64], tri, Sf[:, 1, :], False, True)
            PE.mm(p[:, 64:96], ones, Sf[:, 0, :], True, False)
            tk = PE.mm(p[:, 64:96], ones, Sf[:, 1, :], False, True, inc=True)
            V.tt(POS, p[:, 0:64].rearrange("p (t e) -> p t e", t=2), Sf, ALU.mult, [tk])
            V.ts(POS, POS, 1.0, None, ALU.subtract)
            SQs = [buf(2, 4, CAP) for _ in range(2)]
            XGs = [buf(8, 4 * CAP) for _ in range(2)]
            read = {}

            def one_hot(q):
                return V.tt(SQs[q % 2], POS[:, :, 4 * q:4 * q + 4].unsqueeze(3).broadcast_to([128, 2, 4, CAP]),
                            par("iota", 0, CAP).unsqueeze(1).unsqueeze(1).broadcast_to([128, 2, 4, CAP]),
                            ALU.is_equal, [read.get(("s", q - 2))])

            def gather(q, tsq):
                S, XG = SQs[q % 2].rearrange("p t e c -> p t (e c)"), XGs[q % 2]
                for k0 in (0, 4):
                    b, p = bank()
                    for k in range(4):
                        for t in range(2):
                            tk = PE.mm(p[:, k * 128:(k + 1) * 128], XN[:, t, (k0 + k) * 128:(k0 + k + 1) * 128],
                                       S[:, t, :], t == 0, t == 1, [tsq], inc=(k == 3 and t == 1))
                    e = V.tt(XG[:, k0:k0 + 4, :], p.rearrange("p (k n) -> p k n", k=4),
                             par(f"g_{stg}", k0, 4).unsqueeze(2).broadcast_to([128, 4, 128]), ALU.mult,
                             [tk, read.get(("x", q - 2))])
                    rel(b, e)
                    yield e
                yield V.tt(SQs[q % 2], SQs[q % 2], Gf[:, :, 4 * q:4 * q + 4].unsqueeze(3).broadcast_to([128, 2, 4, CAP]),
                           ALU.mult, [tk])

            tsq = one_hot(0)
            V.red(gw, EX, ALU.add, [t])
            V.rcp(gw, gw)
            V.ts(den, p2, 1.0, None, ALU.add)
            V.rcp(den, den)
            V.tt(g1, gw, den, ALU.mult)
            V.tt(g2, g1, p2, ALU.mult)
            V.tt(M1, M1, bc(g1, [128, 2, 8]), ALU.mult)
            V.tt(M2, M2, bc(g2, [128, 2, 8]), ALU.mult)
            V.tt(W8, M1, M2, ALU.add)
            spread(G, W8)
            V.red(e1[:, 0, :], p[:, 64:96], ALU.max)
            rel(b, V.last)
            V.ts(e1[:, 0, :], e1[:, 0, :], float(CAP), 0.0, ALU.subtract, ALU.max)
            V.cp(FLAG[:, l:l + 1], e1[:, 0, :])
            V.ts(GO, POS, CAP - 0.5, None, ALU.is_ge)
            V.tt(GO, GO, Gf, ALU.mult)
            _, tx, ts_ = gather(0, tsq)
            SG = [buf(512) for _ in range(2)]
            HI = [buf(512) for _ in range(2)]
            HTr = [buf(4, 128) for _ in range(2)]
            SC = [buf(2, 128) for _ in range(2)]
            YS = [buf(2, 512) for _ in range(2)]
            assert ar["at"] <= TOP
            beside = s5_pre() if nxt == ["odd"] else iter(())
            done = [None, None]
            for q in range(NE // 4):
                u = q % 2
                sg, hi, htr, sc, ys = SG[u], HI[u], HTr[u], SC[u], YS[u]
                S, XG = SQs[u].rearrange("p t e c -> p t (e c)"), XGs[u]
                res = []
                for part in "gu":
                    b, p = bank()
                    for c in range(4):
                        ck = take(f"{stg}_{part}{q}_{c}")
                        for kk in range(2):
                            for j in range(4):
                                k = 2 * c + kk
                                tk = PE.op(lambda e, p=p, j=j, k=k, x=XG, w=ck.ap[:, kk * 4 + j, :]: e.matmul(
                                    p[32 * j:32 * j + 32, :], x[:, k, j * CAP:(j + 1) * CAP], w,
                                    start=(k == 0), stop=(k == 7)),
                                    [ck.tok, tx], chain=False, inc=(kk == 1 and j == 3))
                        ck.free(tk)
                    res.append((b, p, tk))
                read["x", q] = tk
                if q < NE // 4 - 1:
                    tsq = one_hot(q + 1)
                b, p, tk = res[0]
                a = A.act(sg, p, ACT.Silu, [tk, done[u]])
                rel(b, a)
                b, p, tk = res[1]
                v = V.tt(hi, p, sg, ALU.mult, [tk, a])
                rel(b, v)
                b, p = bank()
                for t in range(2):
                    tk = PE.tr(p[:, t * 128:(t + 1) * 128], S[:, t, :], ident, [ts_], inc=(t == 1))
                read["s", q] = tk
                a2 = A.cp(sc, p[:, 0:256].rearrange("p (a b) -> p a b", a=2), [tk, done[u]])
                rel(b, a2)
                b, p = bank()
                for k in range(4):
                    tk = PE.tr(p[:, k * 128:(k + 1) * 128], hi[:, k * 128:(k + 1) * 128], ident, [v], inc=(k == 3))
                v = V.cp(htr, p.rearrange("p (a b) -> p a b", a=4), [tk, done[u]])
                rel(b, v)
                if q < NE // 4 - 1:
                    _, tx, ts_ = gather(q + 1, tsq)
                b0, p0 = bank()
                b1, p1 = bank()
                for k in range(4):
                    ck = take(f"{stg}_d{q}_{k}")
                    for n, p in ((0, p0), (1, p1)):
                        for j in range(4):
                            tk = PE.op(lambda e, p=p, j=j, k=k, n=n, w=ck.ap[:, j, n * 512:(n + 1) * 512], h=htr: e.matmul(
                                p[32 * j:32 * j + 32, :], h[:, k, j * CAP:(j + 1) * CAP], w,
                                start=(k == 0), stop=(k == 3)),
                                [ck.tok, v], chain=False, inc=(n == 1 and j == 3))
                    ck.free(tk)
                a = A.cp(ys[:, 0, :], p0, [tk, done[u]])
                v = V.cp(ys[:, 1, :], p1, [tk, done[u]])
                rel(b0, a)
                rel(b1, v)
                for n, w in ((0, a), (1, v)):
                    for t in range(2):
                        b, p = bank()
                        tk = PE.mm(p, sc[:, t, :], ys[:, n, :], True, True, [w, a2], inc=True)
                        xs = X[:, t, n * 512:(n + 1) * 512]
                        rel(b, V.tt(xs, p, xs, ALU.add, [tk]))
                done[u] = tk
                next(beside, None)
            GOk = GS[:, l * 64:(l + 1) * 64].rearrange("p (t e) -> p t e", t=2)
            V.cp(GOk, GO)
            fence()
            over(l, GOk, FLAG[0:1, l:l + 1])

        TOP = NA - 4328
        lr, st_, rho, th, ph, kf, sn, cs, nr, ni, de, cr, ci, tp = (AR[:, TOP + 16 * i:TOP + 16 * i + 16]
                                                                    for i in range(14))
        lm = AR[:, TOP + 224:TOP + 232]
        AG, KF, SN, CS_ = (AR[:, TOP + 232 + 1024 * i:TOP + 1256 + 1024 * i].rearrange("p (a b) -> p a b", a=4)
                           for i in range(4))
        lam_init = 0.8 - 0.6 * math.exp(-0.3)
        MAGIC = 12582912.0
        C1, C2, C3 = 6.28125, 0.0019350051879882812, 3.0199159819568e-07

        def reduce2pi(dst, src, k):
            V.ts(k, src, 1.0 / (2 * math.pi), MAGIC, ALU.mult, ALU.add)
            V.ts(k, k, MAGIC, None, ALU.subtract)
            V.stt(dst, k, -C1, src, ALU.mult, ALU.add)
            V.stt(dst, k, -C2, dst, ALU.mult, ALU.add)
            V.stt(dst, k, -C3, dst, ALU.mult, ALU.add)
            return V.ts(dst, dst, 3.1415925, -3.1415925, ALU.min, ALU.max)

        def sincos(sn, cs, r, tmp, w):
            t1 = V.stt(tmp, r, -1.0, r, ALU.mult, ALU.max, w)
            A.act(sn, r, ACT.Sin, [t1])
            return A.act(cs, tmp, ACT.Sin, bias=par("hpi"), scale=-1.0)

        def s5_pre():
            st["pre"] = True
            tcst = consts("odd_c")[1]
            V.wait(tcst)
            lp = par("lam", 0, 256).rearrange("p (a b) -> p a b", a=4)
            V.tt(AG[:, 0:1, 0:64], lp[:, 0:1, :], lp[:, 1:2, :], ALU.mult)
            V.tt(AG[:, 1:2, 0:64], lp[:, 2:3, :], lp[:, 3:4, :], ALU.mult)
            V.red(lm[:, 0:2], AG[:, 0:2, 0:64], ALU.add)
            t = A.act(lm[:, 2:4], lm[:, 0:2], ACT.Exp, [V.last])
            V.tt(lm[:, 4:5], lm[:, 3:4], lm[:, 2:3], ALU.subtract, [t])
            V.ts(lm[:, 4:5], lm[:, 4:5], lam_init, None, ALU.subtract)
            V.ts(lr, par("s5_re", 0, 16), -1e-4, None, ALU.min)
            li = par("s5_im", 0, 16)
            t = A.act(st_, par("s5_ls", 0, 16), ACT.Exp)
            V.tt(rho, lr, st_, ALU.mult, [t])
            t = A.act(rho, rho, ACT.Exp, [V.last])
            V.tt(th, li, st_, ALU.mult)
            t = reduce2pi(ph, th, kf)
            t = sincos(sn, cs, ph, tp, [t])
            yield
            V.tt(nr, rho, cs, ALU.mult, [t])
            V.ts(nr, nr, 1.0, None, ALU.subtract)
            V.tt(ni, rho, sn, ALU.mult)
            V.tt(de, lr, lr, ALU.mult)
            V.tt(tp, li, li, ALU.mult)
            V.tt(de, de, tp, ALU.add)
            V.rcp(de, de)
            V.tt(cr, nr, lr, ALU.mult)
            V.tt(tp, ni, li, ALU.mult)
            V.tt(cr, cr, tp, ALU.add)
            V.tt(cr, cr, de, ALU.mult)
            V.tt(ci, ni, lr, ALU.mult)
            V.tt(tp, nr, li, ALU.mult)
            V.tt(ci, ci, tp, ALU.subtract)
            V.tt(ci, ci, de, ALU.mult)
            yield
            trow = CS_T[:, 896:1152]
            for i in range(4):
                V.ts(AG[:, i, :], trow, ph[:, i:i + 1], None, ALU.mult)
            yield
            t = reduce2pi(AG, AG, KF)
            yield
            sincos(SN, CS_, AG, KF, [t])
            yield

        def odd():
            phase()
            if "pre" not in st:
                for _ in s5_pre():
                    pass
            norm_T("g_odd")
            phase()
            cv, tcst = consts("odd_c")
            cosT, sinT, cmask = cv[:, 0:256], cv[:, 256:512], cv[:, 512:768]
            RT, trow = cv[:, 768:896], cv[:, 896:1152]
            OT = buf(8, 256)
            U5 = buf(4, 256)
            QK, VT = buf(8, 256), buf(2, 512)
            SQ, RS = buf(4, 256), buf(4, 256)
            PRb = buf(4, 256)
            PR = [PRb[:, 0:2, :], PRb[:, 2:4, :]]
            AT = [buf(2, 256) for _ in range(2)]
            mx, sm = buf(32), buf(32)
            Y5, BR, BI, TA, TB = (buf(4, 256) for _ in range(5))
            assert ar["at"] <= TOP

            def p2(p):
                return p.rearrange("p (a b) -> p a b", a=2)

            c = take("odd_in3")
            for j in (0, 2):
                b, p, tk = proj_T(c, [j * 128, j * 128 + 128], HT, 8)
                tu = A.cp(U5[:, j:j + 2, :], p2(p), [tk], chain=False)
                rel(b, tu)
            c.free(tk)
            cC, cB = take("s5_C"), take("s5_B")
            sB = cB.ap[:, 0, :].rearrange("p (r i n) -> p r i n", r=2, i=16)
            sC = cC.ap[:, 0, :].rearrange("p (r i n) -> p r i n", r=2, i=16)
            crb, cib = (v.unsqueeze(2).broadcast_to([128, 16, 32]) for v in (cr, ci))
            c_re, c_im = sC[:, 0], sC[:, 1]
            x1, x2, x3 = (v.rearrange("p a b -> p (a b)")[:, 0:512].rearrange("p (a b) -> p a b", a=16)
                          for v in (AG, KF, TA))
            V.tt(x1, c_re, cib, ALU.mult, [cC.tok])
            V.tt(x2, c_im, cib, ALU.mult)
            V.tt(x3, c_im, crb, ALU.mult)
            V.tt(c_re, c_re, crb, ALU.mult)
            V.tt(c_re, c_re, x2, ALU.subtract)
            tC = V.tt(c_im, x1, x3, ALU.add)
            nlam = lm[:, 4:5]

            def attention():
                for i in range(2):
                    c = take(f"odd_in{i}")
                    for j in (0, 2):
                        b, p, tk = yield from proj_T_g(c, [j * 128, j * 128 + 128], HT, 8)
                        t = A.cp(QK[:, i * 4 + j:i * 4 + j + 2, :], p2(p), [tk], chain=False)
                        rel(b, t)
                        yield
                    c.free(tk)
                    X4 = QK[:, 4 * i:4 * i + 4, :]
                    t = V.tt(SQ, X4, X4, ALU.mult, [t, PE.last], chain=False)
                    yield
                    for j in (0, 2):
                        b, p = bank()
                        for ii in range(2):
                            tk = PE.mm(p[:, ii * 256:(ii + 1) * 256], ones64, SQ[:, j + ii, :], True, True, [t],
                                       inc=(ii == 1))
                        rel(b, A.act(RS[:, j:j + 2, :], p2(p), ACT.Ln, [tk, V.last], bias=par("eps6"), scale=1.0 / 64, chain=False))
                    t = A.act(RS, RS, ACT.Exp, scale=-0.5)
                    t = V.stt(X4, X4, par("kn" if i else "qn"), RS, ALU.mult, ALU.mult, [t], chain=False)
                    V.wait(tcst)
                    yield
                    for j in (0, 2):
                        b, p = bank()
                        for ii in range(2):
                            tk = PE.mm(p[:, ii * 256:(ii + 1) * 256], RT, X4[:, j + ii, :], True, True, [t, tcst],
                                       inc=(ii == 1))
                        rel(b, V.tt(SQ[:, j:j + 2, :], p2(p), sinT.unsqueeze(1).broadcast_to([128, 2, 256]), ALU.mult,
                                    [tk], chain=False))
                    V.tt(X4, X4, cosT.unsqueeze(1).broadcast_to([128, 4, 256]), ALU.mult, [PE.last], chain=False)
                    tq = V.tt(X4, X4, SQ, ALU.add)
                c = take("odd_in2")
                for t in range(2):
                    b, p, tk = proj_tok(c, HT, 8, t, 0, 512)
                    rel(b, A.cp(VT[:, t, :], p, [tk], chain=False))
                    yield
                c.free(tk)
                av = [None, None]
                YO = SQ
                for h in range(4):
                    for q in range(2):
                        nk = (q + 1) * 128
                        pr = PR[q]
                        i0 = h * 4 + q * 2
                        for m in range(2):
                            b, p = bank()
                            tk = PE.mm(p[:, 0:nk], QK[m * 64:(m + 1) * 64, h, q * 128:(q + 1) * 128],
                                       QK[m * 64:(m + 1) * 64, 4 + h, 0:nk], True, True, [tq], inc=True)
                            rel(b, V.stt(pr[:, m, 0:nk], p[:, 0:nk], 0.125, cmask[:, 256 - nk:256], ALU.mult, ALU.add,
                                         [tk], chain=False))
                        V.red(mx[:, i0:i0 + 2], pr[:, :, 0:nk], ALU.max)
                        V.ts(mx[:, i0:i0 + 2], mx[:, i0:i0 + 2], -1.0, None, ALU.mult)
                        tv = V.last
                        yield
                        for m in range(2):
                            ta = A.act(pr[:, m, 0:nk], pr[:, m, 0:nk], ACT.Exp, [tv], bias=mx[:, i0 + m:i0 + m + 1], chain=False)
                        V.red(sm[:, i0:i0 + 2], pr[:, :, 0:nk], ALU.add, [ta], chain=False)
                        V.rcp(sm[:, i0:i0 + 2], sm[:, i0:i0 + 2])
                        V.tt(sm[:, i0 + 1:i0 + 2], sm[:, i0 + 1:i0 + 2], nlam, ALU.mult)
                        V.ts(pr[:, 0, 0:nk], pr[:, 0, 0:nk], sm[:, i0:i0 + 1], None, ALU.mult, chain=False)
                        t = V.stt(pr[:, 0, 0:nk], pr[:, 1, 0:nk], sm[:, i0 + 1:i0 + 2], pr[:, 0, 0:nk], ALU.mult,
                                  ALU.add)
                        b, p = bank()
                        for kb in range(q + 1):
                            tk = PE.tr(p[:, kb * 128:(kb + 1) * 128], pr[:, 0, kb * 128:(kb + 1) * 128], ident, [t],
                                       inc=(kb == q))
                        at = AT[h % 2]
                        e = A.cp(at[:, 0:q + 1, q * 128:(q + 1) * 128],
                                 p[:, 0:nk].rearrange("p (a b) -> p a b", a=q + 1), [tk, av[h % 2]], chain=False)
                        rel(b, e)
                        V.wait(tk)
                        yield
                    b, p = bank()
                    PE.mm(p[:, 0:256], VT[:, 0, h * 128:(h + 1) * 128], at[:, 0, :], True, False, [e])
                    tk = PE.mm(p[:, 128:256], VT[:, 1, h * 128:(h + 1) * 128], at[:, 1, 128:256], False, True, inc=True)
                    av[h % 2] = tk
                    rel(b, A.cp(YO[:, h, :], p[:, 0:256], [tk, V.last], chain=False))
                    yield
                t = V.tt(PRb, YO, YO, ALU.mult, [A.last, PE.last], chain=False)
                for j in (0, 2):
                    b, p = bank()
                    for i in range(2):
                        tk = PE.mm(p[:, i * 256:(i + 1) * 256], ones, PRb[:, j + i, :], True, True, [t], inc=(i == 1))
                    rel(b, A.act(RS[:, j:j + 2, :], p2(p), ACT.Ln, [tk], bias=par("eps5"), scale=1.0 / 128, chain=False))
                t = A.act(RS, RS, ACT.Exp, scale=-0.5)
                yield
                V.stt(OT[:, 0:4, :], YO, 1.0 - lam_init, RS, ALU.mult, ALU.mult, [t], chain=False)
                V.ts(OT[:, 0:4, :], OT[:, 0:4, :], par("subln"), None, ALU.mult)

            def s5():
                tout = tsc = None
                for q in range(4):
                    if q:
                        for i in range(4):
                            V.ts(AG[:, i, :], trow, ph[:, q * 4 + i:q * 4 + i + 1], None, ALU.mult, w=[tcst, A.last])
                        t = reduce2pi(AG, AG, KF)
                        tsc = sincos(SN, CS_, AG, KF, [t])
                    yield
                    for part, dst in ((0, BR), (1, BI)):
                        for j in (0, 2):
                            b, p = bank()
                            for i in range(2):
                                tk = PE.mm(p[:, i * 256:(i + 1) * 256], sB[:, part, q * 4 + j + i, :], U5[:, q, :],
                                           True, True, [cB.tok, tu], inc=(i == 1))
                            tb = A.cp(dst[:, j:j + 2, :], p2(p), [tk, tout], chain=False)
                            rel(b, tb)
                    yield
                    V.tt(TA, BR, CS_, ALU.mult, [tb, tsc, tC], chain=False)
                    G.tt(TB, BI, CS_, ALU.mult, [tb, tsc, V.last], chain=False)
                    V.tt(AG, BI, SN, ALU.mult, chain=False)
                    G.tt(KF, BR, SN, ALU.mult, chain=False)
                    V.tt(TA, TA, AG, ALU.add)
                    tg = G.tt(TB, TB, KF, ALU.subtract)
                    yield
                    for i in range(4):
                        r = bc(rho[:, q * 4 + i:q * 4 + i + 1], [128, 256])
                        V.scan(TA[:, i, :], r, TA[:, i, :], 0.0, ALU.mult, ALU.add)
                    for i in range(4):
                        r = bc(rho[:, q * 4 + i:q * 4 + i + 1], [128, 256])
                        V.scan(TB[:, i, :], r, TB[:, i, :], 0.0, ALU.mult, ALU.add, [tg], chain=False)
                    yield
                    tv = V.last
                    G.tt(AG, TB, SN, ALU.mult, [tv], chain=False)
                    V.tt(BR, TA, CS_, ALU.mult)
                    V.tt(BI, TA, SN, ALU.mult, chain=False)
                    V.tt(KF, TB, CS_, ALU.mult, chain=False)
                    tg = G.last
                    V.stt(BI, BI, -1.0, KF, ALU.mult, ALU.subtract)
                    V.tt(BR, BR, AG, ALU.subtract, [tg], chain=False)
                    yield
                    b, p = bank()
                    for part, xx in ((0, BR), (1, BI)):
                        for m in range(4):
                            tk = PE.mm(p[32 * m:32 * m + 32, 0:256], sC[:, part, q * 4 + m, :], xx[:, m, :],
                                       part == 0, part == 1, [V.last, tC], inc=(part == 1 and m == 3))
                    tout = tk
                    rel(b, V.stt(Y5[:, q, :], U5[:, q, :], par("s5_d", q), p[:, 0:256], ALU.mult, ALU.add, [tk], chain=False))
                    yield
                cC.free(tk)
                cB.free(tk)
                c0 = math.sqrt(2.0 / math.pi)
                V.tt(TA, Y5, Y5, ALU.mult)
                V.ts(TA, TA, 0.044715 * c0, c0, ALU.mult, ALU.add)
                V.tt(TA, TA, Y5, ALU.mult)
                t = A.act(TA, TA, ACT.Tanh, [V.last], chain=False)
                yield
                V.ts(TA, TA, 0.5, 0.5, ALU.mult, ALU.add, w=[t], chain=False)
                s5_out.append(V.tt(Y5, Y5, TA, ALU.mult))

            s5_out = []
            sg, ag = s5(), attention()
            for _ in range(4):
                next(sg)
            weave(ag, sg)
            t = s5_out[0]
            glu = take("glu")
            for j in (0, 2):
                b, p, tk = proj_T(glu, [j * 128, j * 128 + 128], Y5, 4, [t])
                a = A.act(TB[:, j:j + 2, :], p2(p), ACT.Sigmoid, [tk], chain=False)
                rel(b, a)
            glu.free(tk)
            t = V.tt(OT[:, 4:8, :], Y5, TB, ALU.mult, [a], chain=False)
            out_proj(["odd_out0", "odd_out1"], OT, [t])

        def hyb(stg):
            phase()
            norm_HL(f"g_{stg}")
            phase()
            cv, tcst = consts(stg + "_c")
            cosT, sinT, tri = cv[:, 0:256], cv[:, 256:512], cv[:, 512:768]
            dec = cv[:, 768:1792].rearrange("p (h n) -> p h n", h=4)
            o = 1792
            cw, cb_ = cv[:, o:o + 96], cv[:, o + 96:o + 120]
            dsk, nw = cv[:, o + 120:o + 136], cv[:, o + 136:o + 152]
            dtb, alog = cv[:, o + 152:o + 184], cv[:, o + 184:o + 216]
            YH, YL = buf(16, 256, of=AR32), buf(16, 256, of=AR32)
            base = ar["at"]
            MG = buf(8, 256)
            ar["at"] = base
            for e in (V, A, PE):
                e.wait(tcst)
            V.ts(cv[:, o:o + 120], cv[:, o:o + 120], 0.5, None, ALU.mult)
            T1, T2 = buf(2, 256), buf(2, 256)
            QRs, KRs, VTs, SGs = ([buf(2, n) for _ in range(2)] for n in (256, 256, 512, 512))
            Y, SQ = buf(4, 256), buf(4, 256)
            PTs = buf(384)
            RS = buf(256)
            SGM = buf(8, 256)

            def p2(p):
                return p.rearrange("p (a b) -> p a b", a=2)

            def rstd(w=()):
                t = A.act(SQ, Y, ACT.Square, [V.last, *w])
                yield
                b, p = bank()
                for i in range(4):
                    tk = PE.mm(p[:, 0:256], ones, SQ[:, i, :], i == 0, i == 3, [t], inc=(i == 3))
                yield
                rel(b, A.act(RS, p[:, 0:256], ACT.Ln, [tk, V.last], bias=par("eps6"), scale=1.0 / 512))
                return A.act(RS, RS, ACT.Exp, scale=-0.5)

            ret = {}

            def ret_in(h):
                QR, KR, VT = QRs[h % 2], KRs[h % 2], VTs[h % 2]
                SG = SGs[h % 2].rearrange("p a (b c) -> p (a b) c", b=2)
                before = ret.get(("end", h - 2), [])
                c = take_cut(f"{stg}_qk{h}")
                for which, dst, sc in ((0, QR, 1.0), (1, KR, 1.0 / 16)):
                    b, p, tk = yield from proj_cut_g(c + 2 * which)
                    V.stt(T1, p2(p), sc, cosT.unsqueeze(1).broadcast_to([128, 2, 256]), ALU.mult, ALU.mult,
                          [tk, *before])
                    rel(b, V.stt(T2, p2(p), sc, sinT.unsqueeze(1).broadcast_to([128, 2, 256]), ALU.mult, ALU.mult))
                    V.tt(dst[:, 0, :], T1[:, 0, :], T2[:, 1, :], ALU.subtract)
                    ret["r", h] = V.tt(dst[:, 1, :], T2[:, 0, :], T1[:, 1, :], ALU.add)
                    yield
                c = take_cut(f"{stg}_v{h}")
                for j in (0, 2):
                    b, p = bank()
                    pair_cut(p[:, 0:256], c + j, 0)
                    yield
                    tk = pair_cut(p[:, 256:512], c + j, 1)
                    ret["v", h] = A.cp(VT[:, :, j * 128:j * 128 + 256], p2(p), [tk, *before])
                    rel(b, A.last)
                    yield
                c = take_cut(f"{stg}_g{h}")
                for j in (0, 2):
                    b, p, tk = yield from proj_cut_g(c + j)
                    ret["g", h] = silu2(SG[:, j:j + 2, :], p2(p), [tk, *before])
                    rel(b, ret["g", h])
                    yield

            def ret_do(h):
                QR, KR, VT = QRs[h % 2], KRs[h % 2], VTs[h % 2]
                SG = SGs[h % 2].rearrange("p a (b c) -> p (a b) c", b=2)
                b, p = bank()
                for i in range(2):
                    PE.mm(p[:, 0:256], KR[:, i, 0:128], QR[:, i, :], i == 0, i == 1, [ret["r", h]])
                for i in range(2):
                    tk = PE.mm(p[:, 256:384], KR[:, i, 128:256], QR[:, i, 128:256], i == 0, i == 1, inc=(i == 1))
                V.tt(PTs[:, 0:256], p[:, 0:256], dec[:, h, :], ALU.mult, [tk])
                tp = V.tt(PTs[:, 256:384], p[:, 256:384], dec[:, h, 0:128], ALU.mult)
                rel(b, tp)
                yield
                yield
                for j in (0, 2):
                    b, p = bank()
                    for i in range(2):
                        d = slice((j + i) * 128, (j + i + 1) * 128)
                        PE.mm(p[:, i * 256:(i + 1) * 256], VT[:, 0, d], PTs[:, 0:256], True, False, [tp, ret["v", h]])
                        tk = PE.mm(p[:, i * 256 + 128:(i + 1) * 256], VT[:, 1, d], PTs[:, 256:384], False, True,
                                   inc=(i == 1))
                    yield
                    rel(b, A.cp(Y[:, j:j + 2, :], p2(p), [tk, V.last]))
                tr = yield from rstd([A.last, PE.last])
                yield
                V.tt(Y, Y, SG, ALU.mult, [ret["g", h]])
                V.stt(Y, Y, 0.5, RS.unsqueeze(1).broadcast_to([128, 4, 256]), ALU.mult, ALU.mult, [tr])
                yield
                pair(YH[:, 4 * h:4 * h + 4, :], YL[:, 4 * h:4 * h + 4, :], Y)
                ret["end", h] = [V.last, PE.last]
                yield

            def two_lines(first, then, after, least):
                done = [0, 0]

                def line_in():
                    for i in range(4):
                        while done[1] < i - 1:
                            yield
                        yield from first(i)
                        done[0] += 1
                    while done[1] < least:
                        yield
                    yield from after()

                def line_do():
                    for i in range(4):
                        while done[0] <= i:
                            yield
                        yield from then(i)
                        done[1] += 1

                weave(line_in(), line_do())

            def gates(gn, dst, w=()):
                for i in range(2):
                    c = take_cut(f"{stg}_{gn}{i}")
                    for j in (0, 2):
                        b, p, tk = yield from proj_cut_g(c + j)
                        ret["gate"] = A.act(dst[:, i * 4 + j:i * 4 + j + 2, :], p2(p), ACT.Tanh, [tk, *w],
                                            scale=0.5)
                        rel(b, A.last)
                        yield

            def merge(on, SGM, first):
                ty = V.last
                done = ret["end", 2] if first else ret["send", 2]
                for i in range(4):
                    j = take_cut(f"{stg}_{on}{i}")
                    b, p = bank()
                    for n in range(2):
                        cut_to(j + 2)
                        hi, lo = whole(j, 16)
                        for k in range(16):
                            o = p[:, n * 256:(n + 1) * 256]
                            PE.mm(o, hi[:, k, :], YH[:, k, :], k == 0, False, [cut[j], ty] if k > 11 else [cut[j], *done])
                            PE.mm(o, hi[:, k, :], YL[:, k, :], False, False)
                            tk = PE.mm(o, lo[:, k, :], YH[:, k, :], False, k == 15, inc=(k == 15))
                        used[j] = used[j + 1] = tk
                        j += 2
                    sl = slice(2 * i, 2 * i + 2)
                    if first:
                        rel(b, V.stt(MG[:, sl, :], SGM[:, sl, :], 1.0, p2(p), ALU.add, ALU.mult, [tk, ret["gate"]]))
                    else:
                        rel(b, V.stt(SGM[:, sl, :], SGM[:, sl, :], 1.0, p2(p), ALU.add, ALU.mult, [tk, ret["gate"]]))
                        V.tt(MG[:, sl, :], MG[:, sl, :], SGM[:, sl, :], ALU.add)
                        pair_half(MH[:, sl, :], ML[:, sl, :], MG[:, sl, :])

            two_lines(ret_in, ret_do, lambda: gates("gr", SGM), 0)
            merge("ro", SGM, True)
            fence()
            ar["at"] = base = base + 2048
            UB = buf(6, 259)
            CVs = [buf(6, 256) for _ in range(2)]
            TH = TMP[:, 0:1536].rearrange("p (a b) -> p a b", a=6)
            XD = cv[:, 768:1792].rearrange("p (t n) -> p t n", t=2)
            ZSs = [buf(4, 256) for _ in range(2)]
            Y, SQ = buf(4, 256), buf(4, 256)
            CB = cv[:, 0:384]
            SE = [buf(2, 384) for _ in range(2)]
            RS = buf(256)
            DTP, LA, CS_ = buf(2, 32), buf(2, 32), buf(2, 32)
            E1, E2 = (cv[:, o:o + 64].rearrange("p (a b) -> p a b", a=2) for o in (384, 448))
            AE = buf(32)
            SGM = AR[:, base:base + 2048].rearrange("p (a b) -> p a b", a=8)
            mh = base + 6 * 259 + 1536
            MH, ML = (AR32[:, mh + i:mh + i + 2048].rearrange("p (a b) -> p a b", a=8) for i in (0, 2048))

            def dt_in():
                c = take_cut(f"{stg}_dt")
                for t in range(2):
                    b, p = bank()
                    tk = pair_cut(p[:, 0:32], c, t, 32)
                    rel(b, V.tt(DTP[:, t, :], p[:, 0:32], dtb, ALU.add, [tk]))
                V.stt(E1, DTP, -1.0, DTP, ALU.mult, ALU.max)
                A.act(E1, E1, ACT.Exp, [V.last], scale=-1.0)
                A.act(AE, alog, ACT.Exp)
                t = A.act(E1, E1, ACT.Ln, bias=par("one"))
                V.ts(E2, DTP, 0.0, None, ALU.max)
                V.tt(DTP, E1, E2, ALU.add, [t])
                t = V.stt(LA, DTP, -1.0, AE.unsqueeze(1).broadcast_to([128, 2, 32]), ALU.mult, ALU.mult)
                V.set(UB[:, :, 0:3], 0.0)
                yield
                b, p = bank()
                PE.mm(p[:, 0:32], tri[:, 0:128], LA[:, 0, :], True, True, [t])
                PE.mm(p[:, 32:64], tri[:, 128:256], LA[:, 0, :], True, False)
                tk = PE.mm(p[:, 32:64], tri[:, 0:128], LA[:, 1, :], False, True, inc=True)
                ret["cs"] = V.cp(CS_, p[:, 0:64].rearrange("p (a b) -> p a b", a=2), [tk])
                rel(b, ret["cs"])
                A.wait(ret["cs"])
                yield

            def ssd_in(g):
                CV, ZS = CVs[g % 2], ZSs[g % 2]
                before = ret.get(("send", g - 2), [])
                tiles = [4 * g, 4 * g + 1, 4 * g + 2, 4 * g + 3, 16 + g, 20 + g]
                todo = []

                def conv(n, i, ta):
                    for m in (2 * n, 2 * n + 1):
                        f = tiles[m]
                        if i == 0:
                            t = V.ts(CV[:, m, :], UB[:, m, 0:256], cw[:, 4 * f:4 * f + 1], cb_[:, f:f + 1],
                                     ALU.mult, ALU.add, w=[ta, *before], chain=False)
                        else:
                            t = V.stt(CV[:, m, :], UB[:, m, i:i + 256], cw[:, 4 * f + i:4 * f + i + 1],
                                      CV[:, m, :], ALU.mult, ALU.add, w=[ret["tap", m]], chain=False)
                        ret["tap", m] = ret["conv"] = t

                c = take_cut(f"{stg}_xs{g}")
                for n, c0 in enumerate((0, 2, 0)):
                    if n == 2:
                        c = take_cut(f"{stg}_bc{g}")
                    b, p, tk = yield from proj_cut_g(c + c0, todo, True)
                    ta = A.cp(UB[:, 2 * n:2 * n + 2, 3:259], p2(p), [tk, *before, ret.get("conv")])
                    rel(b, ta)
                    todo += [lambda n=n, i=i, ta=ta: conv(n, i, ta) for i in range(4)]
                    yield
                c = take_cut(f"{stg}_z{g}")
                for j in (0, 2):
                    b, p, tk = yield from proj_cut_g(c + j, todo, True)
                    ret["z", g] = silu2(ZS[:, j:j + 2, :], p2(p), [tk, *before])
                    rel(b, ret["z", g])
                    if not j:
                        ta = A.act(TH, CV, ACT.Tanh, [ret["conv"], ret.get(("cv", g - 1))])
                        ret["cv", g] = V.stt(CV, TH, 1.0, CV, ALU.add, ALU.mult, [ta])
                    yield

            def ssd_do(g):
                CV, ZS = CVs[g % 2], ZSs[g % 2]
                acs = {}

                def cum(hp):
                    b, p = bank()
                    for i in range(2):
                        hh = 8 * g + 2 * hp + i
                        PE.mm(p[:, i * 256:(i + 1) * 256], LA[:, 0, hh:hh + 1].broadcast_to([128, 128]), tri, True, False)
                        tk = PE.mm(p[:, i * 256 + 128:(i + 1) * 256], LA[:, 1, hh:hh + 1].broadcast_to([128, 128]),
                                   tri[:, 0:128], False, True, inc=(i == 1))
                    se = SE[hp % 2]
                    for i in range(2):
                        hh = 8 * g + 2 * hp + i
                        A.act(se[:, i, 0:256], p[:, i * 256:(i + 1) * 256], ACT.Relu, [tk, ret.get(("se", hp % 2))],
                              bias=CS_[:, 0, hh:hh + 1], scale=-1.0, chain=False)
                        e = A.act(se[:, i, 256:384], p[:, i * 256 + 128:(i + 1) * 256], ACT.Relu,
                                  bias=CS_[:, 1, hh:hh + 1], scale=-1.0, chain=False)
                    rel(b, e)
                    acs[hp] = A.act(se, se, ACT.Exp, scale=-1.0)

                cum(0)
                for t in range(2):
                    b, p = bank()
                    for i in range(4):
                        tk = PE.tr(p[:, i * 128:(i + 1) * 128], CV[:, i, t * 128:(t + 1) * 128], ident, [ret["cv", g]],
                                   inc=(i == 3))
                    txd = V.tt(XD[:, t, :].rearrange("p (h n) -> p h n", h=8), p.rearrange("p (h n) -> p h n", h=8),
                               DTP[:, t, 8 * g:8 * g + 8].unsqueeze(2).broadcast_to([128, 8, 64]), ALU.mult, [tk],
                               chain=False)
                    rel(b, txd)
                    yield
                b, p = bank()
                PE.mm(p[:, 0:256], CV[:, 4, 0:128], CV[:, 5, :], True, True)
                tk = PE.mm(p[:, 256:384], CV[:, 4, 128:256], CV[:, 5, 128:256], True, True, inc=True)
                V.tt(CB[:, 0:256], p[:, 0:256], tri, ALU.mult, [tk])
                tcb = V.tt(CB[:, 256:384], p[:, 256:384], tri[:, 0:128], ALU.mult)
                rel(b, tcb)
                yield
                for hp in range(4):
                    if hp < 3:
                        cum(hp + 1)
                    se = SE[hp % 2]
                    t = V.tt(se, se, CB.unsqueeze(1).broadcast_to([128, 2, 384]), ALU.mult, [acs[hp], tcb], chain=False)
                    yield
                    yield
                    b, p = bank()
                    for i in range(2):
                        xc = slice((2 * hp + i) * 64, (2 * hp + i + 1) * 64)
                        o2 = p[i * 64:(i + 1) * 64, :]
                        PE.mm(o2[:, 0:256], XD[:, 0, xc], se[:, i, 0:256], True, False, [t])
                        tk = PE.mm(o2[:, 128:256], XD[:, 1, xc], se[:, i, 256:384], False, True, inc=(i == 1))
                    ret["se", hp % 2] = tk
                    rel(b, V.stt(Y[:, hp, :], CV[:, hp, :], dsk[:, 4 * g + hp:4 * g + hp + 1], p[:, 0:256],
                                 ALU.mult, ALU.add, [tk], chain=False))
                V.stt(Y, Y, 0.5, ZS, ALU.mult, ALU.mult, [ret["z", g]])
                yield
                tr = yield from rstd([PE.last])
                yield
                for i in range(4):
                    V.stt(Y[:, i, :], Y[:, i, :], nw[:, 4 * g + i:4 * g + i + 1], RS, ALU.mult, ALU.mult, [tr],
                          chain=False)
                yield
                pair(YH[:, 4 * g:4 * g + 4, :], YL[:, 4 * g:4 * g + 4, :], Y)
                ret["send", g] = [V.last, PE.last]
                yield

            weave(dt_in())
            two_lines(ssd_in, ssd_do, lambda: gates("gs", SGM, [ret["conv"], *ret["send", 2]]), 3)
            merge("so", SGM, False)
            tm = V.last
            for i in range(2):
                j = take_cut(f"{stg}_wo{i}")
                acc = [bank() for t in range(2)]
                for kh in range(2):
                    cut_to(j + 2)
                    hi, lo = whole(j, 4)
                    for t in range(2):
                        ts_ = slice(t * 128, (t + 1) * 128)
                        for k in range(4):
                            kk, o = 4 * kh + k, acc[t][1]
                            PE.mm(o, MH[:, kk, ts_], hi[:, k, :], kk == 0, False, [cut[j], tm])
                            PE.mm(o, ML[:, kk, ts_], hi[:, k, :], False, False)
                            tk = PE.mm(o, MH[:, kk, ts_], lo[:, k, :], False, kk == 7, inc=(k == 3))
                        if kh:
                            xs = X[:, t, i * 512:(i + 1) * 512]
                            rel(acc[t][0], V.tt(xs, acc[t][1], xs, ALU.add, [tk]))
                    used[j] = used[j + 1] = tk
                    j += 2

        def ffn(stg):
            phase()
            nxt = stages[stages.index(stg) + 1:][:1]
            if nxt and nxt[0] + "_c" in coffs:
                consts(nxt[0] + "_c")
            norm_HL(f"g_{stg}")
            fence()
            FH, FL = buf(22, 256, of=AR32), buf(22, 256, of=AR32)
            SG, FF = ([buf(2, 256) for _ in range(2)] for _ in range(2))
            ht = []
            for i in range(11):
                c = take_cut(f"{stg}_gu{i}")
                b, p = bank()
                for n in range(2):
                    tk = mm_cut(p[:, n * 256:(n + 1) * 256], c + n)
                a = A.act(SG[i % 2], p.rearrange("p (a b) -> p a b", a=2), ACT.Silu, [tk, ht[i - 2] if i > 1 else None])
                rel(b, a)
                b, p = bank()
                for n in range(2):
                    tk = mm_cut(p[:, n * 256:(n + 1) * 256], c + 2 + n)
                rel(b, V.tt(FF[i % 2], p.rearrange("p (a b) -> p a b", a=2), SG[i % 2], ALU.mult, [tk, a]))
                ht.append(pair(FH[:, 2 * i:2 * i + 2, :], FL[:, 2 * i:2 * i + 2, :], FF[i % 2]))
            acc = {(t, n): bank() for t in range(2) for n in range(2)}
            for i in range(11):
                if i % 2 == 0:
                    j = take_cut(f"{stg}_dn{i // 2}")
                cut_to(j + 2)
                hi, lo = whole(j, 2)
                for t in range(2):
                    ts_ = slice(t * 128, (t + 1) * 128)
                    for n in range(2):
                        o, cc = acc[t, n][1], slice(n * 512, (n + 1) * 512)
                        for k in range(2):
                            kk = 2 * i + k
                            PE.mm(o, FH[:, kk, ts_], hi[:, k, cc], kk == 0, False, [cut[j], ht[i]])
                            PE.mm(o, FL[:, kk, ts_], hi[:, k, cc], False, False)
                            tk = PE.mm(o, FH[:, kk, ts_], lo[:, k, cc], False, kk == 21, inc=(k == 1))
                        if i == 10:
                            xs = X[:, t, n * 512:(n + 1) * 512]
                            rel(acc[t, n][0], V.tt(xs, acc[t, n][1], xs, ALU.add, [tk]))
                used[j] = used[j + 1] = tk
                j += 2

        def fin():
            phase()
            c = take("fin_w")
            ss, t2 = rstd_x()
            for t in range(2):
                V.stt(X[:, t, :], X[:, t, :], ss[:, t:t + 1], c.ap[:, 0, :], ALU.mult, ALU.mult, [t2, c.tok])

        for s in stages:
            if s == "even":
                even()
            elif s in ("moe0", "moe1"):
                moe(s, int(s[-1]))
            elif s == "odd":
                odd_start = st["take"]
                odd()
            elif s.startswith("hyb"):
                hyb(s)
            elif s.startswith("ffn"):
                ffn(s)
            else:
                fin()
        SP.dma(out_d.rearrange("(t p) d -> p t d", p=128), X, s_out, [V.last])
        SP.wait((s_out, 16))

        block = ctx.enter_context(nc.Block())

        @block.sync
        def _(eng):
            SP.emit(eng)

        @block.scalar
        def _(eng):
            A.emit(eng)

        @block.vector
        def _(eng):
            V.emit(eng)

        @block.gpsimd
        def _(eng):
            G.emit(eng)

        @block.tensor
        def _(eng):
            PE.emit(eng)


def rows(w):
    return w.reshape(-1, 128, w.shape[1]).transpose(1, 0, 2)


def cols(v):
    return v.reshape(-1, 128).T


def brow(v):
    return np.broadcast_to(v.reshape(1, -1), (128, v.size))


def pack_chunk(name, inp):
    f = np.float32
    if name == "even_c":
        o = np.zeros((128, 1184), f)
        h, r = np.arange(128) // 64, np.arange(128) % 64
        same = h[:, None] == h[None, :]
        R, Cc = r[:, None], r[None, :]
        blk = (R // 16) == (Cc // 16)
        o[:, 0:128] = same
        o[:, 128:256] = same & (R < Cc) & blk
        o[:, 256:384] = same & (Cc < R) & blk
        o[:, 384:512] = same & (Cc < R) & ~blk
        o[:, 512:640] = same & (R < Cc)
        o[:, 640:704] = R <= np.arange(64)[None, :]
        o[:, 704:768] = R == np.arange(64)[None, :]
        for g, w in enumerate((2, 4, 8, 16)):
            o[:, 1088 + 16 * g:1104 + 16 * g] = w / np.minimum(np.arange(1, 17), w)
        o[:, 1152] = 1.0
        return o
    if name.startswith("even_in"):
        i = int(name[-1])
        return rows(inp["even_w_in"][0][:, i * 512:min((i + 1) * 512, 2304)])
    if name == "lora":
        o = np.zeros((128, 3, 512), f)
        o[0:64, 0] = inp["rw_w2"][0]
        o[64:128, 0] = inp["rw_a2"][0]
        o[:, 1] = inp["rw_g2"][0]
        o[:, 2] = inp["pool_w"][0].transpose(1, 0, 2).reshape(128, 512)
        return o
    if name.startswith("even_out"):
        i = int(name[-1])
        return rows(inp["even_w_out"][0][:, i * 512:(i + 1) * 512])
    if name.startswith("moe"):
        l = int(name[3])
        if name.endswith("_r"):
            return rows(np.concatenate([inp["moe_w_group"][l], inp["moe_w_expert"][l]], axis=1))
        q, c = (int(v) for v in name[6:].split("_"))
        w = inp[{"g": "moe_w_gate", "u": "moe_w_up", "d": "moe_w_down"}[name[5]]][l, 4 * q:4 * q + 4]
        if name[5] == "d":
            return w[:, c * 128:(c + 1) * 128].transpose(1, 0, 2)
        return w[:, c * 256:(c + 1) * 256].reshape(4, 2, 128, 512).transpose(2, 1, 0, 3)
    if name == "odd_c":
        o = np.zeros((128, 1152), f)
        inv = (10000.0 ** (-np.arange(0, 64, 2, dtype=f) / f(64))).astype(f)
        ang = np.arange(T, dtype=f)[None, :] * inv[np.arange(128) % 32][:, None]
        o[:, 0:256] = np.cos(ang)
        o[:, 256:512] = np.sin(ang)
        q = np.arange(128)
        o[:, 640:768] = np.where(q[:, None] >= q[None, :], 0.0, -1e30)
        for m in range(128):
            d = m % 64
            if d < 32:
                o[m + 32, 768 + m] = -1.0
            else:
                o[m - 32, 768 + m] = 1.0
        o[:, 896:1152] = np.arange(256)
        return o
    if name.startswith("odd_in"):
        i = int(name[-1])
        return rows(inp["odd_w_in"][0][:, i * 512:(i + 1) * 512])
    if name.startswith("odd_out"):
        i = int(name[-1])
        return rows(inp["odd_w_out"][0][:, i * 512:(i + 1) * 512])
    if name in ("s5_B", "s5_C"):
        o = np.zeros((128, 2, 16, 128 if name == "s5_B" else 32), f)
        for r, part in enumerate(("re", "im")):
            m = inp[("s5_b_" if name == "s5_B" else "s5_c_") + part][0]
            for g in range(32):
                i, gg = g // 2, g % 2
                ch, s = 16 * gg, 64 * gg
                if name == "s5_B":
                    ch += 32 * (i % 4)
                    o[ch:ch + 16, r, i, s:s + 64] = m[g].T
                else:
                    o[s:s + 64, r, i, ch:ch + 16] = m[g].T
        return o
    if name == "glu":
        return rows(inp["s5_w_glu"][0])
    if name.startswith("hyb"):
        l, key = int(name[3]), name[5:]
        w = inp["w_in_2"][l]
        if key == "c":
            o = np.zeros((128, 2008), f)
            inv = (10000.0 ** (-np.arange(128, dtype=f) / f(128))).astype(f)
            ang = np.arange(T, dtype=f)[None, :] * inv[:, None]
            o[:, 0:256] = np.cos(ang)
            o[:, 256:512] = np.sin(ang)
            j, i = np.arange(128)[:, None], np.arange(256)[None, :]
            o[:, 512:768] = j <= i
            for h in range(4):
                lg = math.log(1.0 - 2.0 ** (-5.0 - h))
                o[:, 768 + 256 * h:1024 + 256 * h] = np.where(j <= i, np.exp(lg * np.maximum(i - j, 0)), 0.0)
            at = 1792
            o[:, at:at + 96] = inp["conv_w_2"][l].reshape(4, 24, 128).transpose(2, 1, 0).reshape(128, 96)
            o[:, at + 96:at + 120] = cols(inp["conv_b_2"][l])
            o[:, at + 120:at + 136] = cols(np.repeat(inp["d_skip_2"][l], 64))
            o[:, at + 136:at + 152] = cols(inp["ssd_norm_w_2"][l])
            o[:, at + 152:at + 184] = brow(inp["dt_bias_2"][l])
            o[:, at + 184:at + 216] = brow(inp["a_log_2"][l])
            return o
        if key == "dt":
            return rows(w[:, 11264:11296])
        n = int(key[-1])
        k = key[:-1]
        if k == "qk":
            return rows(np.concatenate([w[:, n * 256:(n + 1) * 256], w[:, 1024 + n * 256:1024 + (n + 1) * 256]], 1))
        if k == "bc":
            return rows(np.concatenate([w[:, 10240 + n * 128:10368 + n * 128], w[:, 10752 + n * 128:10880 + n * 128]], 1))
        starts = {"v": 2048, "g": 4096, "z": 6144, "xs": 8192, "gr": 11296, "gs": 12320}
        if k in starts:
            a = starts[k] + n * 512
            return rows(w[:, a:a + 512])
        if k == "ro":
            return rows(inp["ret_out_2"][l][:, n * 256:(n + 1) * 256])
        if k == "so":
            return rows(inp["ssd_out_2"][l][:, n * 256:(n + 1) * 256])
        return rows(inp["w_o_2"][l][:, n * 512:(n + 1) * 512])
    if name.startswith("ffn"):
        l, key = int(name[3]), name[5:]
        if key.startswith("gu"):
            n = int(key[2:])
            w = inp["w_gate_up_2"][l]
            return rows(np.concatenate([w[:, n * 256:(n + 1) * 256], w[:, 2816 + n * 256:2816 + (n + 1) * 256]], 1))
        n = int(key[2:])
        return rows(inp["w_down_2"][l][n * 512:min((n + 1) * 512, 2816)])
    return brow(inp["final_norm_w_2"])


def pack_params(inp):
    o = np.zeros((128, NP), np.float32)

    def put(name, v):
        at, n = PT[name]
        o[:, at:at + n] = v

    for l in range(2):
        put(("g_even", "g_odd")[l], cols(inp["norm_mix_g"][l]))
        put(f"g_moe{l}", cols(inp["norm_ffn_g"][l]))
        put(f"g_hyb{l}", cols(inp["norm_mix_w_2"][l]))
        put(f"g_ffn{l}", cols(inp["norm_ffn_w_2"][l]))
        put(f"rb{l}", brow(np.concatenate([inp["moe_b_group"][l], inp["moe_b_expert"][l]])))
    for name, key in (("mu", "rw_mu"), ("w0", "rw_w0"), ("a0", "rw_a0"), ("k_k", "rw_k_k"), ("k_a", "rw_k_a"),
                      ("r_k", "rw_r_k"), ("ln_g", "rw_ln_g"), ("ln_b", "rw_ln_b"), ("pool_scale", "pool_scale"),
                      ("s5_d", "s5_d"), ("subln", "da_subln")):
        put(name, cols(inp[key][0].reshape(-1)))
    put("qn", cols(np.concatenate([inp["da_q_norm"][0]] * 2)))
    put("kn", cols(np.concatenate([inp["da_k_norm"][0]] * 2)))
    for name, key in (("s5_re", "s5_a_re"), ("s5_im", "s5_a_im"), ("s5_ls", "s5_log_step")):
        put(name, cols(inp[key][0].reshape(-1)))
    put("lam", brow(np.concatenate([inp[f"da_lam_{k}"][0] for k in ("q1", "k1", "q2", "k2")])))
    put("eps6", 1e-6)
    put("eps5", 1e-5)
    put("epsln", 64e-5)
    put("one", 1.0)
    put("hpi", math.pi / 2)
    put("ident", np.eye(128))
    put("ones", 1.0)
    r = np.arange(128)
    put("tri", r[:, None] <= r[None, :])
    put("iota", np.arange(32))
    r = np.arange(128) // 64
    put("ones64", r[:, None] == r[None, :])
    return o


def kernel(**inputs):
    import numpy as _np
    import concourse.bacc as _bacc
    from concourse import mybir as _mybir
    from concourse.bass_utils import run_bass_kernel_spmd as _run

    inputs = {k: _np.asarray(v) for k, v in inputs.items()}
    table = chunk_table(STAGES) + [(name, 1, n) for name, n in const_table(STAGES)]
    W = _np.empty((sum(128 * k * n for _, k, n in table),), _np.float32)
    at = 0
    for name, k, n in table:
        size = 128 * k * n
        W[at:at + size].reshape(128, k, n)[...] = pack_chunk(name, inputs).reshape(128, k, n)
        at += size
    arrays = {"w_dram": W, "p_dram": pack_params(inputs), "x_dram": _np.ascontiguousarray(inputs["x"][0])}
    nc = _bacc.Bacc("TRN2", target_bir_lowering=False, num_devices=1)
    args = [nc.dram_tensor(k, a.shape, _mybir.dt.float32, kind="ExternalInput").ap() for k, a in arrays.items()]
    out = nc.dram_tensor("out_dram", (T, 1024), _mybir.dt.float32, kind="ExternalOutput").ap()
    program(nc, args[0], args[1], args[2], out, STAGES)
    r = _run(nc, [arrays], core_ids=[0])
    return r.results[0]["out_dram"].reshape(1, T, 1024)
```
